# Optimizing a Trainium2 kernel written in Bass

```python
import jax
import jax.numpy as jnp
from jax import lax
import numpy as np

D_MODEL = 1024
BATCH = 1
SEQ = 512
DEPTH = 2
DEC_BATCH = 8
DEC_SEQ = 8
PAST_LEN = 256
PAGE_SIZE = 128

EPS = 1e-6
DN_HEADS = 4
DN_HEAD_DIM = 128
DN_WIDTH = DN_HEADS * DN_HEAD_DIM
CONV_WIDTH = 4
DN_CHUNK = 64
SWA_GROUPS = ((128, 1), (512, 4), (2048, 16))
N_SWA_GROUPS = len(SWA_GROUPS)
SWA_HEADS = 4
SWA_HEAD_DIM = 64
SWA_WIDTH = N_SWA_GROUPS * SWA_HEADS * SWA_HEAD_DIM
SWA_OUT = SWA_HEADS * SWA_HEAD_DIM
SWA_BLOCK = 128
ROPE_THETA = 10000.0
POOL_WINDOWS = (2, 4, 8, 16)
N_POOL_GROUPS = len(POOL_WINDOWS)
POOL_GROUP = 384
POOL_WIDTH = N_POOL_GROUPS * POOL_GROUP
POOL_BUF = max(POOL_WINDOWS) - 1
N_BRANCH = 3
IN_SIZES = (3 * DN_WIDTH, DN_WIDTH, DN_HEADS, DN_HEADS, 3 * SWA_WIDTH, POOL_WIDTH, N_BRANCH * D_MODEL)
IN_COLS = sum(IN_SIZES)
PEER_KEYS = 128
PEER_EXPERTS = PEER_KEYS * PEER_KEYS
PEER_HEADS = 8
PEER_TOPK = 16
PEER_DKEY = 256
PEER_BLOCK = 128

kernel_name = "hybrid_deltanet_dilated_pool_peer_step"

def _rmsnorm(x, g):
    xf = x.astype(jnp.float32)
    y = xf * lax.rsqrt(jnp.mean(xf * xf, axis=-1, keepdims=True) + EPS)
    return (y * g.astype(jnp.float32)).astype(x.dtype)

def _l2norm(x):
    return x * lax.rsqrt(jnp.sum(x * x, axis=-1, keepdims=True) + EPS)

def _rope(x, pos):
    half = x.shape[-1] // 2
    inv = ROPE_THETA ** (-jnp.arange(half, dtype=jnp.float32) / half)
    ang = pos.astype(jnp.float32)[:, None] * inv[None, :]
    shape = (1, x.shape[1]) + (1,) * (x.ndim - 3) + (half,)
    cos = jnp.cos(ang).reshape(shape)
    sin = jnp.sin(ang).reshape(shape)
    xf = x.astype(jnp.float32)
    x1, x2 = xf[..., :half], xf[..., half:]
    return jnp.concatenate([x1 * cos - x2 * sin, x1 * sin + x2 * cos], axis=-1).astype(x.dtype)

def _split_cols(proj):
    parts, off = [], 0
    for size in IN_SIZES:
        parts.append(proj[..., off:off + size])
        off += size
    return parts

def _gated_delta_rule(q, k, v, g, beta, state0):
    B, T, H, dk = q.shape
    dv = v.shape[-1]
    C = min(DN_CHUNK, T)
    pad = (-T) % C
    N = (T + pad) // C

    def chunks(a):
        a = jnp.pad(a, ((0, 0), (0, pad)) + ((0, 0),) * (a.ndim - 2))
        a = a.reshape((B, N, C) + a.shape[2:])
        return jnp.moveaxis(a, 3, 1)

    qc, kc, vc, gc, bc = chunks(q), chunks(k), chunks(v), chunks(g), chunks(beta)
    gc = jnp.cumsum(gc, axis=-1)
    idx = jnp.arange(C)
    incl = idx[:, None] >= idx[None, :]
    strict = idx[:, None] > idx[None, :]
    decay = jnp.exp(jnp.where(incl, gc[..., :, None] - gc[..., None, :], -jnp.inf))
    kb = kc * bc[..., None]
    vb = vc * bc[..., None]
    lower = jnp.einsum('bhncd,bhnsd->bhncs', kb, kc) * jnp.where(strict, decay, 0.0)
    rhs = jnp.concatenate([vb, kb * jnp.exp(gc)[..., None]], axis=-1)
    sol = lax.linalg.triangular_solve(lower, rhs, left_side=True, lower=True, unit_diagonal=True)
    u_c, w_c = sol[..., :dv], sol[..., dv:]
    intra = jnp.einsum('bhncd,bhnsd->bhncs', qc, kc) * decay
    q_dec = qc * jnp.exp(gc)[..., None]
    k_dec = kc * jnp.exp(gc[..., -1:] - gc)[..., None]
    g_last = jnp.exp(gc[..., -1])

    def step(S, inp):
        intra_n, qd_n, u_n, w_n, kd_n, gl_n = inp
        v_new = u_n - jnp.einsum('bhcd,bhde->bhce', w_n, S)
        o_n = jnp.einsum('bhcd,bhde->bhce', qd_n, S) + jnp.einsum('bhcs,bhse->bhce', intra_n, v_new)
        S = S * gl_n[..., None, None] + jnp.einsum('bhcd,bhce->bhde', kd_n, v_new)
        return S, o_n

    xs = tuple(jnp.moveaxis(a, 2, 0) for a in (intra, q_dec, u_c, w_c, k_dec, g_last))
    S, o = lax.scan(step, state0, xs)
    o = jnp.transpose(o, (1, 0, 3, 2, 4)).reshape(B, N * C, H, dv)[:, :T]
    return o, S

def _deltanet(qkv, z, a, b, conv0, state0, conv_w, a_log, dt_bias, dn_norm):
    B, T, Cq = qkv.shape
    ext = jnp.concatenate([conv0.astype(qkv.dtype), qkv], axis=1)
    conv = lax.conv_general_dilated(ext, conv_w[:, None, :].astype(qkv.dtype), window_strides=(1,), padding='VALID',
                                    dimension_numbers=('NWC', 'WIO', 'NWC'), feature_group_count=Cq)
    conv_new = ext[:, ext.shape[1] - (CONV_WIDTH - 1):]
    act = jax.nn.silu(conv.astype(jnp.float32)).reshape(B, T, 3, DN_HEADS, DN_HEAD_DIM)
    q = _l2norm(act[:, :, 0]) * (DN_HEAD_DIM ** -0.5)
    k = _l2norm(act[:, :, 1])
    v = act[:, :, 2]
    beta = jax.nn.sigmoid(b.astype(jnp.float32))
    g = -jnp.exp(a_log.astype(jnp.float32)) * jax.nn.softplus(a.astype(jnp.float32) + dt_bias.astype(jnp.float32))
    o, s_new = _gated_delta_rule(q, k, v, g, beta, state0.astype(jnp.float32))
    zf = z.astype(jnp.float32).reshape(B, T, DN_HEADS, DN_HEAD_DIM)
    o = _rmsnorm(o, dn_norm) * jax.nn.silu(zf)
    return o.reshape(B, T, DN_WIDTH).astype(qkv.dtype), conv_new, s_new.astype(state0.dtype)

def _dilated_prompt(q, k, v, window, dil):
    B, T, H, dh = q.shape
    n_back = window // dil
    L = T // dil
    Bq = SWA_BLOCK
    n_prev = -(-n_back // Bq)
    Lp = -(-L // Bq) * Bq
    nb = Lp // Bq
    z = B * dil

    def phase(a):
        a = a.reshape(B, L, dil, H, dh).transpose(0, 2, 1, 3, 4).reshape(z, L, H, dh)
        return jnp.pad(a.astype(jnp.float32), ((0, 0), (0, Lp - L), (0, 0), (0, 0)))

    qs, ks, vs = phase(q), phase(k), phase(v)
    front = ((0, 0), (n_prev * Bq, 0), (0, 0), (0, 0))
    kp, vp = jnp.pad(ks, front), jnp.pad(vs, front)

    def band(a):
        return jnp.concatenate([a[:, p * Bq:p * Bq + Lp].reshape(z, nb, Bq, H, dh) for p in range(n_prev + 1)], axis=2)

    kband, vband = band(kp), band(vp)
    qbl = qs.reshape(z, nb, Bq, H, dh)
    s = jnp.einsum('znqhd,znkhd->znhqk', qbl, kband) * (dh ** -0.5)
    qi = jnp.arange(Bq)
    kj = jnp.arange((n_prev + 1) * Bq)
    rel = n_prev * Bq + qi[:, None] - kj[None, :]
    qpos = jnp.arange(nb)[:, None, None] * Bq + qi[None, :, None]
    valid = (rel >= 0) & (rel <= n_back) & (qpos - rel >= 0)
    s = jnp.where(valid[None, :, None], s, -jnp.inf)
    m = jnp.max(s, axis=-1)
    p = jnp.exp(s - m[..., None])
    l = jnp.sum(p, axis=-1)
    o = jnp.einsum('znhqk,znkhd->znqhd', p, vband).reshape(z, Lp, H, dh)
    m = jnp.transpose(m, (0, 1, 3, 2)).reshape(z, Lp, H)
    l = jnp.transpose(l, (0, 1, 3, 2)).reshape(z, Lp, H)

    def unphase(a):
        a = a[:, :L].reshape((B, dil, L) + a.shape[2:])
        return jnp.moveaxis(a, 1, 2).reshape((B, T) + a.shape[3:])

    return unphase(o), unphase(m), unphase(l)

def _dilated_sample(q, kcat, vcat, n_buf, window, dil):
    B, T, H, dh = q.shape
    n_back = window // dil
    idx = n_buf + jnp.arange(T)[:, None] - dil * jnp.arange(n_back + 1)[None, :]
    valid = idx >= 0
    idx = jnp.maximum(idx, 0)
    kg = kcat[:, idx].astype(jnp.float32)
    vg = vcat[:, idx].astype(jnp.float32)
    s = jnp.einsum('bthd,btjhd->bthj', q.astype(jnp.float32), kg) * (dh ** -0.5)
    s = jnp.where(valid[None, :, None, :], s, -jnp.inf)
    m = jnp.max(s, axis=-1)
    p = jnp.exp(s - m[..., None])
    l = jnp.sum(p, axis=-1)
    o = jnp.einsum('bthj,btjhd->bthd', p, vg)
    return o, m, l

def _combine_groups(parts):
    m_all = jnp.stack([pt[1] for pt in parts], axis=0)
    M = jnp.max(m_all, axis=0)
    num = sum(jnp.exp(pt[1] - M)[..., None] * pt[0] for pt in parts)
    den = sum(jnp.exp(pt[1] - M) * pt[2] for pt in parts)
    return num / den[..., None]

def _dilated_branch(qkv_b, pos0, prompt, wins0):
    B, T, _ = qkv_b.shape
    qkv = qkv_b.reshape(B, T, 3, N_SWA_GROUPS, SWA_HEADS, SWA_HEAD_DIM)
    pos = pos0 + jnp.arange(T)
    q = _rope(qkv[:, :, 0], pos)
    k = _rope(qkv[:, :, 1], pos)
    v = qkv[:, :, 2]
    parts, new_wins = [], []
    for gi, (window, dil) in enumerate(SWA_GROUPS):
        qg, kg, vg = q[:, :, gi], k[:, :, gi], v[:, :, gi]
        kv_new = jnp.stack([kg, vg], axis=2)
        if prompt:
            parts.append(_dilated_prompt(qg, kg, vg, window, dil))
            kv_all = kv_new
        else:
            buf = wins0[gi]
            kv_all = jnp.concatenate([buf.astype(kv_new.dtype), kv_new], axis=1)
            parts.append(_dilated_sample(qg, kv_all[:, :, 0], kv_all[:, :, 1], buf.shape[1], window, dil))
        keep = min(window, kv_all.shape[1])
        new_wins.append(kv_all[:, kv_all.shape[1] - keep:])
    o = _combine_groups(parts)
    return o.reshape(B, T, SWA_OUT).astype(qkv_b.dtype), new_wins

def _pool_branch(u, prefix, pos0, w_pool, pool_scale):
    B, T, _ = u.shape
    ext = jnp.concatenate([prefix.astype(u.dtype), u], axis=1)
    csum = jnp.pad(jnp.cumsum(ext.astype(jnp.float32), axis=1), ((0, 0), (1, 0), (0, 0)))
    end = csum[:, POOL_BUF + 1:POOL_BUF + 1 + T]
    pos = (pos0 + jnp.arange(T)).astype(jnp.float32)
    uf = u.astype(jnp.float32)
    diffs = []
    for gi, w in enumerate(POOL_WINDOWS):
        lo, hi = gi * POOL_GROUP, (gi + 1) * POOL_GROUP
        start = csum[:, POOL_BUF + 1 - w:POOL_BUF + 1 - w + T, lo:hi]
        count = jnp.minimum(float(w), pos + 1.0)[None, :, None]
        diffs.append((end[..., lo:hi] - start) / count - uf[..., lo:hi])
    d = jnp.stack(diffs, axis=2)
    y = jnp.einsum('btgc,gce->btge', d, w_pool.astype(jnp.float32)).reshape(B, T, POOL_WIDTH)
    return (y * pool_scale.astype(jnp.float32)).astype(u.dtype), ext[:, ext.shape[1] - POOL_BUF:]

def _peer(h, w_query, subkeys, w_up, w_down):
    B, T, D = h.shape
    n = B * T
    xt = h.reshape(n, D)
    q = (xt @ w_query).astype(jnp.float32).reshape(n, PEER_HEADS, 2, PEER_DKEY // 2)
    s = jnp.einsum('nhpd,pkd->nhpk', q, subkeys.astype(jnp.float32))
    s1, i1 = lax.top_k(s[:, :, 0], PEER_TOPK)
    s2, i2 = lax.top_k(s[:, :, 1], PEER_TOPK)
    cand = (s1[..., :, None] + s2[..., None, :]).reshape(n, PEER_HEADS, PEER_TOPK * PEER_TOPK)
    best, ic = lax.top_k(cand, PEER_TOPK)
    expert = (jnp.take_along_axis(i1, ic // PEER_TOPK, axis=-1) * PEER_KEYS
              + jnp.take_along_axis(i2, ic % PEER_TOPK, axis=-1))
    gate = jax.nn.softmax(best, axis=-1)
    nb = -(-n // PEER_BLOCK)
    pad = nb * PEER_BLOCK - n
    xb = jnp.pad(xt, ((0, pad), (0, 0))).reshape(nb, PEER_BLOCK, D)
    eb = jnp.pad(expert, ((0, pad), (0, 0), (0, 0))).reshape(nb, PEER_BLOCK, PEER_HEADS, PEER_TOPK)
    gb = jnp.pad(gate, ((0, pad), (0, 0), (0, 0))).reshape(nb, PEER_BLOCK, PEER_HEADS, PEER_TOPK)

    def block(args):
        xk, ek, gk = args
        up = jnp.take(w_up, ek, axis=0).astype(jnp.float32)
        act = jax.nn.gelu(jnp.einsum('nd,nhkd->nhk', xk.astype(jnp.float32), up), approximate=False) * gk
        down = jnp.take(w_down, ek, axis=0).astype(jnp.float32)
        return jnp.einsum('nhk,nhkd->nd', act, down)

    y = lax.map(block, (xb, eb, gb)).reshape(nb * PEER_BLOCK, D)[:n]
    return y.reshape(B, T, D).astype(h.dtype)

def _layer(x, l, pos0, prompt, delta0, conv0, wins0, pool0, weights):
    (norm_mix, w_in, conv_w, a_log, dt_bias, dn_norm, w_pool, pool_scale, w_branch, w_out,
     norm_ffn, peer_query, peer_subkeys, peer_up, peer_down) = weights
    B, T, _ = x.shape
    h = _rmsnorm(x, norm_mix[l])
    qkv_a, z_a, a_a, b_a, qkv_b, u_c, gate_logits = _split_cols(h @ w_in[l])
    o_a, conv_new, delta_new = _deltanet(qkv_a, z_a, a_a, b_a, conv0, delta0, conv_w[l], a_log[l], dt_bias[l], dn_norm[l])
    o_b, wins_new = _dilated_branch(qkv_b, pos0, prompt, wins0)
    o_c, pool_new = _pool_branch(u_c, pool0, pos0, w_pool[l], pool_scale[l])
    gates = jax.nn.sigmoid(gate_logits.astype(jnp.float32)).astype(x.dtype).reshape(B, T, N_BRANCH, D_MODEL)
    wb = w_branch[l]
    merged = (gates[:, :, 0] * (o_a @ wb[:DN_WIDTH])
              + gates[:, :, 1] * (o_b @ wb[DN_WIDTH:DN_WIDTH + SWA_OUT])
              + gates[:, :, 2] * (o_c @ wb[DN_WIDTH + SWA_OUT:]))
    x = x + merged @ w_out[l]
    x = x + _peer(_rmsnorm(x, norm_ffn[l]), peer_query[l], peer_subkeys[l], peer_up[l], peer_down[l])
    return x, delta_new, conv_new, wins_new, pool_new

def _trunk(x, pos0, prompt, deltas, convs, wins, pools, weights, norm_final):
    new_delta, new_conv, new_pool = [], [], []
    new_wins = [[] for _ in SWA_GROUPS]
    for l in range(DEPTH):
        wins_l = None if prompt else [w[l] for w in wins]
        x, d, c, ws, p = _layer(x, l, pos0, prompt, deltas[l], convs[l], wins_l, pools[l], weights)
        new_delta.append(d)
        new_conv.append(c)
        new_pool.append(p)
        for gi in range(N_SWA_GROUPS):
            new_wins[gi].append(ws[gi])
    y = _rmsnorm(x, norm_final)
    return y, jnp.stack(new_delta), jnp.stack(new_conv), [jnp.stack(w) for w in new_wins], jnp.stack(new_pool)

def setup_inputs(seed: int = 0) -> dict:
    key = jax.random.key(seed)
    ks = jax.random.split(key, 32)
    f32 = jnp.float32

    def nrm(k, shape, scale):
        return jax.random.normal(k, shape, f32) * scale

    win_lens = [min(w, PAST_LEN) for w, _ in SWA_GROUPS]
    dt = jnp.exp(jax.random.uniform(ks[12], (DEPTH, DN_HEADS), f32, float(np.log(1e-3)), float(np.log(1e-1))))
    return {
        'x_prompt': nrm(ks[0], (BATCH, SEQ, D_MODEL), 1.0),
        'x_sample': nrm(ks[1], (DEC_BATCH, DEC_SEQ, D_MODEL), 1.0),
        'state_delta': nrm(ks[2], (DEPTH, DEC_BATCH, DN_HEADS, DN_HEAD_DIM, DN_HEAD_DIM), 0.05),
        'state_conv': nrm(ks[3], (DEPTH, DEC_BATCH, CONV_WIDTH - 1, 3 * DN_WIDTH), 1.0),
        'cache_win0': nrm(ks[4], (DEPTH, DEC_BATCH, win_lens[0], 2, SWA_HEADS, SWA_HEAD_DIM), 1.0),
        'cache_win1': nrm(ks[5], (DEPTH, DEC_BATCH, win_lens[1], 2, SWA_HEADS, SWA_HEAD_DIM), 1.0),
        'cache_win2': nrm(ks[6], (DEPTH, DEC_BATCH, win_lens[2], 2, SWA_HEADS, SWA_HEAD_DIM), 1.0),
        'state_pool': nrm(ks[7], (DEPTH, DEC_BATCH, POOL_BUF, POOL_WIDTH), 1.0),
        'norm_mix': 1.0 + nrm(ks[8], (DEPTH, D_MODEL), 0.02),
        'w_in': nrm(ks[9], (DEPTH, D_MODEL, IN_COLS), D_MODEL ** -0.5),
        'conv_w': nrm(ks[10], (DEPTH, CONV_WIDTH, 3 * DN_WIDTH), CONV_WIDTH ** -0.5),
        'a_log': jnp.log(jax.random.uniform(ks[11], (DEPTH, DN_HEADS), f32, 1.0, 16.0)),
        'dt_bias': dt + jnp.log(-jnp.expm1(-dt)),
        'dn_norm': 1.0 + nrm(ks[13], (DEPTH, DN_HEAD_DIM), 0.02),
        'w_pool': nrm(ks[14], (DEPTH, N_POOL_GROUPS, POOL_GROUP, POOL_GROUP), POOL_GROUP ** -0.5),
        'pool_scale': 1.0 + nrm(ks[15], (DEPTH, POOL_WIDTH), 0.02),
        'w_branch': jnp.concatenate([nrm(ks[16], (DEPTH, DN_WIDTH, D_MODEL), DN_WIDTH ** -0.5),
                                     nrm(ks[17], (DEPTH, SWA_OUT, D_MODEL), SWA_OUT ** -0.5),
                                     nrm(ks[18], (DEPTH, POOL_WIDTH, D_MODEL), POOL_WIDTH ** -0.5)], axis=1),
        'w_out': nrm(ks[19], (DEPTH, D_MODEL, D_MODEL), D_MODEL ** -0.5),
        'norm_ffn': 1.0 + nrm(ks[20], (DEPTH, D_MODEL), 0.02),
        'peer_query': nrm(ks[21], (DEPTH, D_MODEL, PEER_HEADS * PEER_DKEY), D_MODEL ** -0.5),
        'peer_subkeys': nrm(ks[22], (DEPTH, 2, PEER_KEYS, PEER_DKEY // 2), (PEER_DKEY // 2) ** -0.5),
        'peer_up': nrm(ks[23], (DEPTH, PEER_EXPERTS, D_MODEL), D_MODEL ** -0.5),
        'peer_down': nrm(ks[24], (DEPTH, PEER_EXPERTS, D_MODEL), PEER_HEADS ** -0.5),
        'norm_final': 1.0 + nrm(ks[25], (D_MODEL,), 0.02),
    }

def reference(x_prompt, x_sample, state_delta, state_conv, cache_win0, cache_win1, cache_win2, state_pool,
              norm_mix, w_in, conv_w, a_log, dt_bias, dn_norm, w_pool, pool_scale, w_branch, w_out,
              norm_ffn, peer_query, peer_subkeys, peer_up, peer_down, norm_final):
    weights = (norm_mix, w_in, conv_w, a_log, dt_bias, dn_norm, w_pool, pool_scale, w_branch, w_out,
               norm_ffn, peer_query, peer_subkeys, peer_up, peer_down)
    Bp = x_prompt.shape[0]
    zd = jnp.zeros((Bp, DN_HEADS, DN_HEAD_DIM, DN_HEAD_DIM), state_delta.dtype)
    zc = jnp.zeros((Bp, CONV_WIDTH - 1, 3 * DN_WIDTH), x_prompt.dtype)
    zp = jnp.zeros((Bp, POOL_BUF, POOL_WIDTH), x_prompt.dtype)
    y_prompt, delta_p, conv_p, win_p, pool_p = _trunk(
        x_prompt, 0, True, [zd] * DEPTH, [zc] * DEPTH, None, [zp] * DEPTH, weights, norm_final)
    y_sample, delta_s, conv_s, win_s, pool_s = _trunk(
        x_sample, PAST_LEN, False, state_delta, state_conv, (cache_win0, cache_win1, cache_win2), state_pool,
        weights, norm_final)
    return (y_prompt, y_sample, delta_p, delta_s, conv_p, conv_s,
            win_p[0], win_s[0], win_p[1], win_s[1], win_p[2], win_s[2], pool_p, pool_s)


_drawn_inputs = setup_inputs


def setup_inputs(seed=0):
    import zlib

    import numpy as np

    out = dict(_drawn_inputs(seed))
    spreads = {}
    factors = {}
    for name, (base, spread) in spreads.items():
        noise = np.random.default_rng([zlib.crc32(name.encode()), seed]).standard_normal(out[name].shape)
        drawn = base * np.exp(spread * noise) if base else spread * noise
        out[name] = jnp.asarray(drawn.astype(out[name].dtype))
    for name, factor in factors.items():
        out[name] = (out[name] * factor).astype(out[name].dtype)
    return out
```

```python
import numpy as np
from contextlib import ExitStack

import concourse.bass as bass
from concourse import mybir

F32 = mybir.dt.float32
U32 = mybir.dt.uint32
ALU = mybir.AluOpType
ACT = mybir.ActivationFunctionType
AX = mybir.AxisListType

D = 1024
DEPTH = 2
SEQ, NB, NT = 512, 8, 8
PAST = 256
EPS = 1e-6
H, HD = 4, 128
QKV = 3 * H * HD
CONV = 4
GROUPS = ((128, 1), (512, 4), (2048, 16))
SLOTS, SD = 4, 64
SW = len(GROUPS) * SLOTS * SD
POOLS = (2, 4, 8, 16)
PG = 384
PW = len(POOLS) * PG
PBUF = max(POOLS) - 1
C_Z, C_AB, C_B = QKV, QKV + 512, QKV + 512 + 2 * H
C_U = C_B + 3 * SW
C_G = C_U + PW
IN_COLS = C_G + 3 * D
KEYS, PH, TOPK = 128, 8, 16
EXPERTS = KEYS * KEYS
NQ = PH * 2

P = 128
TILES = 5
KT = D // P
NS = NB * NT
TOK = SEQ + NS
ROWS = [P, P, P, P, NS]
LEVELS = 7


_names = {}


def fresh(name):
    _names[name] = _names.get(name, 0) + 1
    return f"{name}_{_names[name]}"


def cols(n):
    return slice(n * P, n * P + ROWS[n])


_at = 0
CONST = {}
for _name, _n in (("ident", P), ("upper_p", P), ("upper_s", P), ("strict_p", P), ("strict_s", P),
                  ("full_s", P), ("levels", LEVELS * P), ("amask", 256 + 512 + 512), ("smask", 832),
                  ("cos", TILES * 32), ("sin", TILES * 32), ("count", len(POOLS) * 16), ("iota", TOPK),
                  ("own", NB), ("ident2", NS)):
    CONST[_name] = (_at, _n)
    _at += _n
N_CONST = _at
NEG = -1.0e30


def constants():
    c = np.zeros((P, N_CONST), np.float32)

    def put(name, a):
        o, n = CONST[name]
        c[: a.shape[0], o:o + n] = a.reshape(a.shape[0], -1)

    i = np.arange(P)
    same = (i[:, None] // NT == i[None, :] // NT) & (i[:, None] < NS) & (i[None, :] < NS)
    le, lt = i[:, None] <= i[None, :], i[:, None] < i[None, :]
    put("ident", np.eye(P))
    put("upper_p", le * 1.0)
    put("upper_s", (le & same) * 1.0)
    put("strict_p", lt * 1.0)
    put("strict_s", (lt & same) * 1.0)
    put("full_s", same * 1.0)
    lv = [((i[None, :] >> j) % 2 == 1) & ((i[:, None] >> j) == (i[None, :] >> j) - 1) for j in range(LEVELS)]
    put("levels", np.stack(lv, 1) * 1.0)
    q, k = i[:, None], i[None, :]
    seg = [(k >= q), (k <= q)]
    for _, dil in GROUPS[1:]:
        res = (q - k) % dil == 0
        seg += [res] * 3 + [res & (k <= q)]
    put("amask", np.where(np.concatenate(seg, 1), 0.0, NEG))
    t = (np.arange(NS) % NT)[:, None]
    b = (np.arange(NS) // NT)[:, None]
    seg = [np.arange(128)[None] >= t]
    for _, dil in GROUPS[1:]:
        seg.append((PAST + t - np.arange(PAST)[None]) % dil == 0)
    for _, dil in GROUPS:
        seg.append((b == b.T) & (t.T <= t) & ((t - t.T) % dil == 0))
    put("smask", np.where(np.concatenate(seg, 1), 0.0, NEG))
    inv = np.float32(10000.0) ** (-np.arange(32, dtype=np.float32) / np.float32(32))
    pos = np.concatenate([np.arange(SEQ), PAST + np.arange(NS) % NT, np.zeros(TILES * P - TOK)])
    ang = pos.astype(np.float32).reshape(TILES, P).T[:, :, None] * inv.astype(np.float32)
    put("cos", np.cos(ang))
    put("sin", np.sin(ang))
    cnt = [1.0 / np.minimum(float(w), np.arange(16) + 1.0) for w in POOLS]
    put("count", np.tile(np.stack(cnt)[None], (P, 1, 1)))
    put("iota", np.tile(np.arange(TOPK, dtype=np.float32), (P, 1)))
    put("ident2", i[:, None] % NS == np.arange(NS)[None])
    put("own", (i[:, None] // NT == np.arange(NB)[None]) * 1.0)
    return c


class Semaphores:

    def __init__(self, make, keep):
        self.loaded = make("loaded")
        self.loaded2 = make("loaded2")
        self.loaded3 = make("loaded3")
        self.map0 = make("map0")
        self.map1 = make("map1")
        self.slab0 = make("slab0")
        self.slab1 = make("slab1")
        self.slab_free = make("slab_free")
        self.stored = make("stored")
        self.link_act = make("link_act")
        self.link_dve = make("link_dve")
        self.link_pool = make("link_pool")
        self.pe_a = make("pe_a")
        self.pe_b = make("pe_b")
        self.pe_c = make("pe_c")
        self.pe_d = make("pe_d")
        self.pe_e = make("pe_e")
        self.act_a = make("act_a")
        self.act_b = make("act_b")
        self.act_c = make("act_c")
        self.act_d = make("act_d")
        self.act_e = make("act_e")
        self.dve_a = make("dve_a")
        self.dve_b = make("dve_b")
        self.dve_c = make("dve_c")
        self.dve_d = make("dve_d")
        self.dve_e = make("dve_e")
        self.pool_a = make("pool_a")
        self.pool_b = make("pool_b")
        self.pool_c = make("pool_c")
        self.pool_d = make("pool_d")
        self.filled = make("filled")
        self.copied = make("copied")
        self.numbers = make("numbers")
        self.paced = make("paced")
        self.dots_done = make("dots_done")
        self.downs_done = make("downs_done")
        self.gelus = make("gelus")
        self.weighted = make("weighted")
        self.diagonal = make("diagonal")
        self.summed = make("summed")
        self.x_copied = make("x_copied")
        self.gate_in = make("gate_in")
        self.gate_exp = make("gate_exp")
        self.routed = make("routed")
        self.scored = make("scored")
        self.doubled = make("doubled")
        self.stored2 = keep("stored2")
        self.values = keep("values")
        self.up0 = keep("up0")
        self.up1 = keep("up1")
        self.up2 = keep("up2")
        self.up3 = keep("up3")
        self.up4 = keep("up4")
        self.up5 = keep("up5")
        self.up6 = keep("up6")
        self.up7 = keep("up7")
        self.down0 = keep("down0")
        self.down1 = keep("down1")
        self.down2 = keep("down2")
        self.down3 = keep("down3")
        self.down4 = keep("down4")
        self.down5 = keep("down5")
        self.down6 = keep("down6")
        self.down7 = keep("down7")


class State:
    pass


class Link:

    def __init__(self, eng, sem):
        self.eng, self.sem, self.n, self.base = eng, sem, 0, 0

    def __call__(self, ins):
        ins.then_inc(self.sem, 1)
        self.n += 1
        self.eng.wait_ge(self.sem, self.base + self.n)


def bc(ap, dim, n):
    v = ap.unsqueeze(dim)
    shape = list(v.shape)
    shape[dim] = n
    return v.broadcast_to(shape)


def table(g, name, rows=P):
    o, n = CONST[name]
    return g.consts[0:rows, o:o + n]


def ident(g, rows=P):
    return table(g, "ident", rows)[:, 0:rows]


def layer(ap, l):
    names = " ".join(f"d{i}" for i in range(len(ap.shape) - 1))
    first = names.split(" ")[0]
    return ap[bass.ds(l, 1)].rearrange(f"a {names} -> (a {first}) {names[len(first) + 1:]}")


def clear_semaphores(nc, g):
    with nc.Block() as block:
        @block.gpsimd
        def _(pool):
            for first, last in g.runs:
                pool.sem_clear(range(first, last + 1))


def norm_stage(nc, g, gamma, rows, transposed=True):
    s = g.s
    with ExitStack() as ctx:
        sb = lambda name, shape: ctx.enter_context(nc.sbuf_tensor(fresh(name), shape, F32))
        gam, junk, ss = sb("gam", [P, D]), sb("junk", [P, D]), sb("ss", [P, 8])
        with nc.Block() as block:
            @block.sync
            def _(sp):
                sp.dma_start(gam[:], gamma.broadcast_to([P, D])).then_inc(s.loaded, 16)

            @block.scalar
            def _(act):
                link = Link(act, s.link_act)
                act.wait_ge(s.filled, 1)
                for n in range(TILES):
                    r = ROWS[n]
                    ins = nc.scalar.activation(junk[0:r], g.x[0:r, n, :], ACT.Square, accum_out=ss[0:r, n:n + 1])
                    if n < TILES - 1:
                        link(ins)
                    else:
                        ins.then_inc(s.act_a, 1)
                act.wait_ge(s.dve_a, 1)
                nc.scalar.activation(ss[:, 0:TILES], ss[:, 0:TILES], ACT.Sqrt).then_inc(s.act_b, 1)
                if transposed:
                    for u in range(2 * TILES):
                        n, half = u // 2, u % 2
                        act.wait_ge(s.pe_a, u + 1)
                        nc.scalar.copy(g.hT[:, 4 * half:4 * half + 4, cols(n)],
                                       g.ps[:, u % 4, :].rearrange("p (k c) -> p k c", k=4)[:, :, 0:ROWS[n]]
                                       ).then_inc(s.act_c, 1)

            @block.vector
            def _(dve):
                link = Link(dve, s.link_dve)
                nc.vector.memset(ss[:], 1.0).then_inc(s.filled, 1)
                dve.wait_ge(s.act_a, 1)
                link(nc.vector.tensor_scalar(ss[:, 0:TILES], ss[:, 0:TILES], 1.0 / D, EPS, ALU.mult, ALU.add))
                nc.vector.reciprocal(ss[:, 0:TILES], ss[:, 0:TILES]).then_inc(s.dve_a, 1)
                dve.wait_ge(s.act_b, 1)
                dve.wait_ge(s.loaded, 16)
                for n in range(TILES):
                    r = ROWS[n]
                    nc.vector.scalar_tensor_tensor(out=rows[0:r, n, :], in0=g.x[0:r, n, :], scalar=ss[0:r, n:n + 1],
                                                   in1=gam[0:r, :], op0=ALU.mult, op1=ALU.mult).then_inc(s.dve_b, 1)

            if transposed:
                @block.tensor
                def _(pe):
                    for u in range(2 * TILES):
                        n, half = u // 2, u % 2
                        pe.wait_ge(s.dve_b, n + 1)
                        if u >= 4:
                            pe.wait_ge(s.act_c, u - 3)
                        for k in range(4):
                            kk = 4 * half + k
                            last = nc.tensor.transpose(g.ps[:, u % 4, k * P:k * P + ROWS[n]],
                                                       rows[0:ROWS[n], n, kk * P:(kk + 1) * P], ident(g, ROWS[n]))
                        last.then_inc(s.pe_a, 1)
    clear_semaphores(nc, g)


BANKS_A, BANKS_B = 3, 2


def project(nc, g, pe, u, weights, rhs, nk, done, free_a, free_b):
    if u >= BANKS_A:
        pe.wait_ge(free_a, u - BANKS_A + 1)
    if u >= BANKS_B:
        pe.wait_ge(free_b, u - BANKS_B + 1)
    for k in range(nk):
        nc.tensor.matmul(part_a(g, u), weights(k), rhs(k)[:, 0:SEQ], start=k == 0, stop=k == nk - 1)
        last = nc.tensor.matmul(part_b(g, u), weights(k), rhs(k)[:, SEQ:TOK], start=k == 0, stop=k == nk - 1)
    last.then_inc(done, 1)


def part_a(g, u):
    return g.ps[:, u % BANKS_A, :]


def part_b(g, u):
    return g.ps[:, BANKS_A + u % BANKS_B, 0:NS]


def load_slabs(sp, g, ring, sources):
    slab = (g.s.slab0, g.s.slab1)
    for i, src in enumerate(sources):
        if i >= 2:
            sp.wait_ge(g.s.slab_free, i - 1)
        nk, w = src.shape[1], src.shape[2]
        sp.dma_start(ring[:, i % 2, 0:nk * w].rearrange("p (k c) -> p k c", k=nk), src).then_inc(slab[i % 2], 16)


def slab_ready(eng, g, i):
    eng.wait_ge((g.s.slab0, g.s.slab1)[i % 2], 16 * (i // 2 + 1))


def slab_view(ring, i, nk, w):
    return ring[:, i % 2, 0:nk * w].rearrange("p (k c) -> p k c", k=nk)


def rows_of(w):
    return w.rearrange("(k p) c -> p k c", p=P)


EXT = CONV - 1 + SEQ + NB * (CONV - 1 + NT)
EXT_S = CONV - 1 + SEQ


def delta_stage(nc, g, t, o, l):
    s = g.s
    w_in = layer(t["w_in"], l)
    with ExitStack() as ctx:
        sb = lambda name, shape, dt=F32, c=ctx: c.enter_context(nc.sbuf_tensor(fresh(name), shape, dt))
        zT, cc = sb("zT", [P, 4, TOK]), sb("cc", [P, 12, TOK])
        vecs, ab = sb("vecs", [P, 64]), sb("ab", [P, TILES, 8])
        heads, gb = sb("heads", [P, 8]), sb("gb", [P, TILES, 8])
        with ExitStack() as inner:
            delta_in(nc, g, t, o, l, w_in, zT, cc, vecs, ab, heads, lambda n, sh: sb(n, sh, F32, inner))
        clear_semaphores(nc, g)
        with ExitStack() as inner:
            delta_chunks(nc, g, t, o, l, zT, cc, vecs, ab, heads, gb, lambda n, sh: sb(n, sh, F32, inner))


def delta_in(nc, g, t, o, l, w_in, zT, cc, vecs, ab, heads, sb):
    s = g.s
    ring, wab = sb("ring", [P, 2, 4096]), sb("wab", [P, KT, 8])
    ext, tail = sb("ext", [P, 12, EXT]), sb("tail", [P, 12, 27])
    vrows, old, new = sb("vrows", [61, P]), sb("old", [24, QKV]), sb("new", [27, QKV])
    sq, rn = sb("sq", [P, 4, TOK]), sb("rn", [P, 4, TOK])
    ones = g.ones
    samples = ext[:, :, EXT_S:EXT].rearrange("p c (b j) -> p c b j", b=NB)
    with nc.Block() as block:
        @block.sync
        def _(sp):
            sp.dma_start(vrows[0:48], layer(t["conv_w"], l).rearrange("w (c p) -> (w c) p", p=P)).then_inc(s.loaded, 16)
            sp.dma_start(vrows[48:60], layer(t["pool_scale"].rearrange("l (c p) -> l c p", p=P), l)).then_inc(s.loaded, 16)
            sp.dma_start(vrows[60:61], t["dn_norm"][bass.ds(l, 1)]).then_inc(s.loaded, 16)
            sp.dma_start(old[:], layer(t["state_conv"], l).rearrange("b j c -> (b j) c")).then_inc(s.loaded, 16)
            sp.dma_start(wab[:], rows_of(w_in)[:, :, C_AB:C_AB + 8]).then_inc(s.loaded2, 16)
            sp.dma_start(heads[:, 0:4], t["a_log"][bass.ds(l, 1)].broadcast_to([P, 4])).then_inc(s.loaded3, 16)
            sp.dma_start(heads[:, 4:8], t["dt_bias"][bass.ds(l, 1)].broadcast_to([P, 4])).then_inc(s.loaded3, 16)
            load_slabs(sp, g, ring, [rows_of(w_in)[:, :, i * 512:(i + 1) * 512] for i in range(4)])
            sp.wait_ge(s.act_d, 3)
            sp.dma_start(layer(o["conv_p"], l).rearrange("b j c -> (b j) c"), new[0:3]).then_inc(s.stored, 16)
            sp.dma_start(layer(o["conv_s"], l).rearrange("b j c -> (b j) c"), new[3:27]).then_inc(s.stored, 16)
            sp.wait_ge(s.stored, 32)
            sp.wait_ge(s.loaded3, 32)

        @block.tensor
        def _(pe):
            pe.wait_ge(s.loaded, 64)
            nc.tensor.transpose(g.ps[:, 5, 0:61], vrows[:], ident(g, 61))
            for c in range(12):
                last = nc.tensor.transpose(g.ps[:, 5, 64 + c * 24:64 + (c + 1) * 24], old[:, c * P:(c + 1) * P], ident(g, 24))
            last.then_inc(s.pe_b, 1)
            for u in range(16):
                if u % 4 == 0:
                    slab_ready(pe, g, u // 4)
                w = slab_view(ring, u // 4, KT, 512)
                project(nc, g, pe, u, lambda k: w[:, k, (u % 4) * P:(u % 4 + 1) * P], lambda k: g.hT[:, k, :], KT,
                        s.pe_a, s.act_a, s.dve_a)
                if u % 4 == 3:
                    pe.wait_ge(s.pe_a, u + 1)
                    pe.sem_inc(s.slab_free, 1)
            pe.wait_ge(s.loaded2, 16)
            for n in range(TILES):
                for k in range(KT):
                    last = nc.tensor.matmul(g.ps[0:ROWS[n], 6, n * 8:n * 8 + 8], g.hT[:, k, cols(n)], wab[:, k, :],
                                            start=k == 0, stop=k == KT - 1)
            last.then_inc(s.pe_c, 1)
            pe.wait_ge(s.dve_b, 1)
            for c in range(12):
                last = nc.tensor.transpose(g.ps[0:27, c // 4, (c % 4) * P:(c % 4 + 1) * P], tail[:, c, :], ident(g))
                if c % 4 == 3:
                    last.then_inc(s.pe_d, 1)
            pe.wait_ge(s.act_d, 3)
            for r in range(2):
                pe.wait_ge(s.act_e, r + 1)
                if r:
                    pe.wait_ge(s.dve_d, 1)
                for c in range(4):
                    nc.tensor.matmul(g.ps[:, c, :], ones[:], sq[:, c, 0:SEQ], start=True, stop=True)
                    last = nc.tensor.matmul(g.ps[:, 4, c * NS:(c + 1) * NS], ones[:], sq[:, c, SEQ:TOK], start=True, stop=True)
                last.then_inc(s.pe_e, 1)

        @block.gpsimd
        def _(pool):
            nc.gpsimd.memset(ext[:, :, 0:CONV - 1], 0.0).then_inc(s.filled, 1)
            nc.gpsimd.memset(ab[:], 0.0).then_inc(s.filled, 1)

        @block.scalar
        def _(act):
            act.wait_ge(s.pe_b, 1)
            nc.scalar.copy(vecs[:, 0:61], g.ps[:, 5, 0:61]).then_inc(s.act_b, 1)
            nc.scalar.copy(samples[:, :, :, 0:CONV - 1],
                           g.ps[:, 5, 64:352].rearrange("p (c b j) -> p c b j", c=12, b=NB)).then_inc(s.act_b, 1)
            for u in range(16):
                act.wait_ge(s.pe_a, u + 1)
                dst = ext[:, u, CONV - 1:EXT_S] if u < 12 else zT[:, u - 12, 0:SEQ]
                nc.scalar.copy(dst, part_a(g, u)).then_inc(s.act_a, 1)
            for c in range(12):
                act.wait_ge(s.dve_c, c + 1)
                nc.scalar.activation(cc[:, c, :], cc[:, c, :], ACT.Silu).then_inc(s.act_c, 1)
            for j in range(3):
                act.wait_ge(s.pe_d, j + 1)
                nc.scalar.copy(new[:, j * 512:(j + 1) * 512], g.ps[0:27, j, :]).then_inc(s.act_d, 1)
            for r in range(2):
                if r:
                    act.wait_ge(s.pe_e, 1)
                act.wait_ge(s.act_c, 12)
                nc.scalar.activation(sq[:], cc[:, 4 * r:4 * r + 4, :], ACT.Square).then_inc(s.act_e, 1)
                act.wait_ge(s.dve_e, r + 1)
                nc.scalar.activation(rn[:], rn[:], ACT.Sqrt).then_inc(s.copied, 1)

        @block.vector
        def _(dve):
            link = Link(dve, s.link_dve)
            for u in range(16):
                dve.wait_ge(s.pe_a, u + 1)
                if u < 12:
                    nc.vector.tensor_copy(samples[:, u, :, CONV - 1:], part_b(g, u).rearrange("p (b j) -> p b j", b=NB)
                                          ).then_inc(s.dve_a, 1)
                else:
                    nc.vector.tensor_copy(zT[:, u - 12, SEQ:TOK], part_b(g, u)).then_inc(s.dve_a, 1)
            dve.wait_ge(s.pe_c, 1)
            dve.wait_ge(s.filled, 2)
            link(nc.vector.tensor_copy(ab[:, 0:4, :], g.ps[:, 6, 0:32].rearrange("p (n c) -> p n c", n=4)))
            link(nc.vector.tensor_copy(ab[0:NS, 4, :], g.ps[0:NS, 6, 32:40]))
            dve.wait_ge(s.act_a, 16)
            dve.wait_ge(s.act_b, 2)
            dve.wait_ge(s.dve_a, 16)
            link(nc.vector.tensor_copy(tail[:, :, 0:3], ext[:, :, EXT_S - 3:EXT_S]))
            nc.vector.tensor_copy(tail[:, :, 3:27].rearrange("p c (b j) -> p c b j", b=NB), samples[:, :, :, NT:NT + 3]
                                  ).then_inc(s.dve_b, 1)
            for c in range(12):
                ins_p = lambda w: ext[:, c, w:w + SEQ]
                ins_s = lambda w: samples[:, c, :, w:w + NT]
                out_p, out_s = cc[:, c, 0:SEQ], cc[:, c, SEQ:TOK].rearrange("p (b j) -> p b j", b=NB)
                wt = lambda w: vecs[:, w * 12 + c:w * 12 + c + 1]
                nc.vector.tensor_scalar(out_p, ins_p(0), wt(0), None, ALU.mult).then_inc(s.link_dve, 1)
                link.n += 1
                link(nc.vector.tensor_scalar(out_s, ins_s(0), wt(0), None, ALU.mult))
                for w in range(1, CONV):
                    nc.vector.scalar_tensor_tensor(out=out_p, in0=ins_p(w), scalar=wt(w), in1=out_p, op0=ALU.mult,
                                                   op1=ALU.add).then_inc(s.link_dve, 1)
                    link.n += 1
                    last = nc.vector.scalar_tensor_tensor(out=out_s, in0=ins_s(w), scalar=wt(w), in1=out_s,
                                                          op0=ALU.mult, op1=ALU.add)
                    if w < CONV - 1:
                        link(last)
                last.then_inc(s.dve_c, 1)
            for r in range(2):
                dve.wait_ge(s.pe_e, r + 1)
                link(nc.vector.tensor_scalar(rn[:, :, 0:SEQ], g.ps[:, 0:4, :], EPS, None, ALU.add))
                link(nc.vector.tensor_scalar(rn[:, :, SEQ:TOK], g.ps[:, 4, 0:4 * NS].rearrange("p (c n) -> p c n", c=4),
                                             EPS, None, ALU.add))
                dve.sem_inc(s.dve_d, 1)
                nc.vector.reciprocal(rn[:], rn[:]).then_inc(s.dve_e, 1)
                dve.wait_ge(s.copied, r + 1)
                q = cc[:, 4 * r:4 * r + 4, :]
                link(nc.vector.scalar_tensor_tensor(out=q, in0=rn[:], scalar=HD ** -0.5 if r == 0 else 1.0, in1=q,
                                                    op0=ALU.mult, op1=ALU.mult))


def heads_of(a, n):
    r = ROWS[n]
    return a[0:r, n * 512:n * 512 + H * r].rearrange("p (h c) -> p h c", h=H)


SQ = 4 * 512 + H * NS


def delta_chunks(nc, g, t, o, l, zT, cc, vecs, ab, heads, gb, sb):
    s = g.s
    krow, vrow = sb("krow", [P, TILES, 512]), sb("vrow", [P, TILES, 512])
    dec, low, lowm, inv, invT, mid = (sb(n, [P, SQ]) for n in ("dec", "low", "lowm", "inv", "invT", "mid"))
    kbg = sb("kbg", [P, TILES, 512])
    st = sb("st", [P, H, NB, HD])
    cl, lastg = sb("cl", [P, TILES, 12]), sb("lastg", [P, 4 * H + H * NB])
    qT = lambda n, h: cc[:, h, cols(n)]
    kT = lambda n, h: cc[:, 4 + h, cols(n)]
    upper = lambda n: table(g, "upper_p" if n < 4 else "upper_s", ROWS[n])[:, 0:ROWS[n]]
    strict = lambda n: table(g, "strict_p" if n < 4 else "strict_s", ROWS[n])[:, 0:ROWS[n]]
    full = lambda n: (g.ones[:] if n < 4 else table(g, "full_s", NS)[:, 0:NS])
    level = lambda n, j: table(g, "levels", ROWS[n])[:, j * P:j * P + ROWS[n]]
    row = lambda a, n: a[0:ROWS[n], n, :].rearrange("p (h d) -> p h d", h=H)
    bank = lambda b, r, w: g.ps[0:r, b, 0:H * w].rearrange("p (h c) -> p h c", h=H)
    run = lambda j: [n for n in range(TILES) if n < 4 or j < 3]
    todo = [(j, n) for j in range(LEVELS) for n in run(j)]
    egr = st[:, 0:4].rearrange("p h b d -> p (h b d)")

    with nc.Block() as block:
        @block.tensor
        def _(pe):
            for u in range(2 * TILES):
                n, v = u // 2, u % 2
                if u >= 2:
                    pe.wait_ge(s.act_a, u - 1)
                for h in range(H):
                    last = nc.tensor.transpose(g.ps[0:ROWS[n], u % 2, h * P:(h + 1) * P], cc[:, 4 + 4 * v + h, cols(n)], ident(g))
                last.then_inc(s.pe_a, 1)
            for n in range(TILES):
                r = ROWS[n]
                pe.wait_ge(s.dve_b, n + 1)
                nc.tensor.matmul(bank(2, P, r), g.ones[0:r, :], heads_of(lowm, n), start=True, stop=True)
                nc.tensor.matmul(bank(3, P, r), g.ones[0:r, :], heads_of(mid, n), start=True, stop=True)
                nc.tensor.matmul(g.ps[0:r, 4, 0:4], upper(n), gb[0:r, n, 0:4], start=True, stop=True)
                nc.tensor.matmul(g.ps[0:r, 4, 4:8], full(n), gb[0:r, n, 0:4], start=True, stop=True)
                for h in range(H):
                    nc.tensor.matmul(g.ps[0:r, 5, h * r:(h + 1) * r], kT(n, h), kT(n, h), start=True, stop=True)
                for h in range(H):
                    last = nc.tensor.matmul(g.ps[0:r, 6, h * r:(h + 1) * r], kT(n, h), qT(n, h), start=True, stop=True)
                last.then_inc(s.pe_b, 1)

        @block.scalar
        def _(act):
            link = Link(act, s.link_act)
            act.wait_ge(s.dve_a, 1)
            link(nc.scalar.activation(ab[:, :, 0:4], ab[:, :, 0:4], ACT.Exp, scale=-1.0))
            link(nc.scalar.activation(heads[:, 0:4], heads[:, 0:4], ACT.Exp))
            nc.scalar.activation(ab[:, :, 0:4], ab[:, :, 0:4], ACT.Ln, bias=1.0).then_inc(s.act_b, 1)
            nc.scalar.activation(gb[:, :, 4:8], ab[:, :, 4:8], ACT.Sigmoid).then_inc(s.act_b, 1)
            for u in range(2 * TILES):
                n, v = u // 2, u % 2
                act.wait_ge(s.pe_a, u + 1)
                nc.scalar.copy((vrow if v else krow)[0:ROWS[n], n, :], g.ps[0:ROWS[n], u % 2, :]).then_inc(s.act_a, 1)
            for n in range(TILES):
                r = ROWS[n]
                act.wait_ge(s.pe_b, n + 1)
                if n >= 2:
                    act.wait_ge(s.dve_c, n - 1)
                nc.scalar.activation(egr[:, (n % 2) * 512:(n % 2) * 512 + H * r].rearrange("p (h c) -> p h c", h=H),
                                     bank(2, P, r), ACT.Exp).then_inc(s.act_c, 1)
                act.wait_ge(s.dve_d, n + 1)
                nc.scalar.activation(heads_of(dec, n), heads_of(dec, n), ACT.Exp).then_inc(s.act_d, 1)
                nc.scalar.activation(cl[0:r, n, 0:8], cl[0:r, n, 0:8], ACT.Exp).then_inc(s.act_d, 1)

        @block.vector
        def _(dve):
            link = Link(dve, s.link_dve)
            dt = bc(heads[:, 4:8], 1, TILES)
            a = ab[:, :, 0:4]
            link(nc.vector.tensor_tensor(a, a, dt, ALU.add))
            link(nc.vector.tensor_scalar(gb[:, :, 0:4], a, 0.0, None, ALU.max))
            link(nc.vector.tensor_scalar(cl[:, :, 0:4], a, -1.0, None, ALU.mult))
            nc.vector.tensor_tensor(a, a, cl[:, :, 0:4], ALU.max).then_inc(s.dve_a, 1)
            dve.wait_ge(s.act_b, 2)
            link(nc.vector.tensor_tensor(gb[:, :, 0:4], gb[:, :, 0:4], a, ALU.add))
            link(nc.vector.scalar_tensor_tensor(out=gb[:, :, 0:4], in0=gb[:, :, 0:4], scalar=-1.0,
                                                in1=bc(heads[:, 0:4], 1, TILES), op0=ALU.mult, op1=ALU.mult))
            for n in range(TILES):
                r = ROWS[n]
                link(nc.vector.tensor_tensor(heads_of(lowm, n), bc(upper(n), 1, H), bc(gb[0:r, n, 0:4], 2, r), ALU.mult))
                link(nc.vector.tensor_tensor(heads_of(mid, n), bc(ident(g, r), 1, H), bc(gb[0:r, n, 4:8], 2, r), ALU.mult))
                dve.sem_inc(s.dve_b, 1)
                dve.wait_ge(s.pe_b, n + 1)
                link(nc.vector.tensor_copy(cl[0:r, n, 0:8], g.ps[0:r, 4, 0:8]))
                dve.wait_ge(s.act_c, n + 1)
                link(nc.vector.tensor_tensor(heads_of(dec, n), bank(2, r, r), bc(cl[0:r, n, 0:4], 2, r), ALU.subtract))
                link(nc.vector.tensor_scalar(heads_of(dec, n), heads_of(dec, n), 0.0, None, ALU.min))
                nc.vector.tensor_tensor(cl[0:r, n, 4:8], cl[0:r, n, 4:8], cl[0:r, n, 0:4], ALU.subtract).then_inc(s.dve_d, 1)
                dve.wait_ge(s.act_d, 2 * n + 2)
                link(nc.vector.tensor_tensor(heads_of(dec, n), heads_of(dec, n), bc(upper(n), 1, H), ALU.mult))
                link(nc.vector.tensor_tensor(heads_of(low, n), heads_of(dec, n), bank(3, r, r), ALU.mult))
                link(nc.vector.tensor_tensor(heads_of(low, n), heads_of(low, n), bc(strict(n), 1, H), ALU.mult))
                link(nc.vector.tensor_tensor(heads_of(low, n), heads_of(low, n), bank(5, r, r), ALU.mult))
                link(nc.vector.tensor_tensor(heads_of(dec, n), heads_of(dec, n), bank(6, r, r), ALU.mult))
                e = egr[:, (n % 2) * 512:(n % 2) * 512 + H * r].rearrange("p (h c) -> p h c", h=H)
                dve.wait_ge(s.act_c, n + 1)
                link(nc.vector.tensor_tensor(cc[:, 0:H, cols(n)], cc[:, 0:H, cols(n)], e, ALU.mult))
                if n < 4:
                    ins = nc.vector.tensor_copy(lastg[:, 4 * n:4 * n + 4], e[:, :, r - 1])
                else:
                    ins = nc.vector.tensor_copy(lastg[:, 16:48].rearrange("p (h b) -> p h b", h=H),
                                                e.rearrange("p h (b j) -> p h b j", j=NT)[:, :, :, NT - 1])
                link(ins)
                dve.sem_inc(s.dve_c, 1)
                link(nc.vector.tensor_tensor(cl[0:r, n, 8:12], gb[0:r, n, 4:8], cl[0:r, n, 0:4], ALU.mult))
                link(nc.vector.tensor_copy(heads_of(inv, n), bc(ident(g, r), 1, H)))
                link(nc.vector.tensor_copy(heads_of(invT, n), bc(ident(g, r), 1, H)))
                dve.sem_inc(s.dve_e, 1)

        @block.gpsimd
        def _(pool):
            for n in range(TILES):
                r = ROWS[n]
                pool.wait_ge(s.dve_e, n + 1)
                pool.wait_ge(s.act_a, 2 * n + 2)
                nc.gpsimd.tensor_tensor(row(kbg, n), row(krow, n), bc(cl[0:r, n, 8:12], 2, HD), ALU.mult).then_inc(s.pool_a, 1)
                pool.wait_ge(s.pool_a, 2 * n + 1)
                nc.gpsimd.tensor_tensor(row(krow, n), row(krow, n), bc(cl[0:r, n, 4:8], 2, HD), ALU.mult).then_inc(s.pool_b, 1)
                nc.gpsimd.tensor_tensor(row(vrow, n), row(vrow, n), bc(gb[0:r, n, 4:8], 2, HD), ALU.mult).then_inc(s.pool_a, 1)
    clear_semaphores(nc, g)

    with nc.Block() as block:
        @block.gpsimd
        def _(pool):
            for i, (j, n) in enumerate(todo):
                if j > 0:
                    pool.wait_ge(s.pe_a, todo.index((j - 1, n)) + 1)
                nc.gpsimd.tensor_tensor(heads_of(lowm, n), heads_of(low, n), bc(level(n, j), 1, H), ALU.mult).then_inc(s.pool_a, 1)

        @block.tensor
        def _(pe):
            for j in range(LEVELS):
                for n in run(j):
                    i, r = todo.index((j, n)), ROWS[n]
                    pe.wait_ge(s.pool_a, i + 1)
                    if j > 0:
                        pe.wait_ge(s.dve_a, todo.index((j - 1, n)) + 1)
                    if i >= 2:
                        pe.wait_ge(s.act_a, i - 1)
                    for h in range(H):
                        last = nc.tensor.matmul(g.ps[0:r, i % 2, h * r:(h + 1) * r], heads_of(lowm, n)[:, h], heads_of(inv, n)[:, h],
                                                start=True, stop=True)
                    last.then_inc(s.pe_a, 1)
                for n in run(j):
                    i, r = todo.index((j, n)), ROWS[n]
                    pe.wait_ge(s.act_a, i + 1)
                    if i >= 2:
                        pe.wait_ge(s.dve_a, i - 1)
                    for h in range(H):
                        nc.tensor.matmul(g.ps[0:r, 2 + i % 2, h * r:(h + 1) * r], heads_of(invT, n)[:, h], heads_of(mid, n)[:, h],
                                         start=True, stop=True)
                        last = nc.tensor.matmul(g.ps[0:r, 4 + i % 2, h * r:(h + 1) * r], heads_of(mid, n)[:, h],
                                                heads_of(invT, n)[:, h], start=True, stop=True)
                    last.then_inc(s.pe_b, 1)

        @block.scalar
        def _(act):
            for i, (j, n) in enumerate(todo):
                act.wait_ge(s.pe_a, i + 1)
                if j > 0:
                    act.wait_ge(s.pe_b, todo.index((j - 1, n)) + 1)
                nc.scalar.copy(heads_of(mid, n), bank(i % 2, ROWS[n], ROWS[n])).then_inc(s.act_a, 1)

        @block.vector
        def _(dve):
            link = Link(dve, s.link_dve)
            for i, (j, n) in enumerate(todo):
                r = ROWS[n]
                dve.wait_ge(s.pe_b, i + 1)
                nc.vector.tensor_tensor(heads_of(inv, n), heads_of(inv, n), bank(2 + i % 2, r, r), ALU.subtract
                                        ).then_inc(s.link_dve, 1)
                nc.vector.tensor_tensor(heads_of(invT, n), heads_of(invT, n), bank(4 + i % 2, r, r), ALU.subtract
                                        ).then_inc(s.dve_a, 1)
    clear_semaphores(nc, g)

    state = low[:, 0:512].rearrange("p (h e) -> p h e", h=H)
    vnew = low[:, 512:1536].rearrange("p (i h e) -> p i h e", i=2, h=H)
    ws = low[:, 1536:1536 + H * NS].rearrange("p (h c) -> p h c", h=H)
    kdm = lowm[0:NS, 0:2048].rearrange("p (i b d) -> p i b d", i=2, b=NB)
    wT = mid
    sd_out = layer(o["delta_s"], l)
    with nc.Block() as block:
        @block.sync
        def _(sp):
            for h in range(H):
                sp.dma_start(st[:, h], layer(t["state_delta"], l)[:, h].rearrange("b d e -> d b e")).then_inc(s.loaded, 16)
            sp.wait_ge(s.dve_b, 4)
            sp.dma_start(layer(o["delta_p"], l)[0].rearrange("h d e -> d h e"), state).then_inc(s.stored, 16)
            for h in range(H):
                sp.wait_ge(s.dve_c, 2 * h + 2)
                sp.dma_start(sd_out[:, h].rearrange("b d e -> d b e"), st[:, h]).then_inc(s.stored, 16)
            sp.wait_ge(s.stored, 16 * 5)

        @block.tensor
        def _(pe):
            for n in range(TILES):
                r = ROWS[n]
                if n >= 2:
                    pe.wait_ge(s.act_a, n - 1)
                for h in range(H):
                    last = nc.tensor.matmul(g.ps[:, n % 2, h * r:(h + 1) * r], row(kbg, n)[:, h], heads_of(invT, n)[:, h],
                                            start=True, stop=True)
                last.then_inc(s.pe_a, 1)
            for n in range(4):
                pe.wait_ge(s.act_a, n + 1)
                if n:
                    pe.wait_ge(s.dve_b, n)
                else:
                    pe.wait_ge(s.filled, 1)
                for h in range(H):
                    nc.tensor.matmul(g.ps[:, 2, h * P:(h + 1) * P], heads_of(invT, n)[:, h], row(vrow, n)[:, h], start=True, stop=False)
                    last = nc.tensor.matmul(g.ps[:, 2, h * P:(h + 1) * P], wT[:, n * 512 + h * P:n * 512 + (h + 1) * P], state[:, h],
                                            start=False, stop=True)
                last.then_inc(s.pe_b, 1)
                pe.wait_ge(s.act_b, n + 1)
                for h in range(H):
                    last = nc.tensor.matmul(g.ps[:, 4, h * P:(h + 1) * P], row(krow, n)[:, h], vnew[:, n % 2, h], start=True, stop=True)
                last.then_inc(s.pe_c, 1)
                if n:
                    pe.wait_ge(s.act_c, n)
                for h in range(H):
                    nc.tensor.matmul(g.ps[:, 3, h * P:(h + 1) * P], state[:, h], qT(n, h), start=True, stop=False)
                    last = nc.tensor.matmul(g.ps[:, 3, h * P:(h + 1) * P], vnew[:, n % 2, h], heads_of(dec, n)[:, h],
                                            start=False, stop=True)
                last.then_inc(s.pe_d, 1)
            pe.wait_ge(s.loaded, 64)
            pe.wait_ge(s.act_a, 5)
            for h in range(H):
                for b in range(NB):
                    c = h * NS + b * NT
                    last = nc.tensor.matmul(g.ps[:, 5, c:c + NT], st[:, h, b], wT[:, 2048 + c:2048 + c + NT], start=True, stop=True)
            last.then_inc(s.pe_b, 1)
            pe.wait_ge(s.act_b, 5)
            for h in range(H):
                nc.tensor.matmul(g.ps[0:NS, 6, h * P:(h + 1) * P], heads_of(invT, 4)[:, h], row(vrow, 4)[:, h], start=True, stop=False)
                last = nc.tensor.matmul(g.ps[0:NS, 6, h * P:(h + 1) * P], ws[:, h], ident(g), start=False, stop=True)
            last.then_inc(s.pe_b, 1)
            pe.wait_ge(s.act_b, 6)
            for h in range(H):
                c = h * NS
                nc.tensor.matmul(g.ps[:, 7, c:c + NS], vnew[0:NS, 0, h], heads_of(dec, 4)[:, h], start=True, stop=False)
                for b in range(NB):
                    last = nc.tensor.matmul(g.ps[:, 7, c + b * NT:c + (b + 1) * NT], st[:, h, b], cc[:, h, SEQ + b * NT:SEQ + (b + 1) * NT],
                                            start=False, stop=b == NB - 1)
            last.then_inc(s.pe_d, 1)
            for u in range(2 * H):
                h, half = u // 2, u % 2
                pe.wait_ge(s.pool_a, h + 1)
                if u >= 2:
                    pe.wait_ge(s.dve_c, u - 1)
                for b in range(4):
                    last = nc.tensor.matmul(g.ps[:, u % 2, b * P:(b + 1) * P], kdm[:, h % 2, 4 * half + b], vnew[0:NS, 0, h],
                                            start=True, stop=True)
                last.then_inc(s.pe_e, 1)

        @block.gpsimd
        def _(pool):
            for h in range(H):
                if h >= 2:
                    pool.wait_ge(s.pe_e, 2 * (h - 1))
                nc.gpsimd.tensor_tensor(kdm[:, h % 2], bc(row(krow, 4)[:, h], 1, NB), bc(table(g, "own", NS), 2, HD), ALU.mult
                                        ).then_inc(s.pool_a, 1)

        @block.scalar
        def _(act):
            for n in range(TILES):
                act.wait_ge(s.pe_a, n + 1)
                r = ROWS[n]
                nc.scalar.mul(wT[:, n * 512:n * 512 + H * r], g.ps[:, n % 2, 0:H * r], -1.0).then_inc(s.act_a, 1)
            for n in range(4):
                act.wait_ge(s.pe_b, n + 1)
                if n >= 2:
                    act.wait_ge(s.pe_d, n - 1)
                nc.scalar.copy(vnew[:, n % 2], bank(2, P, HD)).then_inc(s.act_b, 1)
                act.wait_ge(s.pe_d, n + 1)
                nc.scalar.copy(g.oa[:, :, cols(n)], bank(3, P, P)).then_inc(s.act_c, 1)
            act.wait_ge(s.pe_b, 5)
            nc.scalar.copy(ws, bank(5, P, NS)).then_inc(s.act_b, 1)
            act.wait_ge(s.pe_b, 6)
            nc.scalar.copy(vnew[0:NS, 0], bank(6, NS, HD)).then_inc(s.act_b, 1)
            act.wait_ge(s.pe_d, 5)
            nc.scalar.copy(g.oa[:, :, cols(4)], bank(7, P, NS)).then_inc(s.act_c, 1)

        @block.vector
        def _(dve):
            link = Link(dve, s.link_dve)
            nc.vector.memset(state, 0.0).then_inc(s.filled, 1)
            for n in range(4):
                dve.wait_ge(s.pe_c, n + 1)
                dve.wait_ge(s.pe_d, n + 1)
                dve.wait_ge(s.filled, 1)
                link(nc.vector.tensor_tensor(state, state, bc(lastg[:, 4 * n:4 * n + 4], 2, HD), ALU.mult))
                nc.vector.tensor_tensor(state, state, bank(4, P, HD), ALU.add).then_inc(s.dve_b, 1)
                dve.wait_ge(s.dve_b, n + 1)
            dve.wait_ge(s.pe_d, 5)
            for u in range(2 * H):
                h, half = u // 2, u % 2
                part = st[:, h, 4 * half:4 * half + 4]
                k = 16 + h * NB + 4 * half
                link(nc.vector.tensor_tensor(part, part, bc(lastg[:, k:k + 4], 2, HD), ALU.mult))
                dve.wait_ge(s.pe_e, u + 1)
                nc.vector.tensor_tensor(part, part, g.ps[:, u % 2, :].rearrange("p (b e) -> p b e", b=4), ALU.add).then_inc(s.dve_c, 1)
    clear_semaphores(nc, g)

    sq, rn = dec[:].rearrange("p (h c) -> p h c", h=H), lowm[:].rearrange("p (h c) -> p h c", h=H)
    with nc.Block() as block:
        @block.scalar
        def _(act):
            nc.scalar.activation(sq, g.oa[:], ACT.Square).then_inc(s.act_a, 1)
            nc.scalar.activation(zT[:], zT[:], ACT.Silu).then_inc(s.act_b, 1)
            act.wait_ge(s.dve_a, 1)
            nc.scalar.activation(rn, rn, ACT.Sqrt).then_inc(s.act_c, 1)

        @block.tensor
        def _(pe):
            pe.wait_ge(s.act_a, 1)
            for h in range(H):
                nc.tensor.matmul(g.ps[:, h, :], g.ones[:], sq[:, h, 0:SEQ], start=True, stop=True)
                last = nc.tensor.matmul(g.ps[:, 4, h * NS:(h + 1) * NS], g.ones[:], sq[:, h, SEQ:TOK], start=True, stop=True)
            last.then_inc(s.pe_a, 1)

        @block.vector
        def _(dve):
            link = Link(dve, s.link_dve)
            dve.wait_ge(s.pe_a, 1)
            link(nc.vector.tensor_scalar(rn[:, :, 0:SEQ], g.ps[:, 0:4, :], 1.0 / HD, EPS, ALU.mult, ALU.add))
            link(nc.vector.tensor_scalar(rn[:, :, SEQ:TOK], bank(4, P, NS), 1.0 / HD, EPS, ALU.mult, ALU.add))
            nc.vector.reciprocal(rn, rn).then_inc(s.dve_a, 1)
            dve.wait_ge(s.act_b, 1)
            link(nc.vector.tensor_tensor(g.oa[:], g.oa[:], zT[:], ALU.mult))
            dve.wait_ge(s.act_c, 1)
            link(nc.vector.scalar_tensor_tensor(out=g.oa[:], in0=g.oa[:], scalar=vecs[:, 60:61], in1=rn, op0=ALU.mult, op1=ALU.mult))
            nc.vector.tensor_copy(g.pscale[:], vecs[:, 48:60]).then_inc(s.dve_b, 1)
    clear_semaphores(nc, g)


def window_stage(nc, g, t, o, l):
    s = g.s
    w_in = layer(t["w_in"], l)
    with ExitStack() as ctx:
        sb = lambda name, shape, c=ctx: c.enter_context(nc.sbuf_tensor(fresh(name), shape, F32))
        vals = sb("vals", [P, TILES, SW])
        qkT = sb("qkT", [P, 12, TOK])
        with ExitStack() as inner:
            window_in(nc, g, t, o, l, w_in, vals, qkT, lambda n, sh: sb(n, sh, inner))
        clear_semaphores(nc, g)
        with ExitStack() as inner:
            window_prompt(nc, g, vals, qkT, lambda n, sh: sb(n, sh, inner))
        clear_semaphores(nc, g)
        with ExitStack() as inner:
            window_samples(nc, g, t, l, vals, qkT, lambda n, sh: sb(n, sh, inner))
        clear_semaphores(nc, g)


WB = 384


def window_in(nc, g, t, o, l, w_in, vals, qkT, sb):
    s = g.s
    ring = sb("ring", [P, 2, KT * WB])
    qk = sb("qk", [P, TILES, 2 * SW])
    tmp = sb("tmp", [P, 2, 4 * 24 * 32])
    half = lambda n, i: qk[0:ROWS[n], n, :].rearrange("p (h a d) -> p h a d", h=24, a=2)[:, :, i]
    trig = lambda name, n: bc(table(g, name, ROWS[n])[:, n * 32:(n + 1) * 32], 1, 24)
    work = lambda n, i: tmp[0:ROWS[n], n % 2, i * 768:(i + 1) * 768].rearrange("p (h d) -> p h d", h=24)
    heads2 = lambda ap: ap.rearrange("b t v h d -> b t v (h d)")
    with nc.Block() as block:
        @block.sync
        def _(sp):
            load_slabs(sp, g, ring, [rows_of(w_in)[:, :, C_B + i * WB:C_B + (i + 1) * WB] for i in range(6)])

        @block.gpsimd
        def _(pool):
            for i in range(3):
                src, dst = heads2(layer(t[f"cache_win{i}"], l)), heads2(layer(o[f"win{i}_s"], l))
                keep = min(GROUPS[i][0], PAST + NT)
                drop = src.shape[1] + NT - keep
                pool.dma_start(dst[:, 0:keep - NT], src[:, drop:]).then_inc(s.stored2, 16)
            for n in range(TILES):
                r = ROWS[n]
                pool.wait_ge(s.act_b, 3 * TILES + n + 1)
                if n >= 2:
                    pool.wait_ge(s.dve_a, 2 * (n - 1))
                nc.gpsimd.tensor_tensor(work(n, 2), half(n, 1), trig("sin", n), ALU.mult).then_inc(s.pool_a, 1)
                nc.gpsimd.tensor_tensor(work(n, 3), half(n, 1), trig("cos", n), ALU.mult).then_inc(s.pool_a, 1)
            pool.wait_ge(s.stored2, (l + 1) * 48)
            pool.sem_inc(s.paced, 1)

        @block.tensor
        def _(pe):
            for i in range(6):
                slab_ready(pe, g, i)
                w = slab_view(ring, i, KT, WB)
                for n in range(TILES):
                    u = i * TILES + n
                    if u >= 4:
                        pe.wait_ge(s.act_b, u - 3)
                    for k in range(KT):
                        last = nc.tensor.matmul(g.ps[0:ROWS[n], u % 4, 0:WB], g.hT[:, k, cols(n)], w[:, k, :],
                                                start=k == 0, stop=k == KT - 1)
                    last.then_inc(s.pe_a, 1)
                pe.wait_ge(s.pe_a, (i + 1) * TILES)
                pe.sem_inc(s.slab_free, 1)
            for u in range(3 * TILES):
                n, j = u // 3, u % 3
                pe.wait_ge(s.dve_a, 2 * n + 2)
                if u >= 4:
                    pe.wait_ge(s.act_c, u - 3)
                for c in range(4):
                    k = 4 * j + c
                    last = nc.tensor.transpose(g.ps[:, 4 + u % 4, c * P:c * P + ROWS[n]], qk[0:ROWS[n], n, k * P:(k + 1) * P],
                                               ident(g, ROWS[n]))
                last.then_inc(s.pe_b, 1)

        @block.scalar
        def _(act):
            for i in range(6):
                for n in range(TILES):
                    u, r = i * TILES + n, ROWS[n]
                    act.wait_ge(s.pe_a, u + 1)
                    dst = qk[0:r, n, i * WB:(i + 1) * WB] if i < 4 else vals[0:r, n, (i - 4) * WB:(i - 3) * WB]
                    nc.scalar.copy(dst, g.ps[0:r, u % 4, 0:WB]).then_inc(s.act_b, 1)
            for u in range(3 * TILES):
                n, j = u // 3, u % 3
                act.wait_ge(s.pe_b, u + 1)
                nc.scalar.copy(qkT[:, 4 * j:4 * j + 4, cols(n)],
                               g.ps[:, 4 + u % 4, :].rearrange("p (k c) -> p k c", k=4)[:, :, 0:ROWS[n]]).then_inc(s.act_c, 1)
            count = 0
            for i in range(3):
                for n in range(4):
                    if i == 0 and n < 3:
                        continue
                    at = n * P if i else 0
                    for kv in range(2):
                        src = (qk[:, n, SW + i * 256:SW + (i + 1) * 256], vals[:, n, i * 256:(i + 1) * 256])[kv]
                        act.dma_start(heads2(layer(o[f"win{i}_p"], l))[0, at:at + P, kv], src).then_inc(s.stored, 16)
                        count += 16
                keep = min(GROUPS[i][0], PAST + NT)
                for kv in range(2):
                    src = (qk[0:NS, 4, SW + i * 256:SW + (i + 1) * 256], vals[0:NS, 4, i * 256:(i + 1) * 256])[kv]
                    for b in range(NB):
                        act.dma_start(heads2(layer(o[f"win{i}_s"], l))[b, keep - NT:keep, kv], src[b * NT:(b + 1) * NT]
                                      ).then_inc(s.stored, 16)
                        count += 16
            act.wait_ge(s.stored, count)

        @block.vector
        def _(dve):
            link = Link(dve, s.link_dve)
            for n in range(TILES):
                dve.wait_ge(s.act_b, 3 * TILES + n + 1)
                link(nc.vector.tensor_tensor(work(n, 0), half(n, 0), trig("cos", n), ALU.mult))
                link(nc.vector.tensor_tensor(work(n, 1), half(n, 0), trig("sin", n), ALU.mult))
                dve.wait_ge(s.pool_a, 2 * n + 2)
                nc.vector.tensor_tensor(half(n, 0), work(n, 0), work(n, 2), ALU.subtract).then_inc(s.dve_a, 1)
                nc.vector.tensor_tensor(half(n, 1), work(n, 1), work(n, 3), ALU.add).then_inc(s.dve_a, 1)


SEG = (0, 256, 768, 1280)
LEN_S = (128, 256, 256)


def window_prompt(nc, g, vals, qkT, sb):
    s = g.s
    sc, pT = sb("sc", [P, 2, 1280]), sb("pT", [P, 2, 10, P])
    stat = sb("stat", [P, 2, 4])
    units = [(n, h) for n in range(4) for h in range(SLOTS)]
    qT = lambda n, i, h: qkT[(h % 2) * SD:(h % 2 + 1) * SD, 2 * i + h // 2, cols(n)]
    kTt = lambda m0, m1, i, h: qkT[(h % 2) * SD:(h % 2 + 1) * SD, 6 + 2 * i + h // 2, m0 * P:m1 * P]

    def segments(n):
        out, at = [], 0
        for i in range(3):
            m0 = max(0, n - 1) if i == 0 else 0
            w = (n + 1 - m0) * P
            out.append((i, m0, n + 1 - m0, at, SEG[i + 1] - w))
            at += w
        return out, at

    mask = table(g, "amask")
    with nc.Block() as block:
        @block.tensor
        def _(pe):
            quad = [0]

            def scores(u):
                n, h = units[u]
                if u >= 1:
                    pe.wait_ge(s.dve_a, u)
                for i, m0, m, at, _ in segments(n)[0]:
                    last = nc.tensor.matmul(g.ps[:, i, 0:m * P], qT(n, i, h), kTt(m0, m0 + m, i, h), start=True, stop=True)
                last.then_inc(s.pe_a, 1)

            def weigh(u):
                n, h = units[u]
                tiles = [(i, m0 + j) for i, m0, m, _, _ in segments(n)[0] for j in range(m)]
                pe.wait_ge(s.dve_b, u + 1)
                for q in range(0, len(tiles), 4):
                    if quad[0] >= 2:
                        pe.wait_ge(s.act_b, quad[0] - 1)
                    for j in range(q, min(q + 4, len(tiles))):
                        last = nc.tensor.transpose(g.ps[:, 3 + quad[0] % 2, (j - q) * P:(j - q + 1) * P],
                                                   sc[:, u % 2, j * P:(j + 1) * P], ident(g))
                    last.then_inc(s.pe_b, 1)
                    quad[0] += 1
                pe.wait_ge(s.act_b, quad[0])
                if u >= 2:
                    pe.wait_ge(s.dve_c, u - 1)
                r = (h % 2) * SD
                for j, (i, m) in enumerate(tiles):
                    last = nc.tensor.matmul(g.ps[r:r + SD, 5 + u % 2, 0:P], vals[:, m, i * 256 + h * SD:i * 256 + (h + 1) * SD],
                                            pT[:, u % 2, j, :], start=j == 0, stop=j == len(tiles) - 1)
                last.then_inc(s.pe_c, 1)

            scores(0)
            for u in range(len(units)):
                if u + 1 < len(units):
                    scores(u + 1)
                weigh(u)

        @block.scalar
        def _(act):
            quad = 0

            def exps(u):
                n, h = units[u]
                w = segments(n)[1]
                act.wait_ge(s.dve_d, u + 1)
                nc.scalar.activation(sc[:, u % 2, 0:w], sc[:, u % 2, 0:w], ACT.Exp, bias=stat[:, u % 2, 1:2], scale=SD ** -0.5,
                                     accum_out=stat[:, u % 2, 2:3]).then_inc(s.act_a, 1)

            exps(0)
            for u in range(len(units)):
                n, h = units[u]
                if u + 1 < len(units):
                    exps(u + 1)
                count = segments(n)[1] // P
                if u >= 2:
                    act.wait_ge(s.pe_c, u - 1)
                for q in range(0, count, 4):
                    m = min(4, count - q)
                    act.wait_ge(s.pe_b, quad + 1)
                    nc.scalar.copy(pT[:, u % 2, q:q + m, :], g.ps[:, 3 + quad % 2, 0:m * P].rearrange("p (k c) -> p k c", k=m)
                                   ).then_inc(s.act_b, 1)
                    quad += 1

        @block.vector
        def _(dve):
            link = Link(dve, s.link_dve)

            def first(u):
                n, h = units[u]
                seg, w = segments(n)
                dve.wait_ge(s.pe_a, u + 1)
                if u >= 2:
                    dve.wait_ge(s.pe_c, u - 1)
                for i, m0, m, at, mk in seg:
                    last = nc.vector.tensor_tensor(sc[:, u % 2, at:at + m * P], g.ps[:, i, 0:m * P], mask[:, mk:mk + m * P], ALU.add)
                    if i < 2:
                        link(last)
                last.then_inc(s.dve_a, 1)
                dve.wait_ge(s.dve_a, u + 1)
                link(nc.vector.reduce_max(stat[:, u % 2, 0:1], sc[:, u % 2, 0:w], AX.X))
                nc.vector.tensor_scalar(stat[:, u % 2, 1:2], stat[:, u % 2, 0:1], -SD ** -0.5, None, ALU.mult).then_inc(s.dve_d, 1)

            first(0)
            for u in range(len(units)):
                n, h = units[u]
                w = segments(n)[1]
                if u + 1 < len(units):
                    first(u + 1)
                dve.wait_ge(s.act_a, u + 1)
                link(nc.vector.reciprocal(stat[:, u % 2, 3:4], stat[:, u % 2, 2:3]))
                nc.vector.tensor_scalar(sc[:, u % 2, 0:w], sc[:, u % 2, 0:w], stat[:, u % 2, 3:4], None, ALU.mult).then_inc(s.dve_b, 1)
                dve.wait_ge(s.pe_c, u + 1)
                r = (h % 2) * SD
                nc.vector.tensor_copy(g.ob[r:r + SD, h // 2, cols(n)], g.ps[r:r + SD, 5 + u % 2, 0:P]).then_inc(s.dve_c, 1)


def window_samples(nc, g, t, l, vals, qkT, sb):
    s = g.s
    kc, vc = sb("kc", [P, 2, 5, 256]), sb("vc", [P, NB, 5, 256])
    kTc = sb("kTc", [P, 10, P])
    sT = sb("sT", [P, 20, NS])
    sc, pT, stat = sb("sc", [NS, 2, 832]), sb("pT", [P, 2, 8, NS]), sb("stat", [NS, 2, 4])
    tiles = [(0, 0), (1, 0), (1, 1), (2, 0), (2, 1)]
    q_s = lambda i, h: qkT[(h % 2) * SD:(h % 2 + 1) * SD, 2 * i + h // 2, SEQ:TOK]
    k_s = lambda i, h: qkT[(h % 2) * SD:(h % 2 + 1) * SD, 6 + 2 * i + h // 2, SEQ:TOK]
    caches = [layer(t[f"cache_win{i}"], l).rearrange("b t v h d -> b t v (h d)") for i in range(3)]
    mask = table(g, "smask", NS)
    with nc.Block() as block:
        @block.sync
        def _(sp):
            for b in range(NB):
                if b >= 2:
                    sp.wait_ge(s.act_a, 3 * (b - 1))
                for j, (i, m) in enumerate(tiles):
                    sp.dma_start(kc[:, b % 2, j], caches[i][b, m * P:(m + 1) * P, 0]).then_inc((s.slab0, s.slab1)[b % 2], 16)

        @block.gpsimd
        def _(pool):
            for b in range(NB):
                for j, (i, m) in enumerate(tiles):
                    pool.dma_start(vc[:, b, j], caches[i][b, m * P:(m + 1) * P, 1]).then_inc(s.values, 16)

        @block.tensor
        def _(pe):
            for b in range(NB):
                pe.wait_ge((s.slab0, s.slab1)[b % 2], 80 * (b // 2 + 1))
                for q in range(3):
                    u = 3 * b + q
                    if b:
                        pe.wait_ge(s.act_a, u - 2)
                    for e in range(4 * q, min(4 * q + 4, 10)):
                        j, pair = e // 2, e % 2
                        last = nc.tensor.transpose(g.ps[:, q, (e % 4) * P:(e % 4 + 1) * P], kc[:, b % 2, j, pair * P:(pair + 1) * P], ident(g))
                    last.then_inc(s.pe_a, 1)
                pe.wait_ge(s.act_a, 3 * b + 3)
                if b >= 2:
                    pe.wait_ge(s.dve_a, 2 * (b - 1))
                for j, (i, m) in enumerate(tiles):
                    for h in range(SLOTS):
                        r = (h % 2) * SD
                        c = (2 * j + h // 2) * NT
                        last = nc.tensor.matmul(g.ps[:, 3 + 2 * (b % 2) + h % 2, c:c + NT], kTc[r:r + SD, 2 * j + h // 2, :],
                                                q_s(i, h)[:, b * NT:(b + 1) * NT], start=True, stop=True)
                last.then_inc(s.pe_b, 1)
            pe.wait_ge(s.dve_a, 2 * NB)
            pe.wait_ge(s.act_a, 3 * NB)
            for h in range(SLOTS):
                if h:
                    pe.wait_ge(s.dve_b, h)
                for j in range(5):
                    bank, c = (5, j * P) if j < 4 else (6, 0)
                    nc.tensor.transpose(g.ps[0:NS, bank, c:c + P], sT[:, 4 * j + h, :], ident(g))
                for i in range(3):
                    last = nc.tensor.matmul(g.ps[0:NS, 6, P + i * NS:P + (i + 1) * NS], q_s(i, h), k_s(i, h), start=True, stop=True)
                last.then_inc(s.pe_c, 1)
                pe.wait_ge(s.dve_d, h + 1)
                if h:
                    pe.wait_ge(s.act_c, h)
                for j in range(5):
                    nc.tensor.transpose(g.ps[:, 0, j * NS:(j + 1) * NS], sc[:, h % 2, j * P:(j + 1) * P], ident(g, NS))
                for i in range(3):
                    last = nc.tensor.transpose(g.ps[0:NS, 0, (5 + i) * NS:(6 + i) * NS], sc[:, h % 2, 640 + i * NS:640 + (i + 1) * NS],
                                               ident(g, NS))
                last.then_inc(s.pe_d, 1)
                pe.wait_ge(s.act_c, h + 1)
                if h == 0:
                    pe.wait_ge(s.values, (l + 1) * (16 * 5 * NB))
                    pe.sem_inc(s.paced, 1)
                r = (h % 2) * SD
                if h >= 2:
                    pe.wait_ge(s.dve_c, h - 1)
                for i in range(3):
                    nc.tensor.matmul(g.ps[r:r + SD, 1 + h % 2, 0:NS], vals[0:NS, 4, i * 256 + h * SD:i * 256 + (h + 1) * SD],
                                     pT[0:NS, h % 2, 5 + i, :], start=i == 0, stop=False)
                for b in range(NB):
                    for j in range(5):
                        last = nc.tensor.matmul(g.ps[r:r + SD, 1 + h % 2, b * NT:(b + 1) * NT], vc[:, b, j, h * SD:(h + 1) * SD],
                                                pT[:, h % 2, j, b * NT:(b + 1) * NT], start=False, stop=j == 4 and b == NB - 1)
                last.then_inc(s.pe_e, 1)

        @block.scalar
        def _(act):
            for b in range(NB):
                for q in range(3):
                    act.wait_ge(s.pe_a, 3 * b + q + 1)
                    if b:
                        act.wait_ge(s.pe_b, b)
                    m = min(4, 10 - 4 * q)
                    nc.scalar.copy(kTc[:, 4 * q:4 * q + m, :], g.ps[:, q, 0:m * P].rearrange("p (k c) -> p k c", k=m)
                                   ).then_inc(s.act_a, 1)
            for h in range(SLOTS):
                act.wait_ge(s.dve_e, h + 1)
                nc.scalar.activation(sc[:, h % 2], sc[:, h % 2], ACT.Exp, bias=stat[:, h % 2, 1:2], scale=SD ** -0.5,
                                     accum_out=stat[:, h % 2, 2:3]).then_inc(s.act_b, 1)
                act.wait_ge(s.pe_d, h + 1)
                if h >= 2:
                    act.wait_ge(s.pe_e, h - 1)
                nc.scalar.copy(pT[:, h % 2, 0:5], g.ps[:, 0, 0:5 * NS].rearrange("p (k c) -> p k c", k=5)).then_inc(s.link_act, 1)
                nc.scalar.copy(pT[0:NS, h % 2, 5:8], g.ps[0:NS, 0, 5 * NS:8 * NS].rearrange("p (k c) -> p k c", k=3)
                               ).then_inc(s.act_c, 1)

        @block.vector
        def _(dve):
            link = Link(dve, s.link_dve)
            for b in range(NB):
                dve.wait_ge(s.pe_b, b + 1)
                for a in range(2):
                    nc.vector.tensor_copy(sT[:].rearrange("p (e a) c -> p e a c", a=2)[:, :, a, b * NT:(b + 1) * NT],
                                          g.ps[:, 3 + 2 * (b % 2) + a, 0:10 * NT].rearrange("p (e c) -> p e c", e=10)).then_inc(s.dve_a, 1)
            for h in range(SLOTS):
                dve.wait_ge(s.pe_c, h + 1)
                if h >= 2:
                    dve.wait_ge(s.pe_d, h - 1)
                link(nc.vector.tensor_tensor(sc[:, h % 2, 0:512], g.ps[0:NS, 5, :], mask[:, 0:512], ALU.add))
                nc.vector.tensor_tensor(sc[:, h % 2, 512:832], g.ps[0:NS, 6, 0:320], mask[:, 512:832], ALU.add).then_inc(s.dve_b, 1)
                dve.wait_ge(s.dve_b, h + 1)
                link(nc.vector.reduce_max(stat[:, h % 2, 0:1], sc[:, h % 2], AX.X))
                nc.vector.tensor_scalar(stat[:, h % 2, 1:2], stat[:, h % 2, 0:1], -SD ** -0.5, None, ALU.mult).then_inc(s.dve_e, 1)
                dve.wait_ge(s.act_b, h + 1)
                link(nc.vector.reciprocal(stat[:, h % 2, 3:4], stat[:, h % 2, 2:3]))
                nc.vector.tensor_scalar(sc[:, h % 2], sc[:, h % 2], stat[:, h % 2, 3:4], None, ALU.mult).then_inc(s.dve_d, 1)
                dve.wait_ge(s.pe_e, h + 1)
                r = (h % 2) * SD
                nc.vector.tensor_copy(g.ob[r:r + SD, h // 2, SEQ:TOK], g.ps[r:r + SD, 1 + h % 2, 0:NS]).then_inc(s.dve_c, 1)


UP = PBUF + SEQ
US = PBUF + NT
UW = UP + NB * US


def pool_stage(nc, g, t, o, l, oc):
    s = g.s
    w_in = layer(t["w_in"], l)
    with ExitStack() as ctx:
        sb = lambda name, shape: ctx.enter_context(nc.sbuf_tensor(fresh(name), shape, F32))
        ring, wp = sb("ring", [P, 2, 4096]), sb("wp", [P, 2, 3, PG])
        ext, sums, spare = sb("ext", [P, 2, 3, UW]), sb("sums", [P, 3, UW]), sb("spare", [P, 3, UW])
        diff = sb("diff", [P, 2, 3, TOK])
        old, tail = sb("old", [NB * PBUF, PW]), sb("tail", [P, 3, PBUF + NS])
        new = sb("new", [PBUF + NS, PW])
        smp = lambda i, c: ext[:, i, c, UP:UW].rearrange("p (b j) -> p b j", b=NB)
        pool_p, pool_s = layer(o["pool_p"], l), layer(o["pool_s"], l)
        G = len(POOLS)
        with nc.Block() as block:
            @block.sync
            def _(sp):
                sp.dma_start(old[:], layer(t["state_pool"], l).rearrange("b j c -> (b j) c")).then_inc(s.loaded, 16)
                sp.dma_start(pool_s[:, 0:PBUF - NT], layer(t["state_pool"], l)[:, NT:PBUF]).then_inc(s.stored, 16)
                load_slabs(sp, g, ring, [rows_of(w_in)[:, :, C_U + i * 512:C_U + (i + 1) * 512] for i in range(3)])
                for gi in range(G):
                    if gi >= 2:
                        sp.wait_ge(s.pe_d, 3 * (gi - 1))
                    sp.dma_start(wp[:, gi % 2], rows_of(layer(t["w_pool"], l)[gi])).then_inc((s.map0, s.map1)[gi % 2], 16)
                sp.wait_ge(s.act_c, G)
                sp.dma_start(pool_p[0], new[0:PBUF]).then_inc(s.stored, 16)
                for b in range(NB):
                    sp.dma_start(pool_s[b, PBUF - NT:], new[PBUF + b * NT:PBUF + (b + 1) * NT]).then_inc(s.stored, 16)
                sp.wait_ge(s.stored, 16 * (2 + NB))

            @block.gpsimd
            def _(pool):
                for i in range(2):
                    nc.gpsimd.memset(ext[:, i, :, 0:PBUF], 0.0).then_inc(s.filled, 1)

            @block.tensor
            def _(pe):
                def maps(gi):
                    pe.wait_ge((s.map0, s.map1)[gi % 2], 16 * (gi // 2 + 1))
                    pe.wait_ge(s.dve_c, gi + 1)
                    for c in range(3):
                        u = 3 * gi + c
                        if u:
                            pe.wait_ge(s.act_d, 2 * u)
                        for k in range(3):
                            nc.tensor.matmul(g.ps[:, 6, :], wp[:, gi % 2, k, c * P:(c + 1) * P], diff[:, gi % 2, k, 0:SEQ],
                                             start=k == 0, stop=k == 2)
                            last = nc.tensor.matmul(g.ps[:, 7, 0:NS], wp[:, gi % 2, k, c * P:(c + 1) * P], diff[:, gi % 2, k, SEQ:TOK],
                                                    start=k == 0, stop=k == 2)
                        last.then_inc(s.pe_d, 1)

                pe.wait_ge(s.loaded, 16)
                for gi in range(G):
                    if gi:
                        pe.wait_ge(s.dve_b, gi)
                    for c in range(3):
                        last = nc.tensor.transpose(g.ps[:, 5, c * 120:(c + 1) * 120], old[:, (3 * gi + c) * P:(3 * gi + c + 1) * P],
                                                   ident(g, 120))
                    last.then_inc(s.pe_b, 1)
                    for u in range(3 * gi, 3 * gi + 3):
                        if u % 4 == 0:
                            slab_ready(pe, g, u // 4)
                        w = slab_view(ring, u // 4, KT, 512)
                        project(nc, g, pe, u, lambda k: w[:, k, (u % 4) * P:(u % 4 + 1) * P], lambda k: g.hT[:, k, :], KT,
                                s.pe_a, s.act_a, s.dve_a)
                        if u % 4 == 3:
                            pe.wait_ge(s.pe_a, u + 1)
                            pe.sem_inc(s.slab_free, 1)
                    pe.wait_ge(s.dve_b, gi + 1)
                    for c in range(3):
                        last = nc.tensor.transpose(g.ps[0:PBUF + NS, 5, c * P:(c + 1) * P], tail[:, c, :], ident(g))
                    last.then_inc(s.pe_c, 1)
                    pe.wait_ge(s.act_c, gi + 1)
                    if gi:
                        maps(gi - 1)
                maps(G - 1)

            @block.scalar
            def _(act):
                def scale(gi):
                    for c in range(3):
                        u = 3 * gi + c
                        act.wait_ge(s.pe_d, u + 1)
                        nc.scalar.mul(oc[:, u, 0:SEQ], g.ps[:, 6, :], g.pscale[:, u:u + 1]).then_inc(s.act_d, 1)
                        nc.scalar.mul(oc[:, u, SEQ:TOK], g.ps[:, 7, 0:NS], g.pscale[:, u:u + 1]).then_inc(s.act_d, 1)

                for gi in range(G):
                    if gi >= 2:
                        act.wait_ge(s.dve_c, gi - 1)
                    for u in range(3 * gi, 3 * gi + 3):
                        act.wait_ge(s.pe_a, u + 1)
                        nc.scalar.copy(ext[:, gi % 2, u % 3, PBUF:UP], part_a(g, u)).then_inc(s.act_a, 1)
                    act.wait_ge(s.pe_c, gi + 1)
                    nc.scalar.copy(new[:, gi * PG:(gi + 1) * PG], g.ps[0:PBUF + NS, 5, 0:PG]).then_inc(s.act_c, 1)
                    if gi:
                        scale(gi - 1)
                scale(G - 1)

            @block.vector
            def _(dve):
                link = Link(dve, s.link_dve)
                for gi, w in enumerate(POOLS):
                    i = gi % 2
                    e = ext[:, i]
                    dve.wait_ge(s.pe_b, gi + 1)
                    for c in range(3):
                        link(nc.vector.tensor_copy(smp(i, c)[:, :, 0:PBUF],
                                                   g.ps[:, 5, c * 120:(c + 1) * 120].rearrange("p (b j) -> p b j", b=NB)))
                    for u in range(3 * gi, 3 * gi + 3):
                        dve.wait_ge(s.pe_a, u + 1)
                        nc.vector.tensor_copy(smp(i, u % 3)[:, :, PBUF:], part_b(g, u).rearrange("p (b j) -> p b j", b=NB)
                                              ).then_inc(s.dve_a, 1)
                    dve.wait_ge(s.act_a, 3 * gi + 3)
                    dve.wait_ge(s.dve_a, 3 * gi + 3)
                    dve.wait_ge(s.filled, 2)
                    for c in range(3):
                        link(nc.vector.tensor_copy(tail[:, c, PBUF:].rearrange("p (b j) -> p b j", b=NB), smp(i, c)[:, :, PBUF:]))
                    nc.vector.tensor_copy(tail[:, :, 0:PBUF], e[:, :, UP - PBUF:UP]).then_inc(s.dve_b, 1)
                    link(nc.vector.tensor_tensor(sums[:, :, 1:UW], e[:, :, 1:UW], e[:, :, 0:UW - 1], ALU.add))
                    src, span = sums, 2
                    while span < w:
                        dst = spare if src is sums else sums
                        link(nc.vector.tensor_tensor(dst[:, :, 2 * span - 1:UW], src[:, :, 2 * span - 1:UW],
                                                     src[:, :, span - 1:UW - span], ALU.add))
                        src, span = dst, 2 * span
                    if gi >= 2:
                        dve.wait_ge(s.pe_d, 3 * (gi - 1))
                    d = diff[:, i]
                    link(nc.vector.scalar_tensor_tensor(out=d[:, :, 0:SEQ], in0=src[:, :, PBUF:UP], scalar=1.0 / w,
                                                        in1=e[:, :, PBUF:UP], op0=ALU.mult, op1=ALU.subtract))
                    o_c, _ = CONST["count"]
                    cnt = g.consts[:, o_c + gi * 16:o_c + (gi + 1) * 16]
                    link(nc.vector.tensor_tensor(d[:, :, 0:16], src[:, :, PBUF:PBUF + 16], bc(cnt, 1, 3), ALU.mult))
                    link(nc.vector.tensor_tensor(d[:, :, 0:16], d[:, :, 0:16], e[:, :, PBUF:PBUF + 16], ALU.subtract))
                    for c in range(3):
                        last = nc.vector.scalar_tensor_tensor(
                            out=d[:, c, SEQ:TOK].rearrange("p (b j) -> p b j", b=NB),
                            in0=src[:, c, UP:UW].rearrange("p (b j) -> p b j", b=NB)[:, :, PBUF:], scalar=1.0 / w,
                            in1=smp(i, c)[:, :, PBUF:], op0=ALU.mult, op1=ALU.subtract)
                        if c < 2:
                            link(last)
                    last.then_inc(s.dve_c, 1)
    clear_semaphores(nc, g)


def merge_stage(nc, g, t, l, oc):
    s = g.s
    w_in, w_b, w_o = rows_of(layer(t["w_in"], l)), rows_of(layer(t["w_branch"], l)), rows_of(layer(t["w_out"], l))
    NW = 3 * KT + 18
    src = [(g.oa, 4, 0), (g.ob, 2, 4), (oc, 12, 6)]
    with ExitStack() as ctx:
        sb = lambda name, shape: ctx.enter_context(nc.sbuf_tensor(fresh(name), shape, F32))
        merged = sb("merged", [P, KT, TOK])
        with ExitStack() as inner:
            sbi = lambda name, shape: inner.enter_context(nc.sbuf_tensor(fresh(name), shape, F32))
            ring = sbi("ring", [P, 2, NW * P])
            gate, term = sbi("gate", [P, 2, TOK]), sbi("term", [P, TOK])
            view = lambda j: ring[:, j % 2].rearrange("p (k c) -> p k c", k=NW)
            slab = (s.slab0, s.slab1)
            units = [(j, b) for j in range(KT) for b in range(3)]
            with nc.Block() as block:
                @block.sync
                def _(sp):
                    for j in range(KT):
                        if j >= 2:
                            sp.wait_ge(s.pe_b, 3 * (j - 1))
                        for b in range(3):
                            c = C_G + b * D + j * P
                            sp.dma_start(view(j)[:, b * KT:(b + 1) * KT], w_in[:, :, c:c + P]).then_inc(slab[j % 2], 16)
                        sp.dma_start(view(j)[:, 3 * KT:], w_b[:, :, j * P:(j + 1) * P]).then_inc(slab[j % 2], 16)

                @block.tensor
                def _(pe):
                    for u, (j, b) in enumerate(units):
                        if b == 0:
                            pe.wait_ge(slab[j % 2], 64 * (j // 2 + 1))
                        w = view(j)
                        if u >= 2:
                            pe.wait_ge(s.act_a, 2 * (u - 1))
                        for k in range(KT):
                            nc.tensor.matmul(g.ps[:, u % 2, :], w[:, b * KT + k, :], g.hT[:, k, 0:SEQ], start=k == 0, stop=k == KT - 1)
                            last = nc.tensor.matmul(g.ps[:, 4 + u % 2, 0:NS], w[:, b * KT + k, :], g.hT[:, k, SEQ:TOK],
                                                    start=k == 0, stop=k == KT - 1)
                        last.then_inc(s.pe_a, 1)
                        if u >= 2:
                            pe.wait_ge(s.dve_a, u - 1)
                        out, nk, k0 = src[b]
                        for k in range(nk):
                            nc.tensor.matmul(g.ps[:, 2 + u % 2, :], w[:, 3 * KT + k0 + k, :], out[:, k, 0:SEQ], start=k == 0, stop=k == nk - 1)
                            last = nc.tensor.matmul(g.ps[:, 6 + u % 2, 0:NS], w[:, 3 * KT + k0 + k, :], out[:, k, SEQ:TOK],
                                                    start=k == 0, stop=k == nk - 1)
                        last.then_inc(s.pe_b, 1)

                @block.scalar
                def _(act):
                    for u, (j, b) in enumerate(units):
                        act.wait_ge(s.pe_a, u + 1)
                        if u >= 2:
                            act.wait_ge(s.dve_a, u - 1)
                        nc.scalar.activation(gate[:, u % 2, 0:SEQ], g.ps[:, u % 2, :], ACT.Sigmoid).then_inc(s.act_a, 1)
                        nc.scalar.activation(gate[:, u % 2, SEQ:TOK], g.ps[:, 4 + u % 2, 0:NS], ACT.Sigmoid).then_inc(s.act_a, 1)

                @block.vector
                def _(dve):
                    link = Link(dve, s.link_dve)
                    for u, (j, b) in enumerate(units):
                        dve.wait_ge(s.act_a, 2 * u + 2)
                        dve.wait_ge(s.pe_b, u + 1)
                        to = merged[:, j, :] if b == 0 else term[:]
                        nc.vector.tensor_tensor(to[:, 0:SEQ], gate[:, u % 2, 0:SEQ], g.ps[:, 2 + u % 2, :], ALU.mult).then_inc(s.link_dve, 1)
                        link.n += 1
                        nc.vector.tensor_tensor(to[:, SEQ:TOK], gate[:, u % 2, SEQ:TOK], g.ps[:, 6 + u % 2, 0:NS], ALU.mult).then_inc(s.dve_a, 1)
                        dve.wait_ge(s.dve_a, u + 1)
                        if b:
                            link(nc.vector.tensor_tensor(merged[:, j, :], merged[:, j, :], term[:], ALU.add))
            clear_semaphores(nc, g)
        with ExitStack() as inner:
            ring = inner.enter_context(nc.sbuf_tensor(fresh("ring"), [P, 2, 4096], F32))
            with nc.Block() as block:
                @block.sync
                def _(sp):
                    load_slabs(sp, g, ring, [w_o[:, :, i * 512:(i + 1) * 512] for i in range(2)])

                @block.tensor
                def _(pe):
                    for i in range(2):
                        slab_ready(pe, g, i)
                        w = slab_view(ring, i, KT, 512)
                        for n in range(TILES):
                            u = i * TILES + n
                            if u >= 4:
                                pe.wait_ge(s.dve_a, u - 3)
                            for k in range(KT):
                                last = nc.tensor.matmul(g.ps[0:ROWS[n], u % 4, :], merged[:, k, cols(n)], w[:, k, :], start=k == 0, stop=k == KT - 1)
                            last.then_inc(s.pe_a, 1)

                @block.vector
                def _(dve):
                    for u in range(2 * TILES):
                        i, n = u // TILES, u % TILES
                        part = g.x[0:ROWS[n], n, i * 512:(i + 1) * 512]
                        dve.wait_ge(s.pe_a, u + 1)
                        nc.vector.tensor_tensor(part, part, g.ps[0:ROWS[n], u % 4, :], ALU.add).then_inc(s.dve_a, 1)
            clear_semaphores(nc, g)


def score_stage(nc, g, t, l, sc, router):
    s = g.s
    w_q = rows_of(layer(t["peer_query"], l))
    with ExitStack() as ctx:
        with ExitStack() as inner:
            sbi = lambda name, shape: inner.enter_context(nc.sbuf_tensor(fresh(name), shape, F32))
            ring, keys, keysT, qT = sbi("ring", [P, 2, 4096]), sbi("keys", [P, 2, P]), sbi("keysT", [P, 2, P]), sbi("qT", [P, 2, TOK])
            with nc.Block() as block:
                @block.sync
                def _(sp):
                    sp.dma_start(keys[:], layer(t["peer_subkeys"], l).rearrange("s k d -> k s d")).then_inc(s.loaded, 16)
                    load_slabs(sp, g, ring, [w_q[:, :, i * 512:(i + 1) * 512] for i in range(4)])

                @block.tensor
                def _(pe):
                    def scores(u):
                        pe.wait_ge(s.act_a, 2 * u + 2)
                        if u:
                            pe.wait_ge(s.scored, 2 * u)
                        for n in range(TILES):
                            last = nc.tensor.matmul(g.ps[0:ROWS[n], 5 + n // 4, (n % 4) * P:(n % 4 + 1) * P], qT[:, u % 2, cols(n)],
                                                    keysT[:, u % 2, :], start=True, stop=True)
                        last.then_inc(s.pe_b, 1)

                    pe.wait_ge(s.loaded, 16)
                    for i in range(2):
                        last = nc.tensor.transpose(g.ps[:, 7, i * P:(i + 1) * P], keys[:, i, :], ident(g))
                    last.then_inc(s.pe_c, 1)
                    pe.wait_ge(s.act_c, 1)
                    for u in range(NQ):
                        if u % 4 == 0:
                            slab_ready(pe, g, u // 4)
                        w = slab_view(ring, u // 4, KT, 512)
                        if u >= BANKS_B:
                            pe.wait_ge(s.act_a, 2 * (u - BANKS_B + 1))
                        for k in range(KT):
                            nc.tensor.matmul(part_a(g, u), w[:, k, (u % 4) * P:(u % 4 + 1) * P], g.hT[:, k, 0:SEQ], start=k == 0, stop=k == KT - 1)
                            last = nc.tensor.matmul(part_b(g, u), w[:, k, (u % 4) * P:(u % 4 + 1) * P], g.hT[:, k, SEQ:TOK],
                                                    start=k == 0, stop=k == KT - 1)
                        last.then_inc(s.pe_a, 1)
                        if u % 4 == 3:
                            pe.wait_ge(s.pe_a, u + 1)
                            pe.sem_inc(s.slab_free, 1)
                        if u:
                            scores(u - 1)
                    scores(NQ - 1)

                @block.scalar
                def _(act):
                    def scores(u):
                        act.wait_ge(s.pe_b, u + 1)
                        nc.scalar.copy(sc[:, 0:4, u, :], g.ps[:, 5, :].rearrange("p (n k) -> p n k", n=4)).then_inc(s.scored, 1)
                        nc.scalar.copy(sc[0:NS, 4, u, :], g.ps[0:NS, 6, 0:P]).then_inc(s.scored, 1)

                    act.wait_ge(s.pe_c, 1)
                    nc.scalar.copy(keysT[:], g.ps[:, 7, 0:2 * P].rearrange("p (i k) -> p i k", i=2)).then_inc(s.act_c, 1)
                    for u in range(NQ):
                        act.wait_ge(s.pe_a, u + 1)
                        if u >= 2:
                            act.wait_ge(s.pe_b, u - 1)
                        nc.scalar.copy(qT[:, u % 2, 0:SEQ], part_a(g, u)).then_inc(s.act_a, 1)
                        nc.scalar.copy(qT[:, u % 2, SEQ:TOK], part_b(g, u)).then_inc(s.act_a, 1)
                        if u:
                            scores(u - 1)
                    scores(NQ - 1)
                    router.gate_exp(act, 0, 1)

                @block.vector
                def _(dve):
                    link = Link(dve, s.link_dve)
                    for h in range(PH):
                        dve.wait_ge(s.scored, 4 * h + 4)
                        router.head(link, 0, h)
                    router.finish(dve, link, 0, 1)
            clear_semaphores(nc, g)


class Router:

    def __init__(self, nc, g, sb, sc, ids, gates):
        self.nc, self.g, self.sc, self.ids, self.gates = nc, g, sc, ids, gates
        self.top, self.at = sb("top", [P, 2, TOPK]), sb("at", [P, 2, TOPK], U32)
        self.atf, self.best = sb("atf", [P, 2, TOPK]), sb("best", [P, PH, TOPK])
        self.pos, self.two = sb("pos", [P, TOPK], U32), sb("two", [P, 2, TOPK], U32)
        self.twof, self.num, self.den = sb("twof", [P, 2, TOPK]), sb("num", [P, PH, 2, TOPK]), sb("den", [P, 2, PH])
        self.cand, self.pick = sb("cand", [P, TOPK * TOPK]), sb("pick", [P, 2, TOPK, TOPK])

    def top16(self, link, values, index, data):
        v = self.nc.vector
        link(v.max(values[:, 0:8], data))
        link(v.max_index(index[:, 0:8], values[:, 0:8], data))
        link(v.match_replace(data, values[:, 0:8], data, -3.0e38))
        link(v.max(values[:, 8:16], data))
        link(v.max_index(index[:, 8:16], values[:, 8:16], data))

    def head(self, link, n, h):
        r, v, g = ROWS[n], self.nc.vector, self.g
        for a in range(2):
            self.top16(link, self.top[0:r, a], self.at[0:r, a], self.sc[0:r, n, 2 * h + a, :])
        link(v.tensor_tensor(self.cand[0:r].rearrange("p (a b) -> p a b", a=TOPK), bc(self.top[0:r, 0], 2, TOPK),
                             bc(self.top[0:r, 1], 1, TOPK), ALU.add))
        self.top16(link, self.best[0:r, h], self.pos[0:r], self.cand[0:r])
        link(v.tensor_single_scalar(self.two[0:r, 0], self.pos[0:r], 4, op=ALU.logical_shift_right))
        link(v.tensor_single_scalar(self.two[0:r, 1], self.pos[0:r], 15, op=ALU.bitwise_and))
        link(v.tensor_copy(self.twof[0:r], self.two[0:r]))
        link(v.tensor_copy(self.atf[0:r], self.at[0:r]))
        iota = table(g, "iota", r).unsqueeze(1).unsqueeze(1).broadcast_to([r, 2, TOPK, TOPK])
        link(v.tensor_tensor(self.pick[0:r], iota, bc(self.twof[0:r], 3, TOPK), ALU.is_equal))
        link(v.tensor_tensor(self.pick[0:r], self.pick[0:r], bc(self.atf[0:r], 2, TOPK), ALU.mult))
        link(v.reduce_sum(self.num[0:r, h], self.pick[0:r], AX.X))

    def finish(self, dve, link, n, count):
        v, g, s, r = self.nc.vector, self.g, self.g.s, ROWS[n]
        gt = self.gates[0:r, n, :].rearrange("p (h k) -> p h k", h=PH)
        v.tensor_tensor(gt, self.best[0:r], self.best[0:r, :, 0:1].broadcast_to([r, PH, TOPK]), ALU.subtract).then_inc(s.gate_in, 1)
        link(v.scalar_tensor_tensor(out=self.num[0:r, :, 0], in0=self.num[0:r, :, 0], scalar=float(KEYS), in1=self.num[0:r, :, 1],
                                    op0=ALU.mult, op1=ALU.add))
        link(v.tensor_scalar(self.ids[0:r, n, :].rearrange("p (h k) -> p h k", h=PH), self.num[0:r, :, 0], g.before[0:r], None, ALU.add))
        dve.wait_ge(s.gate_exp, count)
        link(v.reduce_sum(self.den[0:r, 0], gt, AX.X))
        link(v.reciprocal(self.den[0:r, 1], self.den[0:r, 0]))
        v.tensor_tensor(gt, gt, bc(self.den[0:r, 1], 2, TOPK), ALU.mult).then_inc(s.routed, 1)

    def gate_exp(self, act, n, count):
        act.wait_ge(self.g.s.gate_in, count)
        self.nc.scalar.activation(self.gates[0:ROWS[n], n, :], self.gates[0:ROWS[n], n, :], ACT.Exp).then_inc(self.g.s.gate_exp, 1)


GROUP = 4
PLACES = 2 * GROUP
LISTS = 4
LEAD = LISTS * GROUP
CHOICES = PH * TOPK
FULL = CHOICES // GROUP
TURNS = [FULL * ROWS[n] // P for n in range(TILES)]


def expert_stage(nc, g, t, l, rows, sc, ids, gates, router):
    s = g.s
    ups, downs = (s.up0, s.up1, s.up2, s.up3, s.up4, s.up5, s.up6, s.up7), (s.down0, s.down1, s.down2, s.down3, s.down4, s.down5, s.down6, s.down7)
    PER_LAYER = sum(TURNS) // 2
    w_up, w_down = t["peer_up"].rearrange("l e d -> (l e) d"), t["peer_down"].rearrange("l e d -> (l e) d")
    with ExitStack() as ctx:
        sb = lambda name, shape, dt=F32: ctx.enter_context(nc.sbuf_tensor(fresh(name), shape, dt))
        up, down = sb("up", [P, PLACES, D]), sb("down", [P, PLACES, D])
        idx = sb("idx", [P, LISTS, GROUP], U32)
        dot, gel, weight = (sb(name, [P, 2, GROUP]) for name in ("dot", "gel", "weight"))
        diag = sb("diag", [P, 2, GROUP, P])
        with nc.Block() as block:
            @block.sync
            def _(sp):
                sp.dma_start(rows[NS:P, 4, :], rows[0:NS, 4, :]).then_inc(s.doubled, 16)
                sp.wait_ge(s.routed, TILES - 1)
                sp.dma_start(ids[NS:P, 4, 0:CHOICES // 2], ids[0:NS, 4, CHOICES // 2:]).then_inc(s.doubled, 16)
                sp.dma_start(gates[NS:P, 4, 0:CHOICES // 2], gates[0:NS, 4, CHOICES // 2:]).then_inc(s.doubled, 16)

            @block.gpsimd
            def _(pool):
                def numbers(n, turn, part):
                    pool.wait_ge(s.downs_done, (n * FULL + turn) * GROUP + GROUP)
                    pool.sem_inc(s.paced, 1)
                    nc.gpsimd.tensor_copy(idx[:, part], ids[:, n, bass.ds(turn * GROUP, GROUP)]).then_inc(s.numbers, 1)
                    pool.wait_ge(s.numbers, 1)
                    pool.sem_clear(s.numbers)

                def gather(n, turn, part, table, places, done, used):
                    for k in range(GROUP):
                        c = part % 2 * GROUP + k
                        pool.wait_ge(used, (n * FULL + turn) * GROUP + LEAD - PLACES + k + 1)
                        pool.sem_inc(s.paced, 1)
                        pool.indirect_dma_start(places[:, c, :], None, table,
                                                bass.IndirectOffsetOnAxis(ap=idx[:, part, k:k + 1], axis=0)).then_inc(done[c], 16)

                def gather_up(n, turn, part):
                    numbers(n, turn, part)
                    gather(n, turn, part, w_up, up, ups, s.dots_done)

                def gather_down(n, turn, part):
                    gather(n, turn, part, w_down, down, downs, s.downs_done)

                gather_up(0, 0, 0)
                for n in range(TILES):
                    with pool.Fori(0, TURNS[n] // LISTS - 1) as i:
                        for part in range(LISTS):
                            gather_up(n, LISTS * i + part + 1, (part + 1) % LISTS)
                            gather_down(n, LISTS * i + part, part)
                    for part in range(LISTS):
                        turn = TURNS[n] - LISTS + part
                        if part < LISTS - 1:
                            gather_up(n, turn + 1, part + 1)
                        elif n + 1 < TILES:
                            pool.wait_ge(s.routed, n + 1)
                            if n + 1 == TILES - 1:
                                pool.wait_ge(s.doubled, 48)
                            gather_up(n + 1, 0, 0)
                        gather_down(n, turn, part)

            @block.vector
            def _(dve):
                def weights(n, turn, half):
                    dve.wait_ge(s.gelus, n * FULL + turn + 1)
                    nc.vector.tensor_tensor(weight[:, half], gel[:, half], gates[:, n, bass.ds(turn * GROUP, GROUP)],
                                            ALU.mult).then_inc(s.weighted, 1)

                def up_rows(n, half, pair):
                    for k in range(GROUP):
                        c = half * GROUP + k
                        dve.wait_ge(ups[c], (l * PER_LAYER + n * FULL // 2 + pair + 1) * 16)
                        nc.vector.scalar_tensor_tensor(out=up[:, c], in0=up[:, c], scalar=1.0, in1=rows[:, n, :], op0=ALU.mult,
                                                       op1=ALU.mult, accum_out=dot[:, half, k:k + 1]).then_inc(s.dots_done, 1)

                def pair(n, i):
                    up_rows(n, 1, i)
                    weights(n, 2 * i, 0)
                    up_rows(n, 0, i + 1)
                    weights(n, 2 * i + 1, 1)

                dve.sem_inc(s.dots_done, LEAD)
                link = Link(dve, s.link_dve)
                for n in range(TILES):
                    if n:
                        dve.wait_ge(s.routed, n)
                    if n == TILES - 1:
                        dve.wait_ge(s.doubled, 48)
                    up_rows(n, 0, 0)
                    routing = PH + 1 if n + 1 < TILES else 0
                    for i in range(routing):
                        pair(n, i)
                        if i < PH:
                            router.head(link, n + 1, i)
                        else:
                            router.finish(dve, link, n + 1, n + 1)
                    with dve.Fori(routing, TURNS[n] // 2 - 1) as i:
                        pair(n, i)
                    up_rows(n, 1, TURNS[n] // 2 - 1)
                    weights(n, TURNS[n] - 2, 0)
                    weights(n, TURNS[n] - 1, 1)
                link(nc.vector.tensor_scalar(g.before[:], g.before[:], float(EXPERTS), None, ALU.add))

            @block.scalar
            def _(act):
                def gelu(n, turn, half):
                    act.wait_ge(s.dots_done, (n * FULL + turn + 1) * GROUP + LEAD)
                    nc.scalar.activation(gel[:, half], dot[:, half], ACT.Gelu).then_inc(s.gelus, 1)

                def diagonals(n, turn, half):
                    act.wait_ge(s.weighted, n * FULL + turn + 1)
                    for k in range(GROUP):
                        act.wait_ge(s.downs_done, (n * FULL + turn) * GROUP + LEAD - PLACES + k + 1)
                        nc.scalar.activation(diag[:, half, k, 0:ROWS[n]], table(g, "ident" if ROWS[n] == P else "ident2"), ACT.Copy,
                                             scale=weight[:, half, k:k + 1]).then_inc(s.diagonal, 1)

                def copy_x(n):
                    act.wait_ge(s.summed, n + 1)
                    r = ROWS[n]
                    nc.scalar.copy(g.x[0:r, n, :].rearrange("p (a c) -> p a c", a=2), g.ps[0:r, 2 * (n % 2):2 * (n % 2) + 2, :]).then_inc(s.x_copied, 1)

                for n in range(TILES):
                    gelu(n, 0, 0)
                    middle = (PH + 1 if n + 1 < TILES else 2)
                    for first, last in ((0, middle), (middle, TURNS[n] // 2 - 1)):
                        with act.Fori(first, last) as i:
                            gelu(n, 2 * i + 1, 1)
                            diagonals(n, 2 * i, 0)
                            gelu(n, 2 * i + 2, 0)
                            diagonals(n, 2 * i + 1, 1)
                        if first == 0:
                            if n + 1 < TILES:
                                router.gate_exp(act, n + 1, n + 1)
                            if n:
                                copy_x(n - 1)
                    gelu(n, TURNS[n] - 1, 1)
                    diagonals(n, TURNS[n] - 2, 0)
                    diagonals(n, TURNS[n] - 1, 1)
                copy_x(TILES - 1)

            @block.tensor
            def _(pe):
                def add(n, turn, half, pair, last=False):
                    for k in range(GROUP):
                        c = half * GROUP + k
                        pe.wait_ge(s.diagonal, (n * FULL + turn) * GROUP + k + 1)
                        pe.wait_ge(downs[c], (l * PER_LAYER + n * FULL // 2 + pair + 1) * 16)
                        for m in range(2):
                            ins = nc.tensor.matmul(g.ps[0:ROWS[n], 2 * (n % 2) + m, :], diag[:, half, k, 0:ROWS[n]],
                                                   down[:, c, m * 512:(m + 1) * 512], start=False, stop=last and k == GROUP - 1)
                        ins.then_inc(s.downs_done, 1)

                pe.sem_inc(s.downs_done, LEAD)
                for n in range(TILES):
                    r = ROWS[n]
                    if n >= 2:
                        pe.wait_ge(s.x_copied, n - 1)
                    for m in range(2):
                        nc.tensor.matmul(g.ps[0:r, 2 * (n % 2) + m, :], ident(g, r), g.x[0:r, n, m * 512:(m + 1) * 512],
                                         start=True, stop=False)
                    with pe.Fori(0, TURNS[n] // 2 - 1) as i:
                        add(n, 2 * i, 0, i)
                        add(n, 2 * i + 1, 1, i)
                    add(n, TURNS[n] - 2, 0, TURNS[n] // 2 - 1)
                    add(n, TURNS[n] - 1, 1, TURNS[n] // 2 - 1, last=True)
                    pe.wait_ge(s.downs_done, (n * FULL + TURNS[n]) * GROUP + LEAD)
                    pe.sem_inc(s.summed, 1)
    clear_semaphores(nc, g)


def build(nc, t, o):
    with ExitStack() as ctx:
        g = State()
        sb = lambda name, shape, dt=F32: ctx.enter_context(nc.sbuf_tensor(fresh(name), shape, dt))
        numbers = []

        def keep(name):
            return ctx.enter_context(nc.semaphore(name))

        def make(name):
            sem = keep(name)
            numbers.append(sem.num)
            return sem

        g.s = Semaphores(make, keep)
        numbers.sort()
        g.runs, first = [], numbers[0]
        for a, b in zip(numbers, numbers[1:] + [None]):
            if b != a + 1:
                g.runs.append((first, a))
                first = b
        s = g.s
        g.consts, g.ones = sb("consts_sb", [P, N_CONST]), sb("ones", [P, P])
        g.x, g.hT, g.pscale = sb("x", [P, TILES, D]), sb("hT", [P, KT, TOK]), sb("pscale", [P, PW // P])
        g.before = sb("before", [P, 1])
        g.ps = ctx.enter_context(nc.psum_tensor("ps", [P, 8, 512], F32))
        with nc.Block() as block:
            @block.sync
            def _(sp):
                sp.dma_start(g.consts[:], t["consts"]).then_inc(s.loaded, 16)
                sp.dma_start(g.x[:, 0:4, :], t["x_prompt"][0].rearrange("(n p) d -> p n d", p=P)).then_inc(s.loaded, 16)
                sp.dma_start(g.x[0:NS, 4, :], t["x_sample"].rearrange("b t d -> (b t) d")).then_inc(s.loaded, 16)
                sp.wait_ge(s.loaded, 48)

            @block.gpsimd
            def _(pool):
                nc.gpsimd.memset(g.ones[:], 1.0).then_inc(s.filled, 1)
                nc.gpsimd.memset(g.before[:], 0.0).then_inc(s.filled, 1)
                pool.wait_ge(s.filled, 2)
        clear_semaphores(nc, g)
        with nc.Fori(0, DEPTH) as l:
            with ExitStack() as mix:
                sbm = lambda name, shape: mix.enter_context(nc.sbuf_tensor(fresh(name), shape, F32))
                g.oa, g.ob = sbm("oa", [P, H, TOK]), sbm("ob", [P, 2, TOK])
                with ExitStack() as inner:
                    rows = inner.enter_context(nc.sbuf_tensor(fresh("rows"), [P, TILES, D], F32))
                    norm_stage(nc, g, t["norm_mix"][bass.ds(l, 1)], rows)
                delta_stage(nc, g, t, o, l)
                window_stage(nc, g, t, o, l)
                oc = sbm("oc", [P, PW // P, TOK])
                pool_stage(nc, g, t, o, l, oc)
                merge_stage(nc, g, t, l, oc)
            with ExitStack() as ffn:
                sbf = lambda name, shape, dt=F32: ffn.enter_context(nc.sbuf_tensor(fresh(name), shape, dt))
                rows, ids, gates = sbf("rows", [P, TILES, D]), sbf("ids", [P, TILES, CHOICES], U32), sbf("gates", [P, TILES, CHOICES])
                norm_stage(nc, g, t["norm_ffn"][bass.ds(l, 1)], rows)
                sc = sbf("sc", [P, TILES, NQ, KEYS])
                router = Router(nc, g, sbf, sc, ids, gates)
                score_stage(nc, g, t, l, sc, router)
                expert_stage(nc, g, t, l, rows, sc, ids, gates, router)
        with ExitStack() as last:
            rows = last.enter_context(nc.sbuf_tensor(fresh("rows"), [P, TILES, D], F32))
            norm_stage(nc, g, t["norm_final"], rows, transposed=False)
            with nc.Block() as block:
                @block.sync
                def _(sp):
                    sp.dma_start(o["y_p"][0].rearrange("(n p) d -> p n d", p=P), rows[:, 0:4, :]).then_inc(s.stored, 16)
                    sp.dma_start(o["y_s"].rearrange("b t d -> (b t) d"), rows[0:NS, 4, :]).then_inc(s.stored, 16)
                    sp.wait_ge(s.stored, 32)


INPUTS = ["x_prompt", "x_sample", "state_delta", "state_conv", "cache_win0", "cache_win1", "cache_win2", "state_pool",
          "norm_mix", "w_in", "conv_w", "a_log", "dt_bias", "dn_norm", "w_pool", "pool_scale", "w_branch", "w_out",
          "norm_ffn", "peer_query", "peer_subkeys", "peer_up", "peer_down", "norm_final"]


def win(i, prompt):
    rows = min(GROUPS[i][0], SEQ if prompt else PAST + NT)
    return (DEPTH, 1 if prompt else NB, rows, 2, SLOTS, SD)


OUTPUTS = [("y_p", (1, SEQ, D)), ("y_s", (NB, NT, D)), ("delta_p", (DEPTH, 1, H, HD, HD)), ("delta_s", (DEPTH, NB, H, HD, HD)),
           ("conv_p", (DEPTH, 1, CONV - 1, QKV)), ("conv_s", (DEPTH, NB, CONV - 1, QKV)),
           ("win0_p", win(0, True)), ("win0_s", win(0, False)), ("win1_p", win(1, True)), ("win1_s", win(1, False)),
           ("win2_p", win(2, True)), ("win2_s", win(2, False)), ("pool_p", (DEPTH, 1, PBUF, PW)), ("pool_s", (DEPTH, NB, PBUF, PW))]


def kernel(**inputs):
    _names.clear()
    import concourse.bacc as bacc
    from concourse.bass_utils import run_bass_kernel_spmd as run

    nc = bacc.Bacc("TRN2", target_bir_lowering=False, num_devices=1)
    arrays = {f"in_{name}": np.ascontiguousarray(inputs[name]) for name in INPUTS}
    arrays["in_norm_final"] = arrays["in_norm_final"].reshape(1, D)
    arrays["in_consts"] = constants()
    t = {name[3:]: nc.dram_tensor(name, a.shape, mybir.dt.from_np(a.dtype), kind="ExternalInput").ap() for name, a in arrays.items()}
    o = {name: nc.dram_tensor(f"out_{name}", shape, F32, kind="ExternalOutput").ap() for name, shape in OUTPUTS}
    build(nc, t, o)
    r = run(nc, [arrays], core_ids=[0])
    return tuple(r.results[0][f"out_{name}"] for name, _ in OUTPUTS)
```

```python
import numpy as np
from contextlib import ExitStack

import concourse.bass as bass
from concourse import mybir

F32 = mybir.dt.float32
U32 = mybir.dt.uint32
ALU = mybir.AluOpType
ACT = mybir.ActivationFunctionType
AX = mybir.AxisListType

D = 1024
DEPTH = 2
SEQ, NB, NT = 512, 8, 8
PAST = 256
EPS = 1e-6
H, HD = 4, 128
QKV = 3 * H * HD
CONV = 4
GROUPS = ((128, 1), (512, 4), (2048, 16))
SLOTS, SD = 4, 64
SW = len(GROUPS) * SLOTS * SD
POOLS = (2, 4, 8, 16)
PG = 384
PW = len(POOLS) * PG
PBUF = max(POOLS) - 1
C_Z, C_AB, C_B = QKV, QKV + 512, QKV + 512 + 2 * H
C_U = C_B + 3 * SW
C_G = C_U + PW
IN_COLS = C_G + 3 * D
KEYS, PH, TOPK = 128, 8, 16
EXPERTS = KEYS * KEYS
NQ = PH * 2

P = 128
TILES = 5
KT = D // P
NS = NB * NT
TOK = SEQ + NS
HALF = TOK // 2
ROWS = [P, P, P, P, NS]
LEVELS = 7


_names = {}


def fresh(name):
    _names[name] = _names.get(name, 0) + 1
    return f"{name}_{_names[name]}"


def cols(n):
    return slice(n * P, n * P + ROWS[n])


_at = 0
CONST = {}
for _name, _n in (("ident", P), ("upper_p", P), ("upper_s", P), ("strict_p", P), ("strict_s", P),
                  ("full_s", P), ("levels", LEVELS * P), ("amask", 256 + 512 + 512), ("smask", 832),
                  ("cos", TILES * 32), ("sin", TILES * 32), ("count", len(POOLS) * 16), ("iota", TOPK),
                  ("own", NB), ("ident2", NS)):
    CONST[_name] = (_at, _n)
    _at += _n
N_CONST = _at
NEG = -1.0e30


def constants():
    c = np.zeros((P, N_CONST), np.float32)

    def put(name, a):
        o, n = CONST[name]
        c[: a.shape[0], o:o + n] = a.reshape(a.shape[0], -1)

    i = np.arange(P)
    same = (i[:, None] // NT == i[None, :] // NT) & (i[:, None] < NS) & (i[None, :] < NS)
    le, lt = i[:, None] <= i[None, :], i[:, None] < i[None, :]
    put("ident", np.eye(P))
    put("upper_p", le * 1.0)
    put("upper_s", (le & same) * 1.0)
    put("strict_p", lt * 1.0)
    put("strict_s", (lt & same) * 1.0)
    put("full_s", same * 1.0)
    lv = [((i[None, :] >> j) % 2 == 1) & ((i[:, None] >> j) == (i[None, :] >> j) - 1) for j in range(LEVELS)]
    put("levels", np.stack(lv, 1) * 1.0)
    q, k = i[:, None], i[None, :]
    seg = [(k >= q), (k <= q)]
    for _, dil in GROUPS[1:]:
        res = (q - k) % dil == 0
        seg += [res] * 3 + [res & (k <= q)]
    put("amask", np.where(np.concatenate(seg, 1), 0.0, NEG))
    t = (np.arange(NS) % NT)[:, None]
    b = (np.arange(NS) // NT)[:, None]
    seg = [np.arange(128)[None] >= t]
    for _, dil in GROUPS[1:]:
        seg.append((PAST + t - np.arange(PAST)[None]) % dil == 0)
    for _, dil in GROUPS:
        seg.append((b == b.T) & (t.T <= t) & ((t - t.T) % dil == 0))
    put("smask", np.where(np.concatenate(seg, 1), 0.0, NEG))
    inv = np.float32(10000.0) ** (-np.arange(32, dtype=np.float32) / np.float32(32))
    pos = np.concatenate([np.arange(SEQ), PAST + np.arange(NS) % NT, np.zeros(TILES * P - TOK)])
    ang = pos.astype(np.float32).reshape(TILES, P).T[:, :, None] * inv.astype(np.float32)
    put("cos", np.cos(ang))
    put("sin", np.sin(ang))
    cnt = [1.0 / np.minimum(float(w), np.arange(16) + 1.0) for w in POOLS]
    put("count", np.tile(np.stack(cnt)[None], (P, 1, 1)))
    put("iota", np.tile(np.arange(TOPK, dtype=np.float32), (P, 1)))
    put("ident2", i[:, None] % NS == np.arange(NS)[None])
    put("own", (i[:, None] // NT == np.arange(NB)[None]) * 1.0)
    return c


class Semaphores:

    def __init__(self, make, keep):
        self.loaded = make("loaded")
        self.loaded2 = make("loaded2")
        self.loaded3 = make("loaded3")
        self.map0 = make("map0")
        self.map1 = make("map1")
        self.slab0 = make("slab0")
        self.slab1 = make("slab1")
        self.slab_free = make("slab_free")
        self.stored = make("stored")
        self.link_act = make("link_act")
        self.link_dve = make("link_dve")
        self.link_pool = make("link_pool")
        self.pe_a = make("pe_a")
        self.pe_b = make("pe_b")
        self.pe_c = make("pe_c")
        self.pe_d = make("pe_d")
        self.pe_e = make("pe_e")
        self.act_a = make("act_a")
        self.act_b = make("act_b")
        self.act_c = make("act_c")
        self.act_d = make("act_d")
        self.act_e = make("act_e")
        self.dve_a = make("dve_a")
        self.dve_b = make("dve_b")
        self.dve_c = make("dve_c")
        self.dve_d = make("dve_d")
        self.dve_e = make("dve_e")
        self.pool_a = make("pool_a")
        self.pool_b = make("pool_b")
        self.pool_c = make("pool_c")
        self.pool_d = make("pool_d")
        self.filled = make("filled")
        self.copied = make("copied")
        self.numbers = make("numbers")
        self.paced = make("paced")
        self.dots_done = make("dots_done")
        self.downs_done = make("downs_done")
        self.gelus = make("gelus")
        self.weighted = make("weighted")
        self.diagonal = make("diagonal")
        self.summed = make("summed")
        self.x_copied = make("x_copied")
        self.gate_in = make("gate_in")
        self.gate_exp = make("gate_exp")
        self.routed = make("routed")
        self.scored = make("scored")
        self.doubled = make("doubled")
        self.ab_read = make("ab_read")
        self.banks_read = make("banks_read")
        self.stored2 = keep("stored2")
        self.up0 = keep("up0")
        self.up1 = keep("up1")
        self.up2 = keep("up2")
        self.up3 = keep("up3")
        self.up4 = keep("up4")
        self.up5 = keep("up5")
        self.up6 = keep("up6")
        self.up7 = keep("up7")
        self.down0 = keep("down0")
        self.down1 = keep("down1")
        self.down2 = keep("down2")
        self.down3 = keep("down3")
        self.down4 = keep("down4")
        self.down5 = keep("down5")
        self.down6 = keep("down6")
        self.down7 = keep("down7")


class State:
    pass


class Link:

    def __init__(self, eng, sem):
        self.eng, self.sem, self.n, self.base = eng, sem, 0, 0

    def __call__(self, ins):
        ins.then_inc(self.sem, 1)
        self.n += 1
        self.eng.wait_ge(self.sem, self.base + self.n)


def bc(ap, dim, n):
    v = ap.unsqueeze(dim)
    shape = list(v.shape)
    shape[dim] = n
    return v.broadcast_to(shape)


def table(g, name, rows=P):
    o, n = CONST[name]
    return g.consts[0:rows, o:o + n]


def ident(g, rows=P):
    return table(g, "ident", rows)[:, 0:rows]


def layer(ap, l):
    names = " ".join(f"d{i}" for i in range(len(ap.shape) - 1))
    first = names.split(" ")[0]
    return ap[bass.ds(l, 1)].rearrange(f"a {names} -> (a {first}) {names[len(first) + 1:]}")


def clear_semaphores(nc, g):
    with nc.Block() as block:
        @block.gpsimd
        def _(pool):
            for first, last in g.runs:
                pool.sem_clear(range(first, last + 1))


def norm_stage(nc, g, gamma, rows, transposed=True, ring=None, sources=()):
    s = g.s
    with ExitStack() as ctx:
        sb = lambda name, shape: ctx.enter_context(nc.sbuf_tensor(fresh(name), shape, F32))
        gam, junk, ss = sb("gam", [P, D]), sb("junk", [P, D]), sb("ss", [P, 8])
        with nc.Block() as block:
            @block.sync
            def _(sp):
                sp.dma_start(gam[:], gamma.broadcast_to([P, D])).then_inc(s.loaded, 16)
                if sources:
                    load_ahead(sp, g, ring, sources)

            @block.scalar
            def _(act):
                link = Link(act, s.link_act)
                act.wait_ge(s.filled, 1)
                for n in range(TILES):
                    r = ROWS[n]
                    ins = nc.scalar.activation(junk[0:r], g.x[0:r, n, :], ACT.Square, accum_out=ss[0:r, n:n + 1])
                    if n < TILES - 1:
                        link(ins)
                    else:
                        ins.then_inc(s.act_a, 1)
                act.wait_ge(s.dve_a, 1)
                nc.scalar.activation(ss[:, 0:TILES], ss[:, 0:TILES], ACT.Sqrt).then_inc(s.act_b, 1)
                if transposed:
                    for u in range(2 * TILES):
                        n, half = u // 2, u % 2
                        act.wait_ge(s.pe_a, u + 1)
                        nc.scalar.copy(g.hT[:, 4 * half:4 * half + 4, cols(n)],
                                       g.ps[:, u % 4, :].rearrange("p (k c) -> p k c", k=4)[:, :, 0:ROWS[n]]
                                       ).then_inc(s.act_c, 1)

            @block.vector
            def _(dve):
                link = Link(dve, s.link_dve)
                nc.vector.memset(ss[:], 1.0).then_inc(s.filled, 1)
                dve.wait_ge(s.act_a, 1)
                link(nc.vector.tensor_scalar(ss[:, 0:TILES], ss[:, 0:TILES], 1.0 / D, EPS, ALU.mult, ALU.add))
                nc.vector.reciprocal(ss[:, 0:TILES], ss[:, 0:TILES]).then_inc(s.dve_a, 1)
                dve.wait_ge(s.act_b, 1)
                dve.wait_ge(s.loaded, 16)
                for n in range(TILES):
                    r = ROWS[n]
                    nc.vector.scalar_tensor_tensor(out=rows[0:r, n, :], in0=g.x[0:r, n, :], scalar=ss[0:r, n:n + 1],
                                                   in1=gam[0:r, :], op0=ALU.mult, op1=ALU.mult).then_inc(s.dve_b, 1)

            if transposed:
                @block.tensor
                def _(pe):
                    for u in range(2 * TILES):
                        n, half = u // 2, u % 2
                        pe.wait_ge(s.dve_b, n + 1)
                        if u >= 4:
                            pe.wait_ge(s.act_c, u - 3)
                        for k in range(4):
                            kk = 4 * half + k
                            last = nc.tensor.transpose(g.ps[:, u % 4, k * P:k * P + ROWS[n]],
                                                       rows[0:ROWS[n], n, kk * P:(kk + 1) * P], ident(g, ROWS[n]))
                        last.then_inc(s.pe_a, 1)
    clear_semaphores(nc, g)


BANKS_A, BANKS_B = 3, 2


def project(nc, g, pe, u, weights, rhs, nk, done, free_a, free_b):
    if u >= BANKS_A:
        pe.wait_ge(free_a, u - BANKS_A + 1)
    if u >= BANKS_B:
        pe.wait_ge(free_b, 2 * (u - BANKS_B + 1))
    for k in range(nk):
        nc.tensor.matmul(part_a(g, u), weights(k), rhs(k)[:, 0:HALF], start=k == 0, stop=k == nk - 1)
        last = nc.tensor.matmul(part_b(g, u), weights(k), rhs(k)[:, HALF:TOK], start=k == 0, stop=k == nk - 1)
    last.then_inc(done, 1)


def part_a(g, u):
    return g.ps[:, u % BANKS_A, 0:HALF]


def part_b(g, u):
    return g.ps[:, BANKS_A + u % BANKS_B, 0:HALF]


def part_b_prompt(g, u):
    return part_b(g, u)[:, 0:SEQ - HALF]


def part_b_samples(g, u):
    return part_b(g, u)[:, SEQ - HALF:HALF].rearrange("p (b j) -> p b j", b=NB)


def load_ahead(sp, g, ring, sources):
    for i, src in enumerate(sources[0:2]):
        nk, w = src.shape[1], src.shape[2]
        sp.dma_start(ring[:, i, 0:nk * w].rearrange("p (k c) -> p k c", k=nk), src).then_inc(g.s.loaded3, 16)
    sp.wait_ge(g.s.loaded3, 32)


def load_slabs(sp, g, ring, sources, ahead=0):
    slab = (g.s.slab0, g.s.slab1)
    for i, src in enumerate(sources):
        if i < ahead:
            continue
        if i >= 2:
            sp.wait_ge(g.s.slab_free, i - 1)
        nk, w = src.shape[1], src.shape[2]
        sp.dma_start(ring[:, i % 2, 0:nk * w].rearrange("p (k c) -> p k c", k=nk), src).then_inc(slab[i % 2], 16)


def slab_ready(eng, g, i, ahead=0):
    if i >= ahead:
        eng.wait_ge((g.s.slab0, g.s.slab1)[i % 2], 16 * ((i - ahead) // 2 + 1))


def slab_view(ring, i, nk, w):
    return ring[:, i % 2, 0:nk * w].rearrange("p (k c) -> p k c", k=nk)


def rows_of(w):
    return w.rearrange("(k p) c -> p k c", p=P)


EXT = CONV - 1 + SEQ + NB * (CONV - 1 + NT)
EXT_S = CONV - 1 + SEQ


def delta_stage(nc, g, t, o, l):
    s = g.s
    w_in = layer(t["w_in"], l)
    with ExitStack() as ctx:
        sb = lambda name, shape, dt=F32, c=ctx: c.enter_context(nc.sbuf_tensor(fresh(name), shape, dt))
        zT, cc = sb("zT", [P, 4, TOK]), sb("cc", [P, 12, TOK])
        vecs, ab = sb("vecs", [P, 64]), sb("ab", [P, TILES, 8])
        heads, gb = sb("heads", [P, 8]), sb("gb", [P, TILES, 8])
        with ExitStack() as inner:
            ring = sb("ring", [P, 2, 4096], F32, inner)
            slabs = [rows_of(w_in)[:, :, i * 512:(i + 1) * 512] for i in range(4)]
            with ExitStack() as first:
                norm_stage(nc, g, t["norm_mix"][bass.ds(l, 1)], sb("rows", [P, TILES, D], F32, first), ring=ring, sources=slabs)
            delta_in(nc, g, t, o, l, w_in, zT, cc, vecs, ab, heads, ring, slabs, lambda n, sh: sb(n, sh, F32, inner))
        clear_semaphores(nc, g)
        with ExitStack() as inner:
            delta_chunks(nc, g, t, o, l, zT, cc, vecs, ab, heads, gb, lambda n, sh: sb(n, sh, F32, inner))


NORMED = 2 * H


def delta_in(nc, g, t, o, l, w_in, zT, cc, vecs, ab, heads, ring, slabs, sb):
    s = g.s
    wab = sb("wab", [P, KT, 8])
    ext, tail = sb("ext", [P, 12, EXT]), sb("tail", [P, 12, 27])
    vrows, old, new = sb("vrows", [61, P]), sb("old", [24, QKV]), sb("new", [27, QKV])
    sq, rn = sb("sq", [P, 4, TOK]), sb("rn", [P, NORMED, TOK])
    ones = g.ones
    samples = ext[:, :, EXT_S:EXT].rearrange("p c (b j) -> p c b j", b=NB)
    with nc.Block() as block:
        @block.sync
        def _(sp):
            load_slabs(sp, g, ring, slabs, ahead=2)
            sp.wait_ge(s.act_d, 1)
            sp.dma_start(layer(o["conv_p"], l).rearrange("b j c -> (b j) c"), new[0:3]).then_inc(s.stored, 16)
            sp.dma_start(layer(o["conv_s"], l).rearrange("b j c -> (b j) c"), new[3:27]).then_inc(s.stored, 16)
            sp.wait_ge(s.stored, 32)
            sp.wait_ge(s.loaded3, 32)

        @block.tensor
        def _(pe):
            for u in range(16):
                if u % 4 == 0:
                    slab_ready(pe, g, u // 4, ahead=2)
                w = slab_view(ring, u // 4, KT, 512)
                project(nc, g, pe, u, lambda k: w[:, k, (u % 4) * P:(u % 4 + 1) * P], lambda k: g.hT[:, k, :], KT,
                        s.pe_a, s.act_a, s.dve_a)
                if u % 4 == 3:
                    pe.wait_ge(s.pe_a, u + 1)
                    pe.sem_inc(s.slab_free, 1)
                if u == 0:
                    pe.wait_ge(s.loaded, 64)
                    nc.tensor.transpose(g.ps[:, 5, 0:61], vrows[:], ident(g, 61))
                    for c in range(12):
                        last = nc.tensor.transpose(g.ps[:, 5, 64 + c * 24:64 + (c + 1) * 24], old[:, c * P:(c + 1) * P], ident(g, 24))
                    last.then_inc(s.pe_b, 1)
                if u == 8:
                    pe.wait_ge(s.loaded2, 16)
                    for n in range(TILES):
                        for k in range(KT):
                            last = nc.tensor.matmul(g.ps[0:ROWS[n], 6, n * 8:n * 8 + 8], g.hT[:, k, cols(n)], wab[:, k, :],
                                                    start=k == 0, stop=k == KT - 1)
                    last.then_inc(s.pe_c, 1)
                c = u - 2
                if 0 <= c < NORMED:
                    pe.wait_ge(s.act_e, c + 1)
                    if c:
                        pe.wait_ge(s.dve_d, c)
                    else:
                        pe.wait_ge(s.act_b, 2)
                    nc.tensor.matmul(g.ps[:, 7, :], ones[:], sq[:, c % 4, 0:SEQ], start=True, stop=True)
                    nc.tensor.matmul(g.ps[:, 5, 0:NS], ones[:], sq[:, c % 4, SEQ:TOK], start=True, stop=True).then_inc(s.pe_e, 1)
                if u == 13:
                    pe.wait_ge(s.dve_b, 1)
                    pe.wait_ge(s.dve_d, NORMED)
                    pe.wait_ge(s.ab_read, 1)
                    for c in range(12):
                        last = nc.tensor.transpose(g.ps[0:27, 5 + c // 4, (c % 4) * P:(c % 4 + 1) * P], tail[:, c, :], ident(g))
                    last.then_inc(s.pe_d, 1)

        @block.gpsimd
        def _(pool):
            nc.gpsimd.memset(ext[:, :, 0:CONV - 1], 0.0).then_inc(s.filled, 1)
            nc.gpsimd.memset(ab[:], 0.0).then_inc(s.filled, 1)

        @block.scalar
        def _(act):
            act.dma_start(vrows[0:48], layer(t["conv_w"], l).rearrange("w (c p) -> (w c) p", p=P)).then_inc(s.loaded, 16)
            act.dma_start(vrows[48:60], layer(t["pool_scale"].rearrange("l (c p) -> l c p", p=P), l)).then_inc(s.loaded, 16)
            act.dma_start(vrows[60:61], t["dn_norm"][bass.ds(l, 1)]).then_inc(s.loaded, 16)
            act.dma_start(old[:], layer(t["state_conv"], l).rearrange("b j c -> (b j) c")).then_inc(s.loaded, 16)
            act.dma_start(wab[:], rows_of(w_in)[:, :, C_AB:C_AB + 8]).then_inc(s.loaded2, 16)
            act.dma_start(heads[:, 0:4], t["a_log"][bass.ds(l, 1)].broadcast_to([P, 4])).then_inc(s.loaded3, 16)
            act.dma_start(heads[:, 4:8], t["dt_bias"][bass.ds(l, 1)].broadcast_to([P, 4])).then_inc(s.loaded3, 16)
            for u in range(16):
                act.wait_ge(s.pe_a, u + 1)
                dst = ext[:, u, CONV - 1:CONV - 1 + HALF] if u < 12 else zT[:, u - 12, 0:HALF]
                nc.scalar.copy(dst, part_a(g, u)).then_inc(s.act_a, 1)
                if u == 0:
                    act.wait_ge(s.pe_b, 1)
                    nc.scalar.copy(vecs[:, 0:61], g.ps[:, 5, 0:61]).then_inc(s.act_b, 1)
                    nc.scalar.copy(samples[:, :, :, 0:CONV - 1],
                                   g.ps[:, 5, 64:352].rearrange("p (c b j) -> p c b j", c=12, b=NB)).then_inc(s.act_b, 1)
                c = u - 1
                if 0 <= c < 12:
                    act.wait_ge(s.dve_c, c + 1)
                    nc.scalar.activation(cc[:, c, :], cc[:, c, :], ACT.Silu).then_inc(s.act_c, 1)
                if 0 <= c < NORMED:
                    act.wait_ge(s.act_c, c + 1)
                    if c >= 4:
                        act.wait_ge(s.pe_e, c - 3)
                    nc.scalar.activation(sq[:, c % 4, :], cc[:, c, :], ACT.Square).then_inc(s.act_e, 1)
                if u == 10:
                    act.wait_ge(s.dve_e, NORMED)
                    nc.scalar.activation(rn[:], rn[:], ACT.Sqrt).then_inc(s.copied, 1)
                if u == 14:
                    act.wait_ge(s.pe_d, 1)
                    nc.scalar.copy(new[:].rearrange("p (j c) -> p j c", j=3), g.ps[0:27, 5:8, :]).then_inc(s.act_d, 1)

        @block.vector
        def _(dve):
            link = Link(dve, s.link_dve)

            def convolve(c):
                dve.wait_ge(s.act_a, c + 1)
                dve.wait_ge(s.act_b, 2)
                dve.wait_ge(s.dve_a, 2 * (c + 1))
                ins_p = lambda w: ext[:, c, w:w + SEQ]
                ins_s = lambda w: samples[:, c, :, w:w + NT]
                out_p, out_s = cc[:, c, 0:SEQ], cc[:, c, SEQ:TOK].rearrange("p (b j) -> p b j", b=NB)
                wt = lambda w: vecs[:, w * 12 + c:w * 12 + c + 1]
                nc.vector.tensor_scalar(out_p, ins_p(0), wt(0), None, ALU.mult).then_inc(s.link_dve, 1)
                link.n += 1
                link(nc.vector.tensor_scalar(out_s, ins_s(0), wt(0), None, ALU.mult))
                for w in range(1, CONV):
                    nc.vector.scalar_tensor_tensor(out=out_p, in0=ins_p(w), scalar=wt(w), in1=out_p, op0=ALU.mult,
                                                   op1=ALU.add).then_inc(s.link_dve, 1)
                    link.n += 1
                    last = nc.vector.scalar_tensor_tensor(out=out_s, in0=ins_s(w), scalar=wt(w), in1=out_s,
                                                          op0=ALU.mult, op1=ALU.add)
                    if w < CONV - 1:
                        link(last)
                last.then_inc(s.dve_c, 1)

            dve.wait_ge(s.filled, 2)
            for u in range(16):
                dve.wait_ge(s.pe_a, u + 1)
                if u < 12:
                    nc.vector.tensor_copy(ext[:, u, CONV - 1 + HALF:EXT_S], part_b_prompt(g, u)).then_inc(s.dve_a, 1)
                    nc.vector.tensor_copy(samples[:, u, :, CONV - 1:], part_b_samples(g, u)).then_inc(s.dve_a, 1)
                else:
                    nc.vector.tensor_copy(zT[:, u - 12, HALF:TOK], part_b(g, u)).then_inc(s.dve_a, 2)
                if u == 10:
                    dve.wait_ge(s.pe_c, 1)
                    link(nc.vector.tensor_copy(ab[:, 0:4, :], g.ps[:, 6, 0:32].rearrange("p (n c) -> p n c", n=4)))
                    nc.vector.tensor_copy(ab[0:NS, 4, :], g.ps[0:NS, 6, 32:40]).then_inc(s.ab_read, 1)
                c = u - 3
                if 0 <= c < NORMED:
                    dve.wait_ge(s.pe_e, c + 1)
                    link(nc.vector.tensor_scalar(rn[:, c, 0:SEQ], g.ps[:, 7, :], EPS, None, ALU.add))
                    nc.vector.tensor_scalar(rn[:, c, SEQ:TOK], g.ps[:, 5, 0:NS], EPS, None, ALU.add).then_inc(s.dve_d, 1)
                    dve.wait_ge(s.dve_d, c + 1)
                    nc.vector.reciprocal(rn[:, c], rn[:, c]).then_inc(s.dve_e, 1)
                if 0 < u <= 12:
                    convolve(u - 1)
                if u == 12:
                    link(nc.vector.tensor_copy(tail[:, :, 0:3], ext[:, :, EXT_S - 3:EXT_S]))
                    nc.vector.tensor_copy(tail[:, :, 3:27].rearrange("p c (b j) -> p c b j", b=NB), samples[:, :, :, NT:NT + 3]
                                          ).then_inc(s.dve_b, 1)
                if u in (13, 14):
                    r = u - 13
                    dve.wait_ge(s.copied, 1)
                    q = cc[:, 4 * r:4 * r + 4, :]
                    link(nc.vector.scalar_tensor_tensor(out=q, in0=rn[:, 4 * r:4 * r + 4], scalar=HD ** -0.5 if r == 0 else 1.0, in1=q,
                                                        op0=ALU.mult, op1=ALU.mult))


def heads_of(a, n):
    r = ROWS[n]
    return a[0:r, n * 512:n * 512 + H * r].rearrange("p (h c) -> p h c", h=H)


SQ = 4 * 512 + H * NS


def delta_chunks(nc, g, t, o, l, zT, cc, vecs, ab, heads, gb, sb):
    s = g.s
    krow, vrow = sb("krow", [P, TILES, 512]), sb("vrow", [P, TILES, 512])
    dec, low, lowm, inv, invT, mid = (sb(n, [P, SQ]) for n in ("dec", "low", "lowm", "inv", "invT", "mid"))
    kbg = sb("kbg", [P, TILES, 512])
    st = sb("st", [P, H, NB, HD])
    cl, lastg = sb("cl", [P, TILES, 12]), sb("lastg", [P, 4 * H + H * NB])
    qT = lambda n, h: cc[:, h, cols(n)]
    kT = lambda n, h: cc[:, 4 + h, cols(n)]
    upper = lambda n: table(g, "upper_p" if n < 4 else "upper_s", ROWS[n])[:, 0:ROWS[n]]
    strict = lambda n: table(g, "strict_p" if n < 4 else "strict_s", ROWS[n])[:, 0:ROWS[n]]
    full = lambda n: (g.ones[:] if n < 4 else table(g, "full_s", NS)[:, 0:NS])
    level = lambda n, j: table(g, "levels", ROWS[n])[:, j * P:j * P + ROWS[n]]
    row = lambda a, n: a[0:ROWS[n], n, :].rearrange("p (h d) -> p h d", h=H)
    bank = lambda b, r, w: g.ps[0:r, b, 0:H * w].rearrange("p (h c) -> p h c", h=H)
    run = lambda j: [n for n in range(TILES) if n < 4 or j < 3]
    todo = [(j, n) for j in range(LEVELS) for n in run(j)]
    egr = st[:, 0:4].rearrange("p h b d -> p (h b d)")

    with nc.Block() as block:
        @block.tensor
        def _(pe):
            for u in range(2 * TILES):
                n, v = u // 2, u % 2
                if u >= 2:
                    pe.wait_ge(s.act_a, u - 1)
                for h in range(H):
                    last = nc.tensor.transpose(g.ps[0:ROWS[n], u % 2, h * P:(h + 1) * P], cc[:, 4 + 4 * v + h, cols(n)], ident(g))
                last.then_inc(s.pe_a, 1)
            for n in range(TILES):
                r = ROWS[n]
                pe.wait_ge(s.dve_b, n + 1)
                if n:
                    pe.wait_ge(s.banks_read, n)
                nc.tensor.matmul(bank(2, P, r), g.ones[0:r, :], heads_of(lowm, n), start=True, stop=True)
                nc.tensor.matmul(bank(3, P, r), g.ones[0:r, :], heads_of(mid, n), start=True, stop=True)
                nc.tensor.matmul(g.ps[0:r, 4, 0:4], upper(n), gb[0:r, n, 0:4], start=True, stop=True)
                nc.tensor.matmul(g.ps[0:r, 4, 4:8], full(n), gb[0:r, n, 0:4], start=True, stop=True)
                for h in range(H):
                    nc.tensor.matmul(g.ps[0:r, 5, h * r:(h + 1) * r], kT(n, h), kT(n, h), start=True, stop=True)
                for h in range(H):
                    last = nc.tensor.matmul(g.ps[0:r, 6, h * r:(h + 1) * r], kT(n, h), qT(n, h), start=True, stop=True)
                last.then_inc(s.pe_b, 1)

        @block.scalar
        def _(act):
            link = Link(act, s.link_act)
            act.wait_ge(s.dve_a, 1)
            link(nc.scalar.activation(ab[:, :, 0:4], ab[:, :, 0:4], ACT.Exp, scale=-1.0))
            link(nc.scalar.activation(heads[:, 0:4], heads[:, 0:4], ACT.Exp))
            nc.scalar.activation(ab[:, :, 0:4], ab[:, :, 0:4], ACT.Ln, bias=1.0).then_inc(s.act_b, 1)
            nc.scalar.activation(gb[:, :, 4:8], ab[:, :, 4:8], ACT.Sigmoid).then_inc(s.act_b, 1)
            for u in range(2 * TILES):
                n, v = u // 2, u % 2
                act.wait_ge(s.pe_a, u + 1)
                nc.scalar.copy((vrow if v else krow)[0:ROWS[n], n, :], g.ps[0:ROWS[n], u % 2, :]).then_inc(s.act_a, 1)
            for n in range(TILES):
                r = ROWS[n]
                act.wait_ge(s.pe_b, n + 1)
                if n >= 2:
                    act.wait_ge(s.dve_c, n - 1)
                nc.scalar.activation(egr[:, (n % 2) * 512:(n % 2) * 512 + H * r].rearrange("p (h c) -> p h c", h=H),
                                     bank(2, P, r), ACT.Exp).then_inc(s.act_c, 1)
                act.wait_ge(s.dve_d, n + 1)
                nc.scalar.activation(heads_of(dec, n), heads_of(dec, n), ACT.Exp).then_inc(s.act_d, 1)
                nc.scalar.activation(cl[0:r, n, 0:8], cl[0:r, n, 0:8], ACT.Exp).then_inc(s.act_d, 1)

        @block.vector
        def _(dve):
            link = Link(dve, s.link_dve)
            dt = bc(heads[:, 4:8], 1, TILES)
            a = ab[:, :, 0:4]
            link(nc.vector.tensor_tensor(a, a, dt, ALU.add))
            link(nc.vector.tensor_scalar(gb[:, :, 0:4], a, 0.0, None, ALU.max))
            link(nc.vector.tensor_scalar(cl[:, :, 0:4], a, -1.0, None, ALU.mult))
            nc.vector.tensor_tensor(a, a, cl[:, :, 0:4], ALU.max).then_inc(s.dve_a, 1)
            dve.wait_ge(s.act_b, 2)
            link(nc.vector.tensor_tensor(gb[:, :, 0:4], gb[:, :, 0:4], a, ALU.add))
            link(nc.vector.scalar_tensor_tensor(out=gb[:, :, 0:4], in0=gb[:, :, 0:4], scalar=-1.0,
                                                in1=bc(heads[:, 0:4], 1, TILES), op0=ALU.mult, op1=ALU.mult))

            def spread(n):
                r = ROWS[n]
                link(nc.vector.tensor_tensor(heads_of(lowm, n), bc(upper(n), 1, H), bc(gb[0:r, n, 0:4], 2, r), ALU.mult))
                link(nc.vector.tensor_tensor(heads_of(mid, n), bc(ident(g, r), 1, H), bc(gb[0:r, n, 4:8], 2, r), ALU.mult))
                dve.sem_inc(s.dve_b, 1)

            spread(0)
            for n in range(TILES):
                r = ROWS[n]
                if n + 1 < TILES:
                    spread(n + 1)
                dve.wait_ge(s.pe_b, n + 1)
                link(nc.vector.tensor_copy(cl[0:r, n, 0:8], g.ps[0:r, 4, 0:8]))
                dve.wait_ge(s.act_c, n + 1)
                link(nc.vector.tensor_tensor(heads_of(dec, n), bank(2, r, r), bc(cl[0:r, n, 0:4], 2, r), ALU.subtract))
                link(nc.vector.tensor_scalar(heads_of(dec, n), heads_of(dec, n), 0.0, None, ALU.min))
                nc.vector.tensor_tensor(cl[0:r, n, 4:8], cl[0:r, n, 4:8], cl[0:r, n, 0:4], ALU.subtract).then_inc(s.dve_d, 1)
                dve.wait_ge(s.act_d, 2 * n + 2)
                link(nc.vector.tensor_tensor(heads_of(dec, n), heads_of(dec, n), bc(upper(n), 1, H), ALU.mult))
                link(nc.vector.tensor_tensor(heads_of(low, n), heads_of(dec, n), bank(3, r, r), ALU.mult))
                link(nc.vector.tensor_tensor(heads_of(low, n), heads_of(low, n), bc(strict(n), 1, H), ALU.mult))
                link(nc.vector.tensor_tensor(heads_of(low, n), heads_of(low, n), bank(5, r, r), ALU.mult))
                link(nc.vector.tensor_tensor(heads_of(dec, n), heads_of(dec, n), bank(6, r, r), ALU.mult))
                dve.sem_inc(s.banks_read, 1)
                e = egr[:, (n % 2) * 512:(n % 2) * 512 + H * r].rearrange("p (h c) -> p h c", h=H)
                dve.wait_ge(s.act_c, n + 1)
                link(nc.vector.tensor_tensor(cc[:, 0:H, cols(n)], cc[:, 0:H, cols(n)], e, ALU.mult))
                if n < 4:
                    ins = nc.vector.tensor_copy(lastg[:, 4 * n:4 * n + 4], e[:, :, r - 1])
                else:
                    ins = nc.vector.tensor_copy(lastg[:, 16:48].rearrange("p (h b) -> p h b", h=H),
                                                e.rearrange("p h (b j) -> p h b j", j=NT)[:, :, :, NT - 1])
                link(ins)
                dve.sem_inc(s.dve_c, 1)
                link(nc.vector.tensor_tensor(cl[0:r, n, 8:12], gb[0:r, n, 4:8], cl[0:r, n, 0:4], ALU.mult))
                dve.sem_inc(s.dve_e, 1)

        @block.gpsimd
        def _(pool):
            for n in range(TILES):
                for a in (inv, invT):
                    nc.gpsimd.tensor_copy(heads_of(a, n), bc(ident(g, ROWS[n]), 1, H)).then_inc(s.pool_c, 1)
            for n in range(TILES):
                r = ROWS[n]
                pool.wait_ge(s.dve_e, n + 1)
                pool.wait_ge(s.act_a, 2 * n + 2)
                nc.gpsimd.tensor_tensor(row(kbg, n), row(krow, n), bc(cl[0:r, n, 8:12], 2, HD), ALU.mult).then_inc(s.pool_a, 1)
                pool.wait_ge(s.pool_a, 2 * n + 1)
                nc.gpsimd.tensor_tensor(row(krow, n), row(krow, n), bc(cl[0:r, n, 4:8], 2, HD), ALU.mult).then_inc(s.pool_b, 1)
                nc.gpsimd.tensor_tensor(row(vrow, n), row(vrow, n), bc(gb[0:r, n, 4:8], 2, HD), ALU.mult).then_inc(s.pool_a, 1)
    clear_semaphores(nc, g)

    with nc.Block() as block:
        @block.gpsimd
        def _(pool):
            for i, (j, n) in enumerate(todo):
                if j > 0:
                    pool.wait_ge(s.pe_a, todo.index((j - 1, n)) + 1)
                nc.gpsimd.tensor_tensor(heads_of(lowm, n), heads_of(low, n), bc(level(n, j), 1, H), ALU.mult).then_inc(s.pool_a, 1)

        @block.tensor
        def _(pe):
            for j in range(LEVELS):
                for n in run(j):
                    i, r = todo.index((j, n)), ROWS[n]
                    pe.wait_ge(s.pool_a, i + 1)
                    if j > 0:
                        pe.wait_ge(s.dve_a, todo.index((j - 1, n)) + 1)
                    if i >= 2:
                        pe.wait_ge(s.act_a, i - 1)
                    for h in range(H):
                        last = nc.tensor.matmul(g.ps[0:r, i % 2, h * r:(h + 1) * r], heads_of(lowm, n)[:, h], heads_of(inv, n)[:, h],
                                                start=True, stop=True)
                    last.then_inc(s.pe_a, 1)
                for n in run(j):
                    i, r = todo.index((j, n)), ROWS[n]
                    pe.wait_ge(s.act_a, i + 1)
                    if i >= 2:
                        pe.wait_ge(s.dve_a, i - 1)
                    for h in range(H):
                        if j < LEVELS - 1:
                            nc.tensor.matmul(g.ps[0:r, 2 + i % 2, h * r:(h + 1) * r], heads_of(invT, n)[:, h], heads_of(mid, n)[:, h],
                                             start=True, stop=True)
                        last = nc.tensor.matmul(g.ps[0:r, 4 + i % 2, h * r:(h + 1) * r], heads_of(mid, n)[:, h],
                                                heads_of(invT, n)[:, h], start=True, stop=True)
                    last.then_inc(s.pe_b, 1)

        @block.scalar
        def _(act):
            for i, (j, n) in enumerate(todo):
                act.wait_ge(s.pe_a, i + 1)
                if j > 0:
                    act.wait_ge(s.pe_b, todo.index((j - 1, n)) + 1)
                nc.scalar.copy(heads_of(mid, n), bank(i % 2, ROWS[n], ROWS[n])).then_inc(s.act_a, 1)

        @block.vector
        def _(dve):
            link = Link(dve, s.link_dve)
            for i, (j, n) in enumerate(todo):
                r = ROWS[n]
                dve.wait_ge(s.pe_b, i + 1)
                if j < LEVELS - 1:
                    nc.vector.tensor_tensor(heads_of(inv, n), heads_of(inv, n), bank(2 + i % 2, r, r), ALU.subtract
                                            ).then_inc(s.link_dve, 1)
                nc.vector.tensor_tensor(heads_of(invT, n), heads_of(invT, n), bank(4 + i % 2, r, r), ALU.subtract
                                        ).then_inc(s.dve_a, 1)
    clear_semaphores(nc, g)

    state = low[:, 0:512].rearrange("p (h e) -> p h e", h=H)
    vnew = low[:, 512:1536].rearrange("p (i h e) -> p i h e", i=2, h=H)
    ws = low[:, 1536:1536 + H * NS].rearrange("p (h c) -> p h c", h=H)
    kdm = lowm[0:NS, 0:2048].rearrange("p (i b d) -> p i b d", i=2, b=NB)
    wT = mid
    sd_out = layer(o["delta_s"], l)
    with nc.Block() as block:
        @block.sync
        def _(sp):
            for h in range(H):
                sp.dma_start(st[:, h], layer(t["state_delta"], l)[:, h].rearrange("b d e -> d b e")).then_inc(s.loaded, 16)
            sp.wait_ge(s.dve_b, 4)
            sp.dma_start(layer(o["delta_p"], l)[0].rearrange("h d e -> d h e"), state).then_inc(s.stored, 16)
            for h in range(H):
                sp.wait_ge(s.dve_c, 2 * h + 2)
                sp.dma_start(sd_out[:, h].rearrange("b d e -> d b e"), st[:, h]).then_inc(s.stored, 16)
            sp.wait_ge(s.stored, 16 * 5)

        @block.tensor
        def _(pe):
            for n in range(TILES):
                r = ROWS[n]
                if n >= 2:
                    pe.wait_ge(s.act_a, n - 1)
                for h in range(H):
                    last = nc.tensor.matmul(g.ps[:, n % 2, h * r:(h + 1) * r], row(kbg, n)[:, h], heads_of(invT, n)[:, h],
                                            start=True, stop=True)
                last.then_inc(s.pe_a, 1)
            for n in range(4):
                pe.wait_ge(s.act_a, n + 1)
                if n:
                    pe.wait_ge(s.dve_b, n)
                else:
                    pe.wait_ge(s.filled, 1)
                for h in range(H):
                    nc.tensor.matmul(g.ps[:, 2, h * P:(h + 1) * P], heads_of(invT, n)[:, h], row(vrow, n)[:, h], start=True, stop=False)
                    last = nc.tensor.matmul(g.ps[:, 2, h * P:(h + 1) * P], wT[:, n * 512 + h * P:n * 512 + (h + 1) * P], state[:, h],
                                            start=False, stop=True)
                last.then_inc(s.pe_b, 1)
                pe.wait_ge(s.act_b, n + 1)
                for h in range(H):
                    last = nc.tensor.matmul(g.ps[:, 4, h * P:(h + 1) * P], row(krow, n)[:, h], vnew[:, n % 2, h], start=True, stop=True)
                last.then_inc(s.pe_c, 1)
                if n:
                    pe.wait_ge(s.act_c, n)
                for h in range(H):
                    nc.tensor.matmul(g.ps[:, 3, h * P:(h + 1) * P], state[:, h], qT(n, h), start=True, stop=False)
                    last = nc.tensor.matmul(g.ps[:, 3, h * P:(h + 1) * P], vnew[:, n % 2, h], heads_of(dec, n)[:, h],
                                            start=False, stop=True)
                last.then_inc(s.pe_d, 1)
            pe.wait_ge(s.loaded, 64)
            pe.wait_ge(s.act_a, 5)
            for h in range(H):
                for b in range(NB):
                    c = h * NS + b * NT
                    last = nc.tensor.matmul(g.ps[:, 5, c:c + NT], st[:, h, b], wT[:, 2048 + c:2048 + c + NT], start=True, stop=True)
            last.then_inc(s.pe_b, 1)
            pe.wait_ge(s.act_b, 5)
            for h in range(H):
                nc.tensor.matmul(g.ps[0:NS, 6, h * P:(h + 1) * P], heads_of(invT, 4)[:, h], row(vrow, 4)[:, h], start=True, stop=False)
                last = nc.tensor.matmul(g.ps[0:NS, 6, h * P:(h + 1) * P], ws[:, h], ident(g), start=False, stop=True)
            last.then_inc(s.pe_b, 1)
            pe.wait_ge(s.act_b, 6)
            for h in range(H):
                c = h * NS
                nc.tensor.matmul(g.ps[:, 7, c:c + NS], vnew[0:NS, 0, h], heads_of(dec, 4)[:, h], start=True, stop=False)
                for b in range(NB):
                    last = nc.tensor.matmul(g.ps[:, 7, c + b * NT:c + (b + 1) * NT], st[:, h, b], cc[:, h, SEQ + b * NT:SEQ + (b + 1) * NT],
                                            start=False, stop=b == NB - 1)
            last.then_inc(s.pe_d, 1)
            for u in range(2 * H):
                h, half = u // 2, u % 2
                pe.wait_ge(s.pool_a, h + 1)
                if u >= 2:
                    pe.wait_ge(s.dve_c, u - 1)
                for b in range(4):
                    last = nc.tensor.matmul(g.ps[:, u % 2, b * P:(b + 1) * P], kdm[:, h % 2, 4 * half + b], vnew[0:NS, 0, h],
                                            start=True, stop=True)
                last.then_inc(s.pe_e, 1)

        @block.gpsimd
        def _(pool):
            for h in range(H):
                if h >= 2:
                    pool.wait_ge(s.pe_e, 2 * (h - 1))
                nc.gpsimd.tensor_tensor(kdm[:, h % 2], bc(row(krow, 4)[:, h], 1, NB), bc(table(g, "own", NS), 2, HD), ALU.mult
                                        ).then_inc(s.pool_a, 1)

        @block.scalar
        def _(act):
            for n in range(TILES):
                act.wait_ge(s.pe_a, n + 1)
                r = ROWS[n]
                nc.scalar.mul(wT[:, n * 512:n * 512 + H * r], g.ps[:, n % 2, 0:H * r], -1.0).then_inc(s.act_a, 1)
            for n in range(4):
                act.wait_ge(s.pe_b, n + 1)
                if n >= 2:
                    act.wait_ge(s.pe_d, n - 1)
                nc.scalar.copy(vnew[:, n % 2], bank(2, P, HD)).then_inc(s.act_b, 1)
                act.wait_ge(s.pe_d, n + 1)
                nc.scalar.copy(g.oa[:, :, cols(n)], bank(3, P, P)).then_inc(s.act_c, 1)
            act.wait_ge(s.pe_b, 5)
            nc.scalar.copy(ws, bank(5, P, NS)).then_inc(s.act_b, 1)
            act.wait_ge(s.pe_b, 6)
            nc.scalar.copy(vnew[0:NS, 0], bank(6, NS, HD)).then_inc(s.act_b, 1)
            act.wait_ge(s.pe_d, 5)
            nc.scalar.copy(g.oa[:, :, cols(4)], bank(7, P, NS)).then_inc(s.act_c, 1)

        @block.vector
        def _(dve):
            link = Link(dve, s.link_dve)
            nc.vector.memset(state, 0.0).then_inc(s.filled, 1)
            for n in range(4):
                dve.wait_ge(s.pe_c, n + 1)
                dve.wait_ge(s.pe_d, n + 1)
                dve.wait_ge(s.filled, 1)
                link(nc.vector.tensor_tensor(state, state, bc(lastg[:, 4 * n:4 * n + 4], 2, HD), ALU.mult))
                nc.vector.tensor_tensor(state, state, bank(4, P, HD), ALU.add).then_inc(s.dve_b, 1)
                dve.wait_ge(s.dve_b, n + 1)
            dve.wait_ge(s.pe_d, 5)
            for u in range(2 * H):
                h, half = u // 2, u % 2
                part = st[:, h, 4 * half:4 * half + 4]
                k = 16 + h * NB + 4 * half
                link(nc.vector.tensor_tensor(part, part, bc(lastg[:, k:k + 4], 2, HD), ALU.mult))
                dve.wait_ge(s.pe_e, u + 1)
                nc.vector.tensor_tensor(part, part, g.ps[:, u % 2, :].rearrange("p (b e) -> p b e", b=4), ALU.add).then_inc(s.dve_c, 1)
    clear_semaphores(nc, g)

    sq, rn = dec[:].rearrange("p (h c) -> p h c", h=H), lowm[:].rearrange("p (h c) -> p h c", h=H)
    with nc.Block() as block:
        @block.scalar
        def _(act):
            nc.scalar.activation(sq, g.oa[:], ACT.Square).then_inc(s.act_a, 1)
            nc.scalar.activation(zT[:], zT[:], ACT.Silu).then_inc(s.act_b, 1)
            act.wait_ge(s.dve_a, 1)
            nc.scalar.activation(rn, rn, ACT.Sqrt).then_inc(s.act_c, 1)

        @block.tensor
        def _(pe):
            pe.wait_ge(s.act_a, 1)
            for h in range(H):
                nc.tensor.matmul(g.ps[:, h, :], g.ones[:], sq[:, h, 0:SEQ], start=True, stop=True)
                last = nc.tensor.matmul(g.ps[:, 4, h * NS:(h + 1) * NS], g.ones[:], sq[:, h, SEQ:TOK], start=True, stop=True)
            last.then_inc(s.pe_a, 1)

        @block.vector
        def _(dve):
            link = Link(dve, s.link_dve)
            dve.wait_ge(s.pe_a, 1)
            link(nc.vector.tensor_scalar(rn[:, :, 0:SEQ], g.ps[:, 0:4, :], 1.0 / HD, EPS, ALU.mult, ALU.add))
            link(nc.vector.tensor_scalar(rn[:, :, SEQ:TOK], bank(4, P, NS), 1.0 / HD, EPS, ALU.mult, ALU.add))
            nc.vector.reciprocal(rn, rn).then_inc(s.dve_a, 1)
            dve.wait_ge(s.act_b, 1)
            link(nc.vector.tensor_tensor(g.oa[:], g.oa[:], zT[:], ALU.mult))
            dve.wait_ge(s.act_c, 1)
            link(nc.vector.scalar_tensor_tensor(out=g.oa[:], in0=g.oa[:], scalar=vecs[:, 60:61], in1=rn, op0=ALU.mult, op1=ALU.mult))
            nc.vector.tensor_copy(g.pscale[:], vecs[:, 48:60]).then_inc(s.dve_b, 1)
    clear_semaphores(nc, g)


def window_stage(nc, g, t, o, l):
    s = g.s
    w_in = layer(t["w_in"], l)
    with ExitStack() as ctx:
        sb = lambda name, shape, c=ctx: c.enter_context(nc.sbuf_tensor(fresh(name), shape, F32))
        vals = sb("vals", [P, TILES, SW])
        qkT = sb("qkT", [P, 12, TOK])
        with ExitStack() as inner:
            window_in(nc, g, t, o, l, w_in, vals, qkT, lambda n, sh: sb(n, sh, inner))
        clear_semaphores(nc, g)
        with ExitStack() as inner:
            window_prompt(nc, g, vals, qkT, lambda n, sh: sb(n, sh, inner))
        clear_semaphores(nc, g)
        with ExitStack() as inner:
            window_samples(nc, g, t, l, vals, qkT, lambda n, sh: sb(n, sh, inner))
        clear_semaphores(nc, g)


WB = 384


def window_in(nc, g, t, o, l, w_in, vals, qkT, sb):
    s = g.s
    ring = sb("ring", [P, 2, KT * WB])
    qk = sb("qk", [P, TILES, 2 * SW])
    tmp = sb("tmp", [P, 2, 4 * 24 * 32])
    half = lambda n, i: qk[0:ROWS[n], n, :].rearrange("p (h a d) -> p h a d", h=24, a=2)[:, :, i]
    trig = lambda name, n: bc(table(g, name, ROWS[n])[:, n * 32:(n + 1) * 32], 1, 24)
    work = lambda n, i: tmp[0:ROWS[n], n % 2, i * 768:(i + 1) * 768].rearrange("p (h d) -> p h d", h=24)
    heads2 = lambda ap: ap.rearrange("b t v h d -> b t v (h d)")

    def store_rows(eng, kv):
        count = 0
        for i in range(3):
            src = lambda n: (qk[0:ROWS[n], n, SW + i * 256:SW + (i + 1) * 256], vals[0:ROWS[n], n, i * 256:(i + 1) * 256])[kv]
            for n in range(3 if i == 0 else 0, 4):
                at = n * P if i else 0
                eng.dma_start(heads2(layer(o[f"win{i}_p"], l))[0, at:at + P, kv], src(n)).then_inc(s.stored, 16)
                count += 16
            keep = min(GROUPS[i][0], PAST + NT)
            eng.dma_start(heads2(layer(o[f"win{i}_s"], l))[:, keep - NT:keep, kv], src(4)).then_inc(s.stored, 16)
            count += 16
        return 2 * count

    with nc.Block() as block:
        @block.sync
        def _(sp):
            load_slabs(sp, g, ring, [rows_of(w_in)[:, :, C_B + i * WB:C_B + (i + 1) * WB] for i in range(6)])
            sp.wait_ge(s.dve_a, 2 * TILES)
            sp.wait_ge(s.stored, store_rows(sp, 0))

        @block.gpsimd
        def _(pool):
            for i in range(3):
                src, dst = heads2(layer(t[f"cache_win{i}"], l)), heads2(layer(o[f"win{i}_s"], l))
                keep = min(GROUPS[i][0], PAST + NT)
                drop = src.shape[1] + NT - keep
                pool.dma_start(dst[:, 0:keep - NT], src[:, drop:]).then_inc(s.stored2, 16)
            for n in range(TILES):
                r = ROWS[n]
                pool.wait_ge(s.act_b, 3 * TILES + n + 1)
                if n >= 2:
                    pool.wait_ge(s.dve_a, 2 * (n - 1))
                nc.gpsimd.tensor_tensor(work(n, 2), half(n, 1), trig("sin", n), ALU.mult).then_inc(s.pool_a, 1)
                nc.gpsimd.tensor_tensor(work(n, 3), half(n, 1), trig("cos", n), ALU.mult).then_inc(s.pool_a, 1)
            pool.wait_ge(s.stored2, (l + 1) * 48)
            pool.sem_inc(s.paced, 1)

        @block.tensor
        def _(pe):
            for i in range(6):
                slab_ready(pe, g, i)
                w = slab_view(ring, i, KT, WB)
                for n in range(TILES):
                    u = i * TILES + n
                    if u >= 4:
                        pe.wait_ge(s.act_b, u - 3)
                    for k in range(KT):
                        last = nc.tensor.matmul(g.ps[0:ROWS[n], u % 4, 0:WB], g.hT[:, k, cols(n)], w[:, k, :],
                                                start=k == 0, stop=k == KT - 1)
                    last.then_inc(s.pe_a, 1)
                    if i == 5:
                        pe.wait_ge(s.dve_a, 2 * n + 2)
                        for j in range(3):
                            v = 3 * n + j
                            if v >= 4:
                                pe.wait_ge(s.act_c, v - 3)
                            for c in range(4):
                                k = 4 * j + c
                                last = nc.tensor.transpose(g.ps[:, 4 + v % 4, c * P:c * P + ROWS[n]], qk[0:ROWS[n], n, k * P:(k + 1) * P],
                                                           ident(g, ROWS[n]))
                            last.then_inc(s.pe_b, 1)
                if i < 5:
                    pe.wait_ge(s.pe_a, (i + 1) * TILES)
                    pe.sem_inc(s.slab_free, 1)

        @block.scalar
        def _(act):
            for i in range(6):
                for n in range(TILES):
                    u, r = i * TILES + n, ROWS[n]
                    act.wait_ge(s.pe_a, u + 1)
                    dst = qk[0:r, n, i * WB:(i + 1) * WB] if i < 4 else vals[0:r, n, (i - 4) * WB:(i - 3) * WB]
                    nc.scalar.copy(dst, g.ps[0:r, u % 4, 0:WB]).then_inc(s.act_b, 1)
                    for j in range(3 if i == 5 else 0):
                        v = 3 * n + j
                        act.wait_ge(s.pe_b, v + 1)
                        nc.scalar.copy(qkT[:, 4 * j:4 * j + 4, cols(n)],
                                       g.ps[:, 4 + v % 4, :].rearrange("p (k c) -> p k c", k=4)[:, :, 0:ROWS[n]]).then_inc(s.act_c, 1)
            act.wait_ge(s.act_b, 6 * TILES)
            act.wait_ge(s.stored, store_rows(act, 1))

        @block.vector
        def _(dve):
            link = Link(dve, s.link_dve)
            for n in range(TILES):
                dve.wait_ge(s.act_b, 3 * TILES + n + 1)
                link(nc.vector.tensor_tensor(work(n, 0), half(n, 0), trig("cos", n), ALU.mult))
                link(nc.vector.tensor_tensor(work(n, 1), half(n, 0), trig("sin", n), ALU.mult))
                dve.wait_ge(s.pool_a, 2 * n + 2)
                nc.vector.tensor_tensor(half(n, 0), work(n, 0), work(n, 2), ALU.subtract).then_inc(s.dve_a, 1)
                nc.vector.tensor_tensor(half(n, 1), work(n, 1), work(n, 3), ALU.add).then_inc(s.dve_a, 1)


SEG = (0, 256, 768, 1280)
LEN_S = (128, 256, 256)


def window_prompt(nc, g, vals, qkT, sb):
    s = g.s
    sc, pT = sb("sc", [P, 2, 1280]), sb("pT", [P, 2, 10, P])
    stat = sb("stat", [P, 2, 4])
    units = [(n, h) for n in range(4) for h in range(SLOTS)]
    qT = lambda n, i, h: qkT[(h % 2) * SD:(h % 2 + 1) * SD, 2 * i + h // 2, cols(n)]
    kTt = lambda m0, m1, i, h: qkT[(h % 2) * SD:(h % 2 + 1) * SD, 6 + 2 * i + h // 2, m0 * P:m1 * P]

    def segments(n):
        out, at = [], 0
        for i in range(3):
            m0 = max(0, n - 1) if i == 0 else 0
            w = (n + 1 - m0) * P
            out.append((i, m0, n + 1 - m0, at, SEG[i + 1] - w))
            at += w
        return out, at

    mask = table(g, "amask")
    with nc.Block() as block:
        @block.tensor
        def _(pe):
            quad = [0]

            def scores(u):
                n, h = units[u]
                if u >= 1:
                    pe.wait_ge(s.dve_a, u)
                for i, m0, m, at, _ in segments(n)[0]:
                    last = nc.tensor.matmul(g.ps[:, i, 0:m * P], qT(n, i, h), kTt(m0, m0 + m, i, h), start=True, stop=True)
                last.then_inc(s.pe_a, 1)

            def weigh(u):
                n, h = units[u]
                tiles = [(i, m0 + j) for i, m0, m, _, _ in segments(n)[0] for j in range(m)]
                pe.wait_ge(s.dve_b, u + 1)
                for q in range(0, len(tiles), 4):
                    if quad[0] >= 2:
                        pe.wait_ge(s.act_b, quad[0] - 1)
                    for j in range(q, min(q + 4, len(tiles))):
                        last = nc.tensor.transpose(g.ps[:, 3 + quad[0] % 2, (j - q) * P:(j - q + 1) * P],
                                                   sc[:, u % 2, j * P:(j + 1) * P], ident(g))
                    last.then_inc(s.pe_b, 1)
                    quad[0] += 1
                if u + 2 < len(units):
                    scores(u + 2)
                pe.wait_ge(s.act_b, quad[0])
                if u >= 2:
                    pe.wait_ge(s.dve_c, u - 1)
                r = (h % 2) * SD
                for j, (i, m) in enumerate(tiles):
                    last = nc.tensor.matmul(g.ps[r:r + SD, 5 + u % 2, 0:P], vals[:, m, i * 256 + h * SD:i * 256 + (h + 1) * SD],
                                            pT[:, u % 2, j, :], start=j == 0, stop=j == len(tiles) - 1)
                last.then_inc(s.pe_c, 1)

            scores(0)
            scores(1)
            for u in range(len(units)):
                weigh(u)

        @block.scalar
        def _(act):
            quad = 0

            def exps(u):
                n, h = units[u]
                w = segments(n)[1]
                act.wait_ge(s.dve_d, u + 1)
                nc.scalar.activation(sc[:, u % 2, 0:w], sc[:, u % 2, 0:w], ACT.Exp, bias=stat[:, u % 2, 1:2], scale=SD ** -0.5,
                                     accum_out=stat[:, u % 2, 2:3]).then_inc(s.act_a, 1)

            exps(0)
            for u in range(len(units)):
                n, h = units[u]
                if u + 1 < len(units):
                    exps(u + 1)
                count = segments(n)[1] // P
                if u >= 2:
                    act.wait_ge(s.pe_c, u - 1)
                for q in range(0, count, 4):
                    m = min(4, count - q)
                    act.wait_ge(s.pe_b, quad + 1)
                    nc.scalar.copy(pT[:, u % 2, q:q + m, :], g.ps[:, 3 + quad % 2, 0:m * P].rearrange("p (k c) -> p k c", k=m)
                                   ).then_inc(s.act_b, 1)
                    quad += 1

        @block.vector
        def _(dve):
            link = Link(dve, s.link_dve)

            def first(u):
                n, h = units[u]
                seg, w = segments(n)
                dve.wait_ge(s.pe_a, u + 1)
                if u >= 2:
                    dve.wait_ge(s.pe_c, u - 1)
                for i, m0, m, at, mk in seg:
                    last = nc.vector.tensor_tensor(sc[:, u % 2, at:at + m * P], g.ps[:, i, 0:m * P], mask[:, mk:mk + m * P], ALU.add)
                    if i < 2:
                        link(last)
                last.then_inc(s.dve_a, 1)
                dve.wait_ge(s.dve_a, u + 1)
                link(nc.vector.reduce_max(stat[:, u % 2, 0:1], sc[:, u % 2, 0:w], AX.X))
                nc.vector.tensor_scalar(stat[:, u % 2, 1:2], stat[:, u % 2, 0:1], -SD ** -0.5, None, ALU.mult).then_inc(s.dve_d, 1)

            first(0)
            for u in range(len(units)):
                n, h = units[u]
                w = segments(n)[1]
                if u + 1 < len(units):
                    first(u + 1)
                dve.wait_ge(s.act_a, u + 1)
                link(nc.vector.reciprocal(stat[:, u % 2, 3:4], stat[:, u % 2, 2:3]))
                nc.vector.tensor_scalar(sc[:, u % 2, 0:w], sc[:, u % 2, 0:w], stat[:, u % 2, 3:4], None, ALU.mult).then_inc(s.dve_b, 1)
                dve.wait_ge(s.pe_c, u + 1)
                r = (h % 2) * SD
                nc.vector.tensor_copy(g.ob[r:r + SD, h // 2, cols(n)], g.ps[r:r + SD, 5 + u % 2, 0:P]).then_inc(s.dve_c, 1)


RING = 4


def window_samples(nc, g, t, l, vals, qkT, sb):
    s = g.s
    kc, vc = sb("kc", [P, RING, 5, 256]), sb("vc", [P, NB, 5, 256])
    kTc = sb("kTc", [P, 2, 10, P])
    apart = sb("apart", [P, 6, NB, 2, NT])
    sT = sb("sT", [P, 20, NS])
    sc, pT, stat = sb("sc", [NS, 2, 832]), sb("pT", [P, 2, 8, NS]), sb("stat", [NS, 2, 4])
    tiles = [(0, 0), (1, 0), (1, 1), (2, 0), (2, 1)]
    q_s = lambda i, h: qkT[(h % 2) * SD:(h % 2 + 1) * SD, 2 * i + h // 2, SEQ:TOK]
    k_s = lambda i, h: qkT[(h % 2) * SD:(h % 2 + 1) * SD, 6 + 2 * i + h // 2, SEQ:TOK]
    caches = [layer(t[f"cache_win{i}"], l).rearrange("b t v h d -> b t v (h d)") for i in range(3)]
    key_rows = (s.slab0, s.slab1, s.map0, s.map1)
    mask = table(g, "smask", NS)
    with nc.Block() as block:
        @block.sync
        def _(sp):
            for b in range(NB):
                if b >= RING:
                    sp.wait_ge(s.act_a, 3 * (b - RING + 1))
                for i, (j0, j1) in enumerate(((0, 1), (1, 3), (3, 5))):
                    sp.dma_start(kc[:, b % RING, j0:j1], caches[i][b, 0:(j1 - j0) * P, 0].rearrange("(m p) c -> p m c", p=P)
                                 ).then_inc(key_rows[b % RING], 16)
            for j, (i, m) in enumerate(tiles):
                sp.dma_start(vc[:, :, j], caches[i][:, m * P:(m + 1) * P, 1].rearrange("b p c -> p b c")).then_inc(s.loaded2, 16)

        @block.tensor
        def _(pe):
            def keys(b):
                pe.wait_ge(key_rows[b % RING], 48 * (b // RING + 1))
                for q in range(3):
                    if b:
                        pe.wait_ge(s.act_a, 3 * (b - 1) + q + 1)
                    for e in range(4 * q, min(4 * q + 4, 10)):
                        j, pair = e // 2, e % 2
                        last = nc.tensor.transpose(g.ps[:, q, (e % 4) * P:(e % 4 + 1) * P], kc[:, b % RING, j, pair * P:(pair + 1) * P], ident(g))
                    last.then_inc(s.pe_a, 1)

            def cached_scores(b):
                pe.wait_ge(s.act_a, 3 * b + 3)
                pe.wait_ge(s.copied, 2)
                if b >= 2:
                    pe.wait_ge(s.dve_a, b - 1)
                for j, (i, m) in enumerate(tiles):
                    for pair in range(2):
                        last = nc.tensor.matmul(g.ps[:, 3 + b % 2, (2 * j + pair) * 2 * NT:(2 * j + pair + 1) * 2 * NT],
                                                kTc[:, b % 2, 2 * j + pair, :], apart[:, 2 * i + pair, b].rearrange("p a t -> p (a t)"),
                                                start=True, stop=True)
                last.then_inc(s.pe_b, 1)

            def rows(h):
                if h >= 2:
                    pe.wait_ge(s.dve_b, h - 1)
                first = 5 - 2 * (h % 2)
                for j in range(5):
                    bank, c = (first, j * P) if j < 4 else (first + 1, 0)
                    nc.tensor.transpose(g.ps[0:NS, bank, c:c + P], sT[:, 4 * j + h, :], ident(g))
                for i in range(3):
                    last = nc.tensor.matmul(g.ps[0:NS, first + 1, P + i * NS:P + (i + 1) * NS], q_s(i, h), k_s(i, h), start=True, stop=True)
                last.then_inc(s.pe_c, 1)

            keys(0)
            for b in range(NB):
                if b + 1 < NB:
                    keys(b + 1)
                cached_scores(b)
            pe.wait_ge(s.dve_a, NB)
            pe.wait_ge(s.act_a, 3 * NB)
            rows(0)
            for h in range(SLOTS):
                if h + 1 < SLOTS:
                    rows(h + 1)
                pe.wait_ge(s.dve_d, h + 1)
                if h:
                    pe.wait_ge(s.act_c, h)
                for j in range(5):
                    nc.tensor.transpose(g.ps[:, 0, j * NS:(j + 1) * NS], sc[:, h % 2, j * P:(j + 1) * P], ident(g, NS))
                for i in range(3):
                    last = nc.tensor.transpose(g.ps[0:NS, 0, (5 + i) * NS:(6 + i) * NS], sc[:, h % 2, 640 + i * NS:640 + (i + 1) * NS],
                                               ident(g, NS))
                last.then_inc(s.pe_d, 1)
                pe.wait_ge(s.act_c, h + 1)
                if h == 0:
                    pe.wait_ge(s.loaded2, 16 * 5)
                r = (h % 2) * SD
                if h >= 2:
                    pe.wait_ge(s.dve_c, h - 1)
                for i in range(3):
                    nc.tensor.matmul(g.ps[r:r + SD, 1 + h % 2, 0:NS], vals[0:NS, 4, i * 256 + h * SD:i * 256 + (h + 1) * SD],
                                     pT[0:NS, h % 2, 5 + i, :], start=i == 0, stop=False)
                for b in range(NB):
                    for j in range(5):
                        last = nc.tensor.matmul(g.ps[r:r + SD, 1 + h % 2, b * NT:(b + 1) * NT], vc[:, b, j, h * SD:(h + 1) * SD],
                                                pT[:, h % 2, j, b * NT:(b + 1) * NT], start=False, stop=j == 4 and b == NB - 1)
                last.then_inc(s.pe_e, 1)

        @block.scalar
        def _(act):
            for b in range(NB):
                for q in range(3):
                    act.wait_ge(s.pe_a, 3 * b + q + 1)
                    if b >= 2:
                        act.wait_ge(s.pe_b, b - 1)
                    m = min(4, 10 - 4 * q)
                    nc.scalar.copy(kTc[:, b % 2, 4 * q:4 * q + m, :], g.ps[:, q, 0:m * P].rearrange("p (k c) -> p k c", k=m)
                                   ).then_inc(s.act_a, 1)
            def exps(h):
                act.wait_ge(s.dve_e, h + 1)
                nc.scalar.activation(sc[:, h % 2], sc[:, h % 2], ACT.Exp, bias=stat[:, h % 2, 1:2], scale=SD ** -0.5,
                                     accum_out=stat[:, h % 2, 2:3]).then_inc(s.act_b, 1)

            exps(0)
            for h in range(SLOTS):
                if h + 1 < SLOTS:
                    exps(h + 1)
                act.wait_ge(s.pe_d, h + 1)
                if h >= 2:
                    act.wait_ge(s.pe_e, h - 1)
                nc.scalar.copy(pT[:, h % 2, 0:5], g.ps[:, 0, 0:5 * NS].rearrange("p (k c) -> p k c", k=5)).then_inc(s.link_act, 1)
                nc.scalar.copy(pT[0:NS, h % 2, 5:8], g.ps[0:NS, 0, 5 * NS:8 * NS].rearrange("p (k c) -> p k c", k=3)
                               ).then_inc(s.act_c, 1)

        @block.vector
        def _(dve):
            link = Link(dve, s.link_dve)
            nc.vector.memset(apart[:], 0.0).then_inc(s.filled, 1)
            dve.wait_ge(s.filled, 1)
            for a in range(2):
                rows = slice(a * SD, (a + 1) * SD)
                nc.vector.tensor_copy(apart[rows, :, :, a], qkT[rows, 0:6, SEQ:TOK].rearrange("p c (b t) -> p c b t", b=NB)).then_inc(s.copied, 1)
            for b in range(NB):
                dve.wait_ge(s.pe_b, b + 1)
                nc.vector.tensor_copy(sT[:, :, b * NT:(b + 1) * NT], g.ps[:, 3 + b % 2, 0:20 * NT].rearrange("p (e c) -> p e c", e=20)
                                      ).then_inc(s.dve_a, 1)

            def first(h):
                dve.wait_ge(s.pe_c, h + 1)
                if h >= 2:
                    dve.wait_ge(s.pe_d, h - 1)
                bank = 5 - 2 * (h % 2)
                link(nc.vector.tensor_tensor(sc[:, h % 2, 0:512], g.ps[0:NS, bank, :], mask[:, 0:512], ALU.add))
                nc.vector.tensor_tensor(sc[:, h % 2, 512:832], g.ps[0:NS, bank + 1, 0:320], mask[:, 512:832], ALU.add).then_inc(s.dve_b, 1)
                dve.wait_ge(s.dve_b, h + 1)
                link(nc.vector.reduce_max(stat[:, h % 2, 0:1], sc[:, h % 2], AX.X))
                nc.vector.tensor_scalar(stat[:, h % 2, 1:2], stat[:, h % 2, 0:1], -SD ** -0.5, None, ALU.mult).then_inc(s.dve_e, 1)

            first(0)
            for h in range(SLOTS):
                if h + 1 < SLOTS:
                    first(h + 1)
                dve.wait_ge(s.act_b, h + 1)
                link(nc.vector.reciprocal(stat[:, h % 2, 3:4], stat[:, h % 2, 2:3]))
                nc.vector.tensor_scalar(sc[:, h % 2], sc[:, h % 2], stat[:, h % 2, 3:4], None, ALU.mult).then_inc(s.dve_d, 1)
                dve.wait_ge(s.pe_e, h + 1)
                r = (h % 2) * SD
                nc.vector.tensor_copy(g.ob[r:r + SD, h // 2, SEQ:TOK], g.ps[r:r + SD, 1 + h % 2, 0:NS]).then_inc(s.dve_c, 1)


UP = PBUF + SEQ
US = PBUF + NT
UW = UP + NB * US


def pool_stage(nc, g, t, o, l, oc):
    s = g.s
    w_in = layer(t["w_in"], l)
    with ExitStack() as ctx:
        sb = lambda name, shape: ctx.enter_context(nc.sbuf_tensor(fresh(name), shape, F32))
        ring, wp = sb("ring", [P, 2, 4096]), sb("wp", [P, 2, 3, PG])
        ext, sums, spare = sb("ext", [P, 2, 3, UW]), sb("sums", [P, 3, UW]), sb("spare", [P, 3, UW])
        diff = sb("diff", [P, 2, 3, TOK])
        old, tail = sb("old", [NB * PBUF, PW]), sb("tail", [P, 3, PBUF + NS])
        new = sb("new", [PBUF + NS, PW])
        smp = lambda i, c: ext[:, i, c, UP:UW].rearrange("p (b j) -> p b j", b=NB)
        pool_p, pool_s = layer(o["pool_p"], l), layer(o["pool_s"], l)
        G = len(POOLS)
        with nc.Block() as block:
            @block.sync
            def _(sp):
                sp.dma_start(old[:], layer(t["state_pool"], l).rearrange("b j c -> (b j) c")).then_inc(s.loaded, 16)
                sp.dma_start(pool_s[:, 0:PBUF - NT], layer(t["state_pool"], l)[:, NT:PBUF]).then_inc(s.stored, 16)
                load_slabs(sp, g, ring, [rows_of(w_in)[:, :, C_U + i * 512:C_U + (i + 1) * 512] for i in range(3)])
                for gi in range(G):
                    if gi >= 2:
                        sp.wait_ge(s.pe_d, 3 * (gi - 1))
                    sp.dma_start(wp[:, gi % 2], rows_of(layer(t["w_pool"], l)[gi])).then_inc((s.map0, s.map1)[gi % 2], 16)
                sp.wait_ge(s.act_c, G)
                sp.dma_start(pool_p[0], new[0:PBUF]).then_inc(s.stored, 16)
                for b in range(NB):
                    sp.dma_start(pool_s[b, PBUF - NT:], new[PBUF + b * NT:PBUF + (b + 1) * NT]).then_inc(s.stored, 16)
                sp.wait_ge(s.stored, 16 * (2 + NB))

            @block.gpsimd
            def _(pool):
                for i in range(2):
                    nc.gpsimd.memset(ext[:, i, :, 0:PBUF], 0.0).then_inc(s.filled, 1)

            @block.tensor
            def _(pe):
                def maps(gi):
                    pe.wait_ge((s.map0, s.map1)[gi % 2], 16 * (gi // 2 + 1))
                    pe.wait_ge(s.dve_c, gi + 1)
                    for c in range(3):
                        u = 3 * gi + c
                        if u:
                            pe.wait_ge(s.act_d, 2 * u)
                        for k in range(3):
                            nc.tensor.matmul(g.ps[:, 6, :], wp[:, gi % 2, k, c * P:(c + 1) * P], diff[:, gi % 2, k, 0:SEQ],
                                             start=k == 0, stop=k == 2)
                            last = nc.tensor.matmul(g.ps[:, 7, 0:NS], wp[:, gi % 2, k, c * P:(c + 1) * P], diff[:, gi % 2, k, SEQ:TOK],
                                                    start=k == 0, stop=k == 2)
                        last.then_inc(s.pe_d, 1)

                pe.wait_ge(s.loaded, 16)
                for gi in range(G):
                    if gi:
                        pe.wait_ge(s.dve_b, gi)
                    for c in range(3):
                        last = nc.tensor.transpose(g.ps[:, 5, c * 120:(c + 1) * 120], old[:, (3 * gi + c) * P:(3 * gi + c + 1) * P],
                                                   ident(g, 120))
                    last.then_inc(s.pe_b, 1)
                    for u in range(3 * gi, 3 * gi + 3):
                        if u % 4 == 0:
                            slab_ready(pe, g, u // 4)
                        w = slab_view(ring, u // 4, KT, 512)
                        project(nc, g, pe, u, lambda k: w[:, k, (u % 4) * P:(u % 4 + 1) * P], lambda k: g.hT[:, k, :], KT,
                                s.pe_a, s.act_a, s.dve_a)
                        if u % 4 == 3:
                            pe.wait_ge(s.pe_a, u + 1)
                            pe.sem_inc(s.slab_free, 1)
                    pe.wait_ge(s.dve_b, gi + 1)
                    for c in range(3):
                        last = nc.tensor.transpose(g.ps[0:PBUF + NS, 5, c * P:(c + 1) * P], tail[:, c, :], ident(g))
                    last.then_inc(s.pe_c, 1)
                    pe.wait_ge(s.act_c, gi + 1)
                    if gi:
                        maps(gi - 1)
                maps(G - 1)

            @block.scalar
            def _(act):
                def scale(gi):
                    for c in range(3):
                        u = 3 * gi + c
                        act.wait_ge(s.pe_d, u + 1)
                        nc.scalar.mul(oc[:, u, 0:SEQ], g.ps[:, 6, :], g.pscale[:, u:u + 1]).then_inc(s.act_d, 1)
                        nc.scalar.mul(oc[:, u, SEQ:TOK], g.ps[:, 7, 0:NS], g.pscale[:, u:u + 1]).then_inc(s.act_d, 1)

                for gi in range(G):
                    if gi >= 2:
                        act.wait_ge(s.dve_c, gi - 1)
                    for u in range(3 * gi, 3 * gi + 3):
                        act.wait_ge(s.pe_a, u + 1)
                        nc.scalar.copy(ext[:, gi % 2, u % 3, PBUF:PBUF + HALF], part_a(g, u)).then_inc(s.act_a, 1)
                    act.wait_ge(s.pe_c, gi + 1)
                    nc.scalar.copy(new[:, gi * PG:(gi + 1) * PG], g.ps[0:PBUF + NS, 5, 0:PG]).then_inc(s.act_c, 1)
                    if gi:
                        scale(gi - 1)
                scale(G - 1)

            @block.vector
            def _(dve):
                link = Link(dve, s.link_dve)
                for gi, w in enumerate(POOLS):
                    i = gi % 2
                    e = ext[:, i]
                    dve.wait_ge(s.pe_b, gi + 1)
                    for c in range(3):
                        link(nc.vector.tensor_copy(smp(i, c)[:, :, 0:PBUF],
                                                   g.ps[:, 5, c * 120:(c + 1) * 120].rearrange("p (b j) -> p b j", b=NB)))
                    for u in range(3 * gi, 3 * gi + 3):
                        dve.wait_ge(s.pe_a, u + 1)
                        nc.vector.tensor_copy(ext[:, i, u % 3, PBUF + HALF:UP], part_b_prompt(g, u)).then_inc(s.dve_a, 1)
                        nc.vector.tensor_copy(smp(i, u % 3)[:, :, PBUF:], part_b_samples(g, u)).then_inc(s.dve_a, 1)
                    dve.wait_ge(s.act_a, 3 * gi + 3)
                    dve.wait_ge(s.dve_a, 6 * gi + 6)
                    dve.wait_ge(s.filled, 2)
                    for c in range(3):
                        link(nc.vector.tensor_copy(tail[:, c, PBUF:].rearrange("p (b j) -> p b j", b=NB), smp(i, c)[:, :, PBUF:]))
                    nc.vector.tensor_copy(tail[:, :, 0:PBUF], e[:, :, UP - PBUF:UP]).then_inc(s.dve_b, 1)
                    link(nc.vector.tensor_tensor(sums[:, :, 1:UW], e[:, :, 1:UW], e[:, :, 0:UW - 1], ALU.add))
                    src, span = sums, 2
                    while span < w:
                        dst = spare if src is sums else sums
                        link(nc.vector.tensor_tensor(dst[:, :, 2 * span - 1:UW], src[:, :, 2 * span - 1:UW],
                                                     src[:, :, span - 1:UW - span], ALU.add))
                        src, span = dst, 2 * span
                    if gi >= 2:
                        dve.wait_ge(s.pe_d, 3 * (gi - 1))
                    d = diff[:, i]
                    link(nc.vector.scalar_tensor_tensor(out=d[:, :, 0:SEQ], in0=src[:, :, PBUF:UP], scalar=1.0 / w,
                                                        in1=e[:, :, PBUF:UP], op0=ALU.mult, op1=ALU.subtract))
                    o_c, _ = CONST["count"]
                    cnt = g.consts[:, o_c + gi * 16:o_c + (gi + 1) * 16]
                    link(nc.vector.tensor_tensor(d[:, :, 0:16], src[:, :, PBUF:PBUF + 16], bc(cnt, 1, 3), ALU.mult))
                    link(nc.vector.tensor_tensor(d[:, :, 0:16], d[:, :, 0:16], e[:, :, PBUF:PBUF + 16], ALU.subtract))
                    for c in range(3):
                        last = nc.vector.scalar_tensor_tensor(
                            out=d[:, c, SEQ:TOK].rearrange("p (b j) -> p b j", b=NB),
                            in0=src[:, c, UP:UW].rearrange("p (b j) -> p b j", b=NB)[:, :, PBUF:], scalar=1.0 / w,
                            in1=smp(i, c)[:, :, PBUF:], op0=ALU.mult, op1=ALU.subtract)
                        if c < 2:
                            link(last)
                    last.then_inc(s.dve_c, 1)
    clear_semaphores(nc, g)


def merge_stage(nc, g, t, l, oc):
    s = g.s
    w_in, w_b, w_o = rows_of(layer(t["w_in"], l)), rows_of(layer(t["w_branch"], l)), rows_of(layer(t["w_out"], l))
    NW = 3 * KT + 18
    src = [(g.oa, 4, 0), (g.ob, 2, 4), (oc, 12, 6)]
    with ExitStack() as ctx:
        sb = lambda name, shape: ctx.enter_context(nc.sbuf_tensor(fresh(name), shape, F32))
        merged = sb("merged", [P, KT, TOK])
        with ExitStack() as inner:
            sbi = lambda name, shape: inner.enter_context(nc.sbuf_tensor(fresh(name), shape, F32))
            ring = sbi("ring", [P, 2, NW * P])
            gate, term = sbi("gate", [P, 2, TOK]), sbi("term", [P, TOK])
            view = lambda j: ring[:, j % 2].rearrange("p (k c) -> p k c", k=NW)
            slab, first = (s.slab0, s.slab1), (s.map0, s.map1)
            units = [(j, b) for j in range(KT) for b in range(3)]
            with nc.Block() as block:
                @block.sync
                def _(sp):
                    for j in range(KT):
                        if j >= 2:
                            sp.wait_ge(s.pe_b, 3 * (j - 1))
                        for b in range(3):
                            c = C_G + b * D + j * P
                            sp.dma_start(view(j)[:, b * KT:(b + 1) * KT], w_in[:, :, c:c + P]).then_inc((first if b == 0 else slab)[j % 2], 16)
                            if b == 0:
                                sp.dma_start(view(j)[:, 3 * KT:], w_b[:, :, j * P:(j + 1) * P]).then_inc(slab[j % 2], 16)

                @block.tensor
                def _(pe):
                    for u, (j, b) in enumerate(units):
                        if b == 0:
                            pe.wait_ge(first[j % 2], 16 * (j // 2 + 1))
                        w = view(j)
                        if u >= 2:
                            pe.wait_ge(s.act_a, 2 * (u - 1))
                        for k in range(KT):
                            nc.tensor.matmul(g.ps[:, u % 2, 0:HALF], w[:, b * KT + k, :], g.hT[:, k, 0:HALF], start=k == 0, stop=k == KT - 1)
                            last = nc.tensor.matmul(g.ps[:, 4 + u % 2, 0:HALF], w[:, b * KT + k, :], g.hT[:, k, HALF:TOK],
                                                    start=k == 0, stop=k == KT - 1)
                        last.then_inc(s.pe_a, 1)
                        if b == 0:
                            pe.wait_ge(slab[j % 2], 48 * (j // 2 + 1))
                        if u >= 2:
                            pe.wait_ge(s.dve_a, u - 1)
                        out, nk, k0 = src[b]
                        for k in range(nk):
                            nc.tensor.matmul(g.ps[:, 2 + u % 2, 0:HALF], w[:, 3 * KT + k0 + k, :], out[:, k, 0:HALF], start=k == 0, stop=k == nk - 1)
                            last = nc.tensor.matmul(g.ps[:, 6 + u % 2, 0:HALF], w[:, 3 * KT + k0 + k, :], out[:, k, HALF:TOK],
                                                    start=k == 0, stop=k == nk - 1)
                        last.then_inc(s.pe_b, 1)

                @block.scalar
                def _(act):
                    for u, (j, b) in enumerate(units):
                        act.wait_ge(s.pe_a, u + 1)
                        if u >= 2:
                            act.wait_ge(s.dve_a, u - 1)
                        nc.scalar.activation(gate[:, u % 2, 0:HALF], g.ps[:, u % 2, 0:HALF], ACT.Sigmoid).then_inc(s.act_a, 1)
                        nc.scalar.activation(gate[:, u % 2, HALF:TOK], g.ps[:, 4 + u % 2, 0:HALF], ACT.Sigmoid).then_inc(s.act_a, 1)

                @block.vector
                def _(dve):
                    link = Link(dve, s.link_dve)
                    for u, (j, b) in enumerate(units):
                        dve.wait_ge(s.act_a, 2 * u + 2)
                        dve.wait_ge(s.pe_b, u + 1)
                        to = merged[:, j, :] if b == 0 else term[:]
                        nc.vector.tensor_tensor(to[:, 0:HALF], gate[:, u % 2, 0:HALF], g.ps[:, 2 + u % 2, 0:HALF], ALU.mult).then_inc(s.link_dve, 1)
                        link.n += 1
                        nc.vector.tensor_tensor(to[:, HALF:TOK], gate[:, u % 2, HALF:TOK], g.ps[:, 6 + u % 2, 0:HALF], ALU.mult).then_inc(s.dve_a, 1)
                        dve.wait_ge(s.dve_a, u + 1)
                        if b:
                            link(nc.vector.tensor_tensor(merged[:, j, :], merged[:, j, :], term[:], ALU.add))
            clear_semaphores(nc, g)
        with ExitStack() as inner:
            ring = inner.enter_context(nc.sbuf_tensor(fresh("ring"), [P, 2, 4096], F32))
            with nc.Block() as block:
                @block.sync
                def _(sp):
                    load_slabs(sp, g, ring, [w_o[:, :, i * 512:(i + 1) * 512] for i in range(2)])

                @block.tensor
                def _(pe):
                    for i in range(2):
                        slab_ready(pe, g, i)
                        w = slab_view(ring, i, KT, 512)
                        for n in range(TILES):
                            u = i * TILES + n
                            if u >= 4:
                                pe.wait_ge(s.dve_a, u - 3)
                            for k in range(KT):
                                last = nc.tensor.matmul(g.ps[0:ROWS[n], u % 4, :], merged[:, k, cols(n)], w[:, k, :], start=k == 0, stop=k == KT - 1)
                            last.then_inc(s.pe_a, 1)

                @block.vector
                def _(dve):
                    for u in range(2 * TILES):
                        i, n = u // TILES, u % TILES
                        part = g.x[0:ROWS[n], n, i * 512:(i + 1) * 512]
                        dve.wait_ge(s.pe_a, u + 1)
                        nc.vector.tensor_tensor(part, part, g.ps[0:ROWS[n], u % 4, :], ALU.add).then_inc(s.dve_a, 1)
            clear_semaphores(nc, g)


def score_stage(nc, g, t, l, sc, router, ring, w_q):
    s = g.s
    with ExitStack() as ctx:
        with ExitStack() as inner:
            sbi = lambda name, shape: inner.enter_context(nc.sbuf_tensor(fresh(name), shape, F32))
            keys, keysT, qT = sbi("keys", [P, 2, P]), sbi("keysT", [P, 2, P]), sbi("qT", [P, 2, TOK])
            with nc.Block() as block:
                @block.sync
                def _(sp):
                    sp.dma_start(keys[:], layer(t["peer_subkeys"], l).rearrange("s k d -> k s d")).then_inc(s.loaded, 16)
                    load_slabs(sp, g, ring, w_q, ahead=2)

                @block.tensor
                def _(pe):
                    def scores(u):
                        pe.wait_ge(s.act_a, 2 * u + 2)
                        if u:
                            pe.wait_ge(s.scored, 2 * u)
                        for n in range(TILES):
                            last = nc.tensor.matmul(g.ps[0:ROWS[n], 5 + n // 4, (n % 4) * P:(n % 4 + 1) * P], qT[:, u % 2, cols(n)],
                                                    keysT[:, u % 2, :], start=True, stop=True)
                        last.then_inc(s.pe_b, 1)

                    pe.wait_ge(s.loaded, 16)
                    for i in range(2):
                        last = nc.tensor.transpose(g.ps[:, 7, i * P:(i + 1) * P], keys[:, i, :], ident(g))
                    last.then_inc(s.pe_c, 1)
                    pe.wait_ge(s.act_c, 1)
                    for u in range(NQ):
                        if u % 4 == 0:
                            slab_ready(pe, g, u // 4, ahead=2)
                        w = slab_view(ring, u // 4, KT, 512)
                        if u >= BANKS_B:
                            pe.wait_ge(s.act_a, 2 * (u - BANKS_B + 1))
                        for k in range(KT):
                            nc.tensor.matmul(part_a(g, u), w[:, k, (u % 4) * P:(u % 4 + 1) * P], g.hT[:, k, 0:HALF], start=k == 0, stop=k == KT - 1)
                            last = nc.tensor.matmul(part_b(g, u), w[:, k, (u % 4) * P:(u % 4 + 1) * P], g.hT[:, k, HALF:TOK],
                                                    start=k == 0, stop=k == KT - 1)
                        last.then_inc(s.pe_a, 1)
                        if u % 4 == 3:
                            pe.wait_ge(s.pe_a, u + 1)
                            pe.sem_inc(s.slab_free, 1)
                        if u:
                            scores(u - 1)
                    scores(NQ - 1)

                @block.scalar
                def _(act):
                    def scores(u):
                        act.wait_ge(s.pe_b, u + 1)
                        nc.scalar.copy(sc[:, 0:4, u, :], g.ps[:, 5, :].rearrange("p (n k) -> p n k", n=4)).then_inc(s.scored, 1)
                        nc.scalar.copy(sc[0:NS, 4, u, :], g.ps[0:NS, 6, 0:P]).then_inc(s.scored, 1)

                    act.wait_ge(s.pe_c, 1)
                    nc.scalar.copy(keysT[:], g.ps[:, 7, 0:2 * P].rearrange("p (i k) -> p i k", i=2)).then_inc(s.act_c, 1)
                    for u in range(NQ):
                        act.wait_ge(s.pe_a, u + 1)
                        if u >= 2:
                            act.wait_ge(s.pe_b, u - 1)
                        nc.scalar.copy(qT[:, u % 2, 0:HALF], part_a(g, u)).then_inc(s.act_a, 1)
                        nc.scalar.copy(qT[:, u % 2, HALF:TOK], part_b(g, u)).then_inc(s.act_a, 1)
                        if u:
                            scores(u - 1)
                    scores(NQ - 1)
                    router.gate_exp(act, 0, 1)

                @block.vector
                def _(dve):
                    link = Link(dve, s.link_dve)
                    for h in range(PH):
                        dve.wait_ge(s.scored, 4 * h + 4)
                        router.head(link, 0, h)
                    router.finish(dve, link, 0, 1)
            clear_semaphores(nc, g)


class Router:

    def __init__(self, nc, g, sb, sc, ids, gates):
        self.nc, self.g, self.sc, self.ids, self.gates = nc, g, sc, ids, gates
        self.top, self.at = sb("top", [P, 2, TOPK]), sb("at", [P, 2, TOPK], U32)
        self.atf, self.best = sb("atf", [P, 2, TOPK]), sb("best", [P, PH, TOPK])
        self.pos, self.two = sb("pos", [P, TOPK], U32), sb("two", [P, 2, TOPK], U32)
        self.twof, self.num, self.den = sb("twof", [P, 2, TOPK]), sb("num", [P, PH, 2, TOPK]), sb("den", [P, 2, PH])
        self.cand, self.pick = sb("cand", [P, TOPK * TOPK]), sb("pick", [P, 2, TOPK, TOPK])

    def top16(self, link, values, index, data):
        v = self.nc.vector
        link(v.max(values[:, 0:8], data))
        link(v.max_index(index[:, 0:8], values[:, 0:8], data))
        link(v.match_replace(data, values[:, 0:8], data, -3.0e38))
        link(v.max(values[:, 8:16], data))
        link(v.max_index(index[:, 8:16], values[:, 8:16], data))

    def head(self, link, n, h):
        r, v, g = ROWS[n], self.nc.vector, self.g
        for a in range(2):
            self.top16(link, self.top[0:r, a], self.at[0:r, a], self.sc[0:r, n, 2 * h + a, :])
        link(v.tensor_tensor(self.cand[0:r].rearrange("p (a b) -> p a b", a=TOPK), bc(self.top[0:r, 0], 2, TOPK),
                             bc(self.top[0:r, 1], 1, TOPK), ALU.add))
        self.top16(link, self.best[0:r, h], self.pos[0:r], self.cand[0:r])
        link(v.tensor_single_scalar(self.two[0:r, 0], self.pos[0:r], 4, op=ALU.logical_shift_right))
        link(v.tensor_single_scalar(self.two[0:r, 1], self.pos[0:r], 15, op=ALU.bitwise_and))
        link(v.tensor_copy(self.twof[0:r], self.two[0:r]))
        link(v.tensor_copy(self.atf[0:r], self.at[0:r]))
        iota = table(g, "iota", r).unsqueeze(1).unsqueeze(1).broadcast_to([r, 2, TOPK, TOPK])
        link(v.tensor_tensor(self.pick[0:r], iota, bc(self.twof[0:r], 3, TOPK), ALU.is_equal))
        link(v.tensor_tensor(self.pick[0:r], self.pick[0:r], bc(self.atf[0:r], 2, TOPK), ALU.mult))
        link(v.reduce_sum(self.num[0:r, h], self.pick[0:r], AX.X))

    def finish(self, dve, link, n, count):
        v, g, s, r = self.nc.vector, self.g, self.g.s, ROWS[n]
        gt = self.gates[0:r, n, :].rearrange("p (h k) -> p h k", h=PH)
        v.tensor_tensor(gt, self.best[0:r], self.best[0:r, :, 0:1].broadcast_to([r, PH, TOPK]), ALU.subtract).then_inc(s.gate_in, 1)
        link(v.scalar_tensor_tensor(out=self.num[0:r, :, 0], in0=self.num[0:r, :, 0], scalar=float(KEYS), in1=self.num[0:r, :, 1],
                                    op0=ALU.mult, op1=ALU.add))
        link(v.tensor_scalar(self.ids[0:r, n, :].rearrange("p (h k) -> p h k", h=PH), self.num[0:r, :, 0], g.before[0:r], None, ALU.add))
        dve.wait_ge(s.gate_exp, count)
        link(v.reduce_sum(self.den[0:r, 0], gt, AX.X))
        link(v.reciprocal(self.den[0:r, 1], self.den[0:r, 0]))
        v.tensor_tensor(gt, gt, bc(self.den[0:r, 1], 2, TOPK), ALU.mult).then_inc(s.routed, 1)

    def gate_exp(self, act, n, count):
        act.wait_ge(self.g.s.gate_in, count)
        self.nc.scalar.activation(self.gates[0:ROWS[n], n, :], self.gates[0:ROWS[n], n, :], ACT.Exp).then_inc(self.g.s.gate_exp, 1)


GROUP = 4
PLACES = 2 * GROUP
LISTS = 4
LEAD = LISTS * GROUP
CHOICES = PH * TOPK
FULL = CHOICES // GROUP
TURNS = [FULL * ROWS[n] // P for n in range(TILES)]


def expert_stage(nc, g, t, l, rows, sc, ids, gates, router):
    s = g.s
    ups, downs = (s.up0, s.up1, s.up2, s.up3, s.up4, s.up5, s.up6, s.up7), (s.down0, s.down1, s.down2, s.down3, s.down4, s.down5, s.down6, s.down7)
    PER_LAYER = sum(TURNS) // 2
    w_up, w_down = t["peer_up"].rearrange("l e d -> (l e) d"), t["peer_down"].rearrange("l e d -> (l e) d")
    with ExitStack() as ctx:
        sb = lambda name, shape, dt=F32: ctx.enter_context(nc.sbuf_tensor(fresh(name), shape, dt))
        up, down = sb("up", [P, PLACES, D]), sb("down", [P, PLACES, D])
        idx = sb("idx", [P, LISTS, GROUP], U32)
        dot, gel, weight = (sb(name, [P, 2, GROUP]) for name in ("dot", "gel", "weight"))
        diag = sb("diag", [P, 2, GROUP, P])
        with nc.Block() as block:
            @block.sync
            def _(sp):
                sp.dma_start(rows[NS:P, 4, :], rows[0:NS, 4, :]).then_inc(s.doubled, 16)
                sp.wait_ge(s.routed, TILES - 1)
                sp.dma_start(ids[NS:P, 4, 0:CHOICES // 2], ids[0:NS, 4, CHOICES // 2:]).then_inc(s.doubled, 16)
                sp.dma_start(gates[NS:P, 4, 0:CHOICES // 2], gates[0:NS, 4, CHOICES // 2:]).then_inc(s.doubled, 16)

            @block.gpsimd
            def _(pool):
                def numbers(n, turn, part):
                    pool.wait_ge(s.downs_done, (n * FULL + turn) * GROUP + GROUP)
                    pool.sem_inc(s.paced, 1)
                    nc.gpsimd.tensor_copy(idx[:, part], ids[:, n, bass.ds(turn * GROUP, GROUP)]).then_inc(s.numbers, 1)
                    pool.wait_ge(s.numbers, 1)
                    pool.sem_clear(s.numbers)

                def gather(n, turn, part, table, places, done, used):
                    for k in range(GROUP):
                        c = part % 2 * GROUP + k
                        pool.wait_ge(used, (n * FULL + turn) * GROUP + LEAD - PLACES + k + 1)
                        pool.sem_inc(s.paced, 1)
                        pool.indirect_dma_start(places[:, c, :], None, table,
                                                bass.IndirectOffsetOnAxis(ap=idx[:, part, k:k + 1], axis=0)).then_inc(done[c], 16)

                def gather_up(n, turn, part):
                    numbers(n, turn, part)
                    gather(n, turn, part, w_up, up, ups, s.dots_done)

                def gather_down(n, turn, part):
                    gather(n, turn, part, w_down, down, downs, s.downs_done)

                gather_up(0, 0, 0)
                for n in range(TILES):
                    with pool.Fori(0, TURNS[n] // LISTS - 1) as i:
                        for part in range(LISTS):
                            gather_up(n, LISTS * i + part + 1, (part + 1) % LISTS)
                            gather_down(n, LISTS * i + part, part)
                    for part in range(LISTS):
                        turn = TURNS[n] - LISTS + part
                        if part < LISTS - 1:
                            gather_up(n, turn + 1, part + 1)
                        elif n + 1 < TILES:
                            pool.wait_ge(s.routed, n + 1)
                            if n + 1 == TILES - 1:
                                pool.wait_ge(s.doubled, 48)
                            gather_up(n + 1, 0, 0)
                        gather_down(n, turn, part)

            @block.vector
            def _(dve):
                def weights(n, turn, half):
                    dve.wait_ge(s.gelus, n * FULL + turn + 1)
                    nc.vector.tensor_tensor(weight[:, half], gel[:, half], gates[:, n, bass.ds(turn * GROUP, GROUP)],
                                            ALU.mult).then_inc(s.weighted, 1)

                def up_rows(n, half, pair):
                    for k in range(GROUP):
                        c = half * GROUP + k
                        dve.wait_ge(ups[c], (l * PER_LAYER + n * FULL // 2 + pair + 1) * 16)
                        nc.vector.scalar_tensor_tensor(out=up[:, c], in0=up[:, c], scalar=1.0, in1=rows[:, n, :], op0=ALU.mult,
                                                       op1=ALU.mult, accum_out=dot[:, half, k:k + 1]).then_inc(s.dots_done, 1)

                def pair(n, i):
                    up_rows(n, 1, i)
                    weights(n, 2 * i, 0)
                    up_rows(n, 0, i + 1)
                    weights(n, 2 * i + 1, 1)

                dve.sem_inc(s.dots_done, LEAD)
                link = Link(dve, s.link_dve)
                for n in range(TILES):
                    if n:
                        dve.wait_ge(s.routed, n)
                    if n == TILES - 1:
                        dve.wait_ge(s.doubled, 48)
                    up_rows(n, 0, 0)
                    routing = PH + 1 if n + 1 < TILES else 0
                    for i in range(routing):
                        pair(n, i)
                        if i < PH:
                            router.head(link, n + 1, i)
                        else:
                            router.finish(dve, link, n + 1, n + 1)
                    with dve.Fori(routing, TURNS[n] // 2 - 1) as i:
                        pair(n, i)
                    up_rows(n, 1, TURNS[n] // 2 - 1)
                    weights(n, TURNS[n] - 2, 0)
                    weights(n, TURNS[n] - 1, 1)
                link(nc.vector.tensor_scalar(g.before[:], g.before[:], float(EXPERTS), None, ALU.add))

            @block.scalar
            def _(act):
                def gelu(n, turn, half):
                    act.wait_ge(s.dots_done, (n * FULL + turn + 1) * GROUP + LEAD)
                    nc.scalar.activation(gel[:, half], dot[:, half], ACT.Gelu).then_inc(s.gelus, 1)

                def diagonals(n, turn, half):
                    act.wait_ge(s.weighted, n * FULL + turn + 1)
                    for k in range(GROUP):
                        act.wait_ge(s.downs_done, (n * FULL + turn) * GROUP + LEAD - PLACES + k + 1)
                        nc.scalar.activation(diag[:, half, k, 0:ROWS[n]], table(g, "ident" if ROWS[n] == P else "ident2"), ACT.Copy,
                                             scale=weight[:, half, k:k + 1]).then_inc(s.diagonal, 1)

                def copy_x(n):
                    act.wait_ge(s.summed, n + 1)
                    r = ROWS[n]
                    nc.scalar.copy(g.x[0:r, n, :].rearrange("p (a c) -> p a c", a=2), g.ps[0:r, 2 * (n % 2):2 * (n % 2) + 2, :]).then_inc(s.x_copied, 1)

                for n in range(TILES):
                    gelu(n, 0, 0)
                    middle = (PH + 1 if n + 1 < TILES else 2)
                    for first, last in ((0, middle), (middle, TURNS[n] // 2 - 1)):
                        with act.Fori(first, last) as i:
                            gelu(n, 2 * i + 1, 1)
                            diagonals(n, 2 * i, 0)
                            gelu(n, 2 * i + 2, 0)
                            diagonals(n, 2 * i + 1, 1)
                        if first == 0:
                            if n + 1 < TILES:
                                router.gate_exp(act, n + 1, n + 1)
                            if n:
                                copy_x(n - 1)
                    gelu(n, TURNS[n] - 1, 1)
                    diagonals(n, TURNS[n] - 2, 0)
                    diagonals(n, TURNS[n] - 1, 1)
                copy_x(TILES - 1)

            @block.tensor
            def _(pe):
                def add(n, turn, half, pair, last=False):
                    for k in range(GROUP):
                        c = half * GROUP + k
                        pe.wait_ge(s.diagonal, (n * FULL + turn) * GROUP + k + 1)
                        pe.wait_ge(downs[c], (l * PER_LAYER + n * FULL // 2 + pair + 1) * 16)
                        for m in range(2):
                            ins = nc.tensor.matmul(g.ps[0:ROWS[n], 2 * (n % 2) + m, :], diag[:, half, k, 0:ROWS[n]],
                                                   down[:, c, m * 512:(m + 1) * 512], start=False, stop=last and k == GROUP - 1)
                        ins.then_inc(s.downs_done, 1)

                pe.sem_inc(s.downs_done, LEAD)
                for n in range(TILES):
                    r = ROWS[n]
                    if n >= 2:
                        pe.wait_ge(s.x_copied, n - 1)
                    for m in range(2):
                        nc.tensor.matmul(g.ps[0:r, 2 * (n % 2) + m, :], ident(g, r), g.x[0:r, n, m * 512:(m + 1) * 512],
                                         start=True, stop=False)
                    with pe.Fori(0, TURNS[n] // 2 - 1) as i:
                        add(n, 2 * i, 0, i)
                        add(n, 2 * i + 1, 1, i)
                    add(n, TURNS[n] - 2, 0, TURNS[n] // 2 - 1)
                    add(n, TURNS[n] - 1, 1, TURNS[n] // 2 - 1, last=True)
                    pe.wait_ge(s.downs_done, (n * FULL + TURNS[n]) * GROUP + LEAD)
                    pe.sem_inc(s.summed, 1)
    clear_semaphores(nc, g)


def build(nc, t, o):
    with ExitStack() as ctx:
        g = State()
        sb = lambda name, shape, dt=F32: ctx.enter_context(nc.sbuf_tensor(fresh(name), shape, dt))
        numbers = []

        def keep(name):
            return ctx.enter_context(nc.semaphore(name))

        def make(name):
            sem = keep(name)
            numbers.append(sem.num)
            return sem

        g.s = Semaphores(make, keep)
        numbers.sort()
        g.runs, first = [], numbers[0]
        for a, b in zip(numbers, numbers[1:] + [None]):
            if b != a + 1:
                g.runs.append((first, a))
                first = b
        s = g.s
        g.consts, g.ones = sb("consts_sb", [P, N_CONST]), sb("ones", [P, P])
        g.x, g.hT, g.pscale = sb("x", [P, TILES, D]), sb("hT", [P, KT, TOK]), sb("pscale", [P, PW // P])
        g.before = sb("before", [P, 1])
        g.ps = ctx.enter_context(nc.psum_tensor("ps", [P, 8, 512], F32))
        with nc.Block() as block:
            @block.sync
            def _(sp):
                sp.dma_start(g.consts[:], t["consts"]).then_inc(s.loaded, 16)
                sp.dma_start(g.x[:, 0:4, :], t["x_prompt"][0].rearrange("(n p) d -> p n d", p=P)).then_inc(s.loaded, 16)
                sp.dma_start(g.x[0:NS, 4, :], t["x_sample"].rearrange("b t d -> (b t) d")).then_inc(s.loaded, 16)
                sp.wait_ge(s.loaded, 48)

            @block.gpsimd
            def _(pool):
                nc.gpsimd.memset(g.ones[:], 1.0).then_inc(s.filled, 1)
                nc.gpsimd.memset(g.before[:], 0.0).then_inc(s.filled, 1)
                pool.wait_ge(s.filled, 2)
        clear_semaphores(nc, g)
        with nc.Fori(0, DEPTH) as l:
            with ExitStack() as mix:
                sbm = lambda name, shape: mix.enter_context(nc.sbuf_tensor(fresh(name), shape, F32))
                g.oa, g.ob = sbm("oa", [P, H, TOK]), sbm("ob", [P, 2, TOK])
                delta_stage(nc, g, t, o, l)
                window_stage(nc, g, t, o, l)
                oc = sbm("oc", [P, PW // P, TOK])
                pool_stage(nc, g, t, o, l, oc)
                merge_stage(nc, g, t, l, oc)
            with ExitStack() as ffn:
                sbf = lambda name, shape, dt=F32: ffn.enter_context(nc.sbuf_tensor(fresh(name), shape, dt))
                rows, ids, gates = sbf("rows", [P, TILES, D]), sbf("ids", [P, TILES, CHOICES], U32), sbf("gates", [P, TILES, CHOICES])
                sc = sbf("sc", [P, TILES, NQ, KEYS])
                router = Router(nc, g, sbf, sc, ids, gates)
                with ExitStack() as inner:
                    ring = inner.enter_context(nc.sbuf_tensor(fresh("ring"), [P, 2, 4096], F32))
                    w_q = [rows_of(layer(t["peer_query"], l))[:, :, i * 512:(i + 1) * 512] for i in range(4)]
                    norm_stage(nc, g, t["norm_ffn"][bass.ds(l, 1)], rows, ring=ring, sources=w_q)
                    score_stage(nc, g, t, l, sc, router, ring, w_q)
                expert_stage(nc, g, t, l, rows, sc, ids, gates, router)
        with ExitStack() as last:
            rows = last.enter_context(nc.sbuf_tensor(fresh("rows"), [P, TILES, D], F32))
            norm_stage(nc, g, t["norm_final"], rows, transposed=False)
            with nc.Block() as block:
                @block.sync
                def _(sp):
                    sp.dma_start(o["y_p"][0].rearrange("(n p) d -> p n d", p=P), rows[:, 0:4, :]).then_inc(s.stored, 16)
                    sp.dma_start(o["y_s"].rearrange("b t d -> (b t) d"), rows[0:NS, 4, :]).then_inc(s.stored, 16)
                    sp.wait_ge(s.stored, 32)


INPUTS = ["x_prompt", "x_sample", "state_delta", "state_conv", "cache_win0", "cache_win1", "cache_win2", "state_pool",
          "norm_mix", "w_in", "conv_w", "a_log", "dt_bias", "dn_norm", "w_pool", "pool_scale", "w_branch", "w_out",
          "norm_ffn", "peer_query", "peer_subkeys", "peer_up", "peer_down", "norm_final"]


def win(i, prompt):
    rows = min(GROUPS[i][0], SEQ if prompt else PAST + NT)
    return (DEPTH, 1 if prompt else NB, rows, 2, SLOTS, SD)


OUTPUTS = [("y_p", (1, SEQ, D)), ("y_s", (NB, NT, D)), ("delta_p", (DEPTH, 1, H, HD, HD)), ("delta_s", (DEPTH, NB, H, HD, HD)),
           ("conv_p", (DEPTH, 1, CONV - 1, QKV)), ("conv_s", (DEPTH, NB, CONV - 1, QKV)),
           ("win0_p", win(0, True)), ("win0_s", win(0, False)), ("win1_p", win(1, True)), ("win1_s", win(1, False)),
           ("win2_p", win(2, True)), ("win2_s", win(2, False)), ("pool_p", (DEPTH, 1, PBUF, PW)), ("pool_s", (DEPTH, NB, PBUF, PW))]


def kernel(**inputs):
    _names.clear()
    import concourse.bacc as bacc
    from concourse.bass_utils import run_bass_kernel_spmd as run

    nc = bacc.Bacc("TRN2", target_bir_lowering=False, num_devices=1)
    arrays = {f"in_{name}": np.ascontiguousarray(inputs[name]) for name in INPUTS}
    arrays["in_norm_final"] = arrays["in_norm_final"].reshape(1, D)
    arrays["in_consts"] = constants()
    t = {name[3:]: nc.dram_tensor(name, a.shape, mybir.dt.from_np(a.dtype), kind="ExternalInput").ap() for name, a in arrays.items()}
    o = {name: nc.dram_tensor(f"out_{name}", shape, F32, kind="ExternalOutput").ap() for name, shape in OUTPUTS}
    build(nc, t, o)
    r = run(nc, [arrays], core_ids=[0])
    return tuple(r.results[0][f"out_{name}"] for name, _ in OUTPUTS)
```
